# Optimizing a Trainium2 kernel written in Bass

```python
import math
import jax, jax.numpy as jnp
from jax import lax
import numpy as np

D_MODEL = 1024
BATCH = 1
SEQ = 256
DEPTH = 2

N_MIXERS = 2
N_RET_LAYERS = (DEPTH + 1) // 2
N_MLA_LAYERS = DEPTH // 2
DN_ALPHA = (2.0 * DEPTH) ** 0.25
DN_BETA = (8.0 * DEPTH) ** -0.25
LN_EPS = 1e-5
ROPE_BASE = 10000.0

RET_HEADS = 4
RET_DK = D_MODEL // RET_HEADS
RET_DV = 2 * RET_DK
RET_HK = RET_HEADS * RET_DK
RET_HV = RET_HEADS * RET_DV
RET_IN = 2 * RET_HK + 2 * RET_HV
RET_CHUNK = 128

MLA_HEADS = 8
MLA_NOPE = 128
MLA_ROPE = 64
MLA_VDIM = 128
MLA_Q_RANK = 384
MLA_KV_RANK = 256
MLA_IN = MLA_Q_RANK + MLA_KV_RANK + MLA_ROPE
MLA_QBLOCK = 128

PEER_HEADS = 8
PEER_NKEYS = 128
PEER_EXPERTS = PEER_NKEYS * PEER_NKEYS
PEER_DKEY = 256
PEER_HALF = PEER_DKEY // 2
PEER_TOPK = 16
PEER_TOKEN_BLOCK = 128


def layer_norm(x, g, b):
    xf = x.astype(jnp.float32)
    mu = jnp.mean(xf, axis=-1, keepdims=True)
    var = jnp.mean(jnp.square(xf - mu), axis=-1, keepdims=True)
    return ((xf - mu) * lax.rsqrt(var + LN_EPS) * g.astype(jnp.float32) + b.astype(jnp.float32)).astype(x.dtype)

def rms_norm(x, g):
    xf = x.astype(jnp.float32)
    ms = jnp.mean(jnp.square(xf), axis=-1, keepdims=True)
    return (xf * lax.rsqrt(ms + LN_EPS) * g.astype(jnp.float32)).astype(x.dtype)

def rotary(x, positions):
    d = x.shape[-1]
    inv_freq = ROPE_BASE ** (-jnp.arange(0, d, 2, dtype=jnp.float32) / d)
    ang = positions.astype(jnp.float32)[..., None] * inv_freq
    cos = jnp.cos(ang)[:, :, None, :]
    sin = jnp.sin(ang)[:, :, None, :]
    x1, x2 = jnp.split(x.astype(jnp.float32), 2, axis=-1)
    return jnp.concatenate([x1 * cos - x2 * sin, x1 * sin + x2 * cos], axis=-1).astype(x.dtype)

def retention_scan(q, k, v, log_gamma, strict):
    B, S, H, dk = q.shape
    dv = v.shape[-1]
    C = RET_CHUNK
    n_chunks = S // C
    dt = q.dtype
    idx = jnp.arange(C, dtype=jnp.float32)
    diff = idx[:, None] - idx[None, :]
    keep = (diff > 0) if strict else (diff >= 0)
    lg = log_gamma[:, None, None]
    decay = jnp.where(keep[None], jnp.exp(jnp.maximum(diff, 0.0)[None] * lg), 0.0).astype(dt)
    xi = jnp.exp((idx + 1.0)[None, :] * log_gamma[:, None]).astype(dt)
    zeta = jnp.exp((C - 1.0 - idx)[None, :] * log_gamma[:, None]).astype(dt)
    gamma_c = jnp.exp(C * log_gamma).astype(dt)[None, :, None, None]

    def to_chunks(t):
        return t.reshape(B, n_chunks, C, H, t.shape[-1]).transpose(1, 0, 3, 2, 4)

    def step(state, inp):
        qi, ki, vi = inp
        inner = jnp.einsum('bhnm,bhmv->bhnv', jnp.einsum('bhnd,bhmd->bhnm', qi, ki) * decay[None], vi)
        cross = jnp.einsum('bhnd,bhdv->bhnv', qi, state) * xi[None, :, :, None]
        state = gamma_c * state + jnp.einsum('bhmd,bhmv->bhdv', ki * zeta[None, :, :, None], vi)
        return state, inner + cross

    state0 = jnp.zeros((B, H, dk, dv), dt)
    _, out = lax.scan(step, state0, (to_chunks(q), to_chunks(k), to_chunks(v)))
    return out.transpose(1, 0, 3, 2, 4).reshape(B, S, H, dv)

def retention_mixer(x, positions, w_in, log1m_decay, gn_g, gn_b, w_out):
    B, S, _ = x.shape
    proj = x @ w_in
    q, k, v, g = jnp.split(proj, [RET_HK, 2 * RET_HK, 2 * RET_HK + RET_HV], axis=-1)
    q = rotary(q.reshape(B, S, RET_HEADS, RET_DK), positions)
    k = rotary(k.reshape(B, S, RET_HEADS, RET_DK), positions) * (RET_DK ** -0.5)
    v = v.reshape(B, S, RET_HEADS, RET_DV)
    log_gamma = jnp.log1p(-jnp.exp(log1m_decay.astype(jnp.float32)))
    fwd = retention_scan(q, k, v, log_gamma[0], strict=False)
    bwd = jnp.flip(retention_scan(jnp.flip(q, 1), jnp.flip(k, 1), jnp.flip(v, 1), log_gamma[1], strict=True), 1)
    y = (fwd + bwd).astype(jnp.float32)
    mu = jnp.mean(y, axis=-1, keepdims=True)
    var = jnp.mean(jnp.square(y - mu), axis=-1, keepdims=True)
    yn = ((y - mu) * lax.rsqrt(var + LN_EPS)).reshape(B, S, RET_HV)
    yn = (yn * gn_g.astype(jnp.float32) + gn_b.astype(jnp.float32)).astype(x.dtype)
    return (jax.nn.silu(g) * yn) @ w_out

def mla_mixer(x, positions, w_in, q_norm_g, kv_norm_g, w_uq, w_ukv, w_out):
    B, S, _ = x.shape
    c_q, c_kv, k_rope = jnp.split(x @ w_in, [MLA_Q_RANK, MLA_Q_RANK + MLA_KV_RANK], axis=-1)
    q = (rms_norm(c_q, q_norm_g) @ w_uq).reshape(B, S, MLA_HEADS, MLA_NOPE + MLA_ROPE)
    q_nope, q_rope = jnp.split(q, [MLA_NOPE], axis=-1)
    q_rope = rotary(q_rope, positions)
    kv = (rms_norm(c_kv, kv_norm_g) @ w_ukv).reshape(B, S, MLA_HEADS, MLA_NOPE + MLA_VDIM)
    k_nope, v = jnp.split(kv, [MLA_NOPE], axis=-1)
    k_rope = rotary(k_rope[:, :, None, :], positions)[:, :, 0, :]
    scale = (MLA_NOPE + MLA_ROPE) ** -0.5
    nb = S // MLA_QBLOCK

    def blocks(t):
        return t.reshape(B, nb, MLA_QBLOCK, MLA_HEADS, t.shape[-1]).transpose(1, 0, 2, 3, 4)

    def attend(blk):
        qn, qr = blk
        s = jnp.einsum('bqhd,bkhd->bhqk', qn, k_nope) + jnp.einsum('bqhd,bkd->bhqk', qr, k_rope)
        p = jax.nn.softmax(s.astype(jnp.float32) * scale, axis=-1).astype(v.dtype)
        return jnp.einsum('bhqk,bkhd->bqhd', p, v)

    o = lax.map(attend, (blocks(q_nope), blocks(q_rope)))
    o = o.transpose(1, 0, 2, 3, 4).reshape(B, S, MLA_HEADS * MLA_VDIM)
    return o @ w_out

def peer_ffn(x, w_q, sub_keys, u, v):
    B, S, D = x.shape
    T = B * S
    xt = x.reshape(T // PEER_TOKEN_BLOCK, PEER_TOKEN_BLOCK, D)

    def block(xb):
        q = (xb @ w_q).reshape(PEER_TOKEN_BLOCK, PEER_HEADS, 2, PEER_HALF)
        s = jnp.einsum('thcd,hckd->thck', q, sub_keys).astype(jnp.float32)
        s1, i1 = lax.top_k(s[:, :, 0], PEER_TOPK)
        s2, i2 = lax.top_k(s[:, :, 1], PEER_TOPK)
        cand_s = (s1[..., :, None] + s2[..., None, :]).reshape(PEER_TOKEN_BLOCK, PEER_HEADS, PEER_TOPK * PEER_TOPK)
        cand_i = (i1[..., :, None] * PEER_NKEYS + i2[..., None, :]).reshape(PEER_TOKEN_BLOCK, PEER_HEADS, PEER_TOPK * PEER_TOPK)
        top_s, pos = lax.top_k(cand_s, PEER_TOPK)
        eidx = jnp.take_along_axis(cand_i, pos, axis=-1)
        gate = jax.nn.softmax(top_s, axis=-1).astype(xb.dtype)
        h = jax.nn.gelu(jnp.einsum('thkd,td->thk', u[eidx], xb), approximate=False)
        return jnp.einsum('thk,thkd->td', gate * h, v[eidx])

    return lax.map(block, xt).reshape(B, S, D)

def first_inputs(seed: int = 0) -> dict:
    key = jax.random.key(seed)
    ks = jax.random.split(key, 24)
    f32 = jnp.float32
    nrm = lambda k, shape, s: jax.random.normal(k, shape, f32) * s
    x = jax.random.normal(ks[0], (BATCH, SEQ, D_MODEL), f32)
    offsets = jax.random.randint(ks[1], (BATCH, 1), 0, 512, dtype=jnp.int32)
    positions = (offsets + jnp.arange(SEQ, dtype=jnp.int32)[None, :]).astype(jnp.int32)
    ret_w_in = nrm(ks[2], (N_RET_LAYERS, D_MODEL, RET_IN), D_MODEL ** -0.5)
    base = (-5.0 - jnp.arange(RET_HEADS, dtype=f32)) * math.log(2.0)
    ret_log1m_decay = base[None, None, :] + nrm(ks[3], (N_RET_LAYERS, 2, RET_HEADS), 0.05)
    ret_gn_g = 1.0 + nrm(ks[4], (N_RET_LAYERS, RET_HV), 0.02)
    ret_gn_b = nrm(ks[5], (N_RET_LAYERS, RET_HV), 0.02)
    ret_w_out = nrm(ks[6], (N_RET_LAYERS, RET_HV, D_MODEL), DN_BETA * RET_HV ** -0.5)
    mla_w_in = nrm(ks[7], (N_MLA_LAYERS, D_MODEL, MLA_IN), D_MODEL ** -0.5)
    mla_q_norm = 1.0 + nrm(ks[8], (N_MLA_LAYERS, MLA_Q_RANK), 0.02)
    mla_kv_norm = 1.0 + nrm(ks[9], (N_MLA_LAYERS, MLA_KV_RANK), 0.02)
    mla_w_uq = nrm(ks[10], (N_MLA_LAYERS, MLA_Q_RANK, MLA_HEADS * (MLA_NOPE + MLA_ROPE)), MLA_Q_RANK ** -0.5)
    mla_w_ukv = nrm(ks[11], (N_MLA_LAYERS, MLA_KV_RANK, MLA_HEADS * (MLA_NOPE + MLA_VDIM)), MLA_KV_RANK ** -0.5)
    mla_w_out = nrm(ks[12], (N_MLA_LAYERS, MLA_HEADS * MLA_VDIM, D_MODEL), DN_BETA * (MLA_HEADS * MLA_VDIM) ** -0.5)
    peer_w_q = nrm(ks[13], (DEPTH, D_MODEL, PEER_HEADS * PEER_DKEY), D_MODEL ** -0.5)
    peer_sub_keys = nrm(ks[14], (DEPTH, PEER_HEADS, 2, PEER_NKEYS, PEER_HALF), PEER_HALF ** -0.5)
    peer_u = nrm(ks[15], (DEPTH, PEER_EXPERTS, D_MODEL), D_MODEL ** -0.5)
    peer_v = nrm(ks[16], (DEPTH, PEER_EXPERTS, D_MODEL), DN_BETA * (PEER_HEADS * PEER_TOPK) ** -0.5)
    ln_mix_g = 1.0 + nrm(ks[17], (DEPTH, D_MODEL), 0.02)
    ln_mix_b = nrm(ks[18], (DEPTH, D_MODEL), 0.02)
    ln_ffn_g = 1.0 + nrm(ks[19], (DEPTH, D_MODEL), 0.02)
    ln_ffn_b = nrm(ks[20], (DEPTH, D_MODEL), 0.02)
    return {'x': x, 'positions': positions,
            'ret_w_in': ret_w_in, 'ret_log1m_decay': ret_log1m_decay, 'ret_gn_g': ret_gn_g, 'ret_gn_b': ret_gn_b, 'ret_w_out': ret_w_out,
            'mla_w_in': mla_w_in, 'mla_q_norm': mla_q_norm, 'mla_kv_norm': mla_kv_norm, 'mla_w_uq': mla_w_uq, 'mla_w_ukv': mla_w_ukv, 'mla_w_out': mla_w_out,
            'peer_w_q': peer_w_q, 'peer_sub_keys': peer_sub_keys, 'peer_u': peer_u, 'peer_v': peer_v,
            'ln_mix_g': ln_mix_g, 'ln_mix_b': ln_mix_b, 'ln_ffn_g': ln_ffn_g, 'ln_ffn_b': ln_ffn_b}

def first_block(x, positions,
              ret_w_in, ret_log1m_decay, ret_gn_g, ret_gn_b, ret_w_out,
              mla_w_in, mla_q_norm, mla_kv_norm, mla_w_uq, mla_w_ukv, mla_w_out,
              peer_w_q, peer_sub_keys, peer_u, peer_v,
              ln_mix_g, ln_mix_b, ln_ffn_g, ln_ffn_b):
    h = x
    for i in range(DEPTH):
        j = i // N_MIXERS
        if i % N_MIXERS == 0:
            mix = retention_mixer(h, positions, ret_w_in[j], ret_log1m_decay[j], ret_gn_g[j], ret_gn_b[j], ret_w_out[j])
        else:
            mix = mla_mixer(h, positions, mla_w_in[j], mla_q_norm[j], mla_kv_norm[j], mla_w_uq[j], mla_w_ukv[j], mla_w_out[j])
        h = layer_norm(DN_ALPHA * h + mix, ln_mix_g[i], ln_mix_b[i])
        ffn = peer_ffn(h, peer_w_q[i], peer_sub_keys[i], peer_u[i], peer_v[i])
        h = layer_norm(DN_ALPHA * h + ffn, ln_ffn_g[i], ln_ffn_b[i])
    return h


DEPTH_2 = 1

CHUNK = 64
QBLK = 128
MEM_LEN = 256
EPS = 1e-6

POOL_WIDTH = D_MODEL // 4
POOL_GROUPS = 4
POOL_GDIM = POOL_WIDTH // POOL_GROUPS
POOL_WINDOWS = (2, 4, 8, 16)

RWKV_WIDTH = D_MODEL // 4
RWKV_HEAD = 64
RWKV_HEADS = RWKV_WIDTH // RWKV_HEAD
D_DECAY_LORA = 64
D_AAA_LORA = 64
D_GATE_LORA = 128
RWKV_COLS = 3 * RWKV_WIDTH + D_DECAY_LORA + D_AAA_LORA + D_GATE_LORA
RWKV_SPLITS = tuple(int(i) for i in np.cumsum(
    [RWKV_WIDTH, RWKV_WIDTH, RWKV_WIDTH, D_DECAY_LORA, D_AAA_LORA]))
RWKV_GN_EPS = 64e-5

DIFF_WIDTH = D_MODEL // 2
DIFF_HEADS = 4
DIFF_VDIM = DIFF_WIDTH // DIFF_HEADS
DIFF_QK = DIFF_VDIM // 2
DIFF_COLS = 3 * DIFF_WIDTH

P_IN = POOL_WIDTH + RWKV_COLS + DIFF_COLS

XA_HEADS = 4
XA_HEAD = D_MODEL // XA_HEADS
D_FF = 2816
CONV_W = 3


F32 = jnp.float32

def rms_normalize(x, eps=EPS):
    xf = x.astype(F32)
    return xf * lax.rsqrt(jnp.mean(xf * xf, axis=-1, keepdims=True) + eps)

def rmsnorm(x, g):
    return (rms_normalize(x) * g.astype(F32)).astype(x.dtype)

def shift_right(x, n=1):
    return jnp.pad(x, ((0, 0), (n, 0), (0, 0)))[:, :x.shape[1]]

def alibi_slopes(n_heads):
    return jnp.asarray(2.0 ** (-8.0 * (np.arange(n_heads) + 1) / n_heads), dtype=F32)

def pool_mixer(u, w_grp, scale):
    B, S, _ = u.shape
    ug = u.astype(F32).reshape(B, S, POOL_GROUPS, POOL_GDIM)
    t = jnp.arange(S)
    outs = []
    for gi, w in enumerate(POOL_WINDOWS):
        c = jnp.cumsum(ug[:, :, gi], axis=1)
        win_sum = c - shift_right(c, w)
        count = jnp.minimum(t + 1, w).astype(F32)[None, :, None]
        outs.append(win_sum / count - ug[:, :, gi])
    d = jnp.stack(outs, axis=2)
    y = jnp.einsum('bsgc,gcd->bsgd', d, w_grp.astype(F32))
    return (y.reshape(B, S, POOL_WIDTH) * scale.astype(F32)).astype(u.dtype)

def wkv7_scan(r, decay, k, v, a_vec, b_vec):
    B, S, H, N = r.shape

    def step(s, inp):
        r_t, w_t, k_t, v_t, a_t, b_t = inp
        sa = jnp.einsum('bhvk,bhk->bhv', s, a_t)
        s = (s * w_t[:, :, None, :] + sa[..., None] * b_t[:, :, None, :]
             + v_t[..., None] * k_t[:, :, None, :])
        y = jnp.einsum('bhvk,bhk->bhv', s, r_t)
        return s, y

    seq_first = lambda a: jnp.moveaxis(a, 1, 0)
    s0 = jnp.zeros((B, H, N, N), F32)
    _, ys = lax.scan(step, s0, (seq_first(r), seq_first(decay), seq_first(k),
                                seq_first(v), seq_first(a_vec), seq_first(b_vec)))
    return jnp.moveaxis(ys, 0, 1)

def rwkv7_mixer(z, mu, w0, w2, a0, a2, g2, k_k, k_a, r_k, ln_w, ln_b):
    B, S, _ = z.shape
    H, N = RWKV_HEADS, RWKV_HEAD
    zf = z.astype(F32)
    zm = zf + mu.astype(F32) * (shift_right(zf) - zf)
    r, k, v, wd, ad, gd = jnp.split(zm, RWKV_SPLITS, axis=-1)
    w = -jax.nn.softplus(-(w0 + jnp.tanh(wd) @ w2)) - 0.5
    a = jax.nn.sigmoid(a0 + ad @ a2)
    g = jax.nn.sigmoid(gd) @ g2
    heads = lambda t: t.reshape(B, S, H, N)
    r, w, k, v, a = heads(r), heads(w), heads(k), heads(v), heads(a)
    kk = k * k_k.astype(F32).reshape(H, N)
    kk = kk / jnp.maximum(jnp.sqrt(jnp.sum(kk * kk, -1, keepdims=True)), 1e-12)
    k = k * (1.0 + (a - 1.0) * k_a.astype(F32).reshape(H, N))
    decay = jnp.exp(-jnp.exp(w))
    y = wkv7_scan(r, decay, k, v, -kk, kk * a)
    mean = jnp.mean(y, -1, keepdims=True)
    var = jnp.mean(jnp.square(y - mean), -1, keepdims=True)
    y = ((y - mean) * lax.rsqrt(var + RWKV_GN_EPS)).reshape(B, S, RWKV_WIDTH)
    y = y * ln_w.astype(F32) + ln_b.astype(F32)
    bonus = jnp.sum(r * k * r_k.astype(F32), -1, keepdims=True) * v
    y = y + bonus.reshape(B, S, RWKV_WIDTH)
    return (y * g).astype(z.dtype)

def diff_attention(z, q_norm, k_norm, lq1, lk1, lq2, lk2, subln, lambda_init):
    B, S, _ = z.shape
    H = DIFF_HEADS
    q, k, v = jnp.split(z.astype(F32), 3, axis=-1)
    q = rms_normalize(q.reshape(B, S, H, 2, DIFF_QK)) * q_norm.astype(F32)
    k = rms_normalize(k.reshape(B, S, H, 2, DIFF_QK)) * k_norm.astype(F32)
    v = v.reshape(B, S, H, DIFF_VDIM)
    lam = (jnp.exp(jnp.sum(lq1.astype(F32) * lk1.astype(F32)))
           - jnp.exp(jnp.sum(lq2.astype(F32) * lk2.astype(F32))) + lambda_init)
    slopes = alibi_slopes(H)
    nblk = S // QBLK
    qb = q.reshape(B, nblk, QBLK, H, 2, DIFF_QK).transpose(1, 0, 2, 3, 4, 5)
    kpos = jnp.arange(S)
    kchunk = kpos // CHUNK
    scale = DIFF_QK ** -0.5

    def block(args):
        q_blk, start = args
        qpos = start + jnp.arange(QBLK)
        s = jnp.einsum('bqhcd,bkhcd->bhcqk', q_blk, k) * scale
        dist = jnp.abs(qpos[:, None] - kpos[None, :]).astype(F32)
        bias = -slopes[:, None, None, None] * dist
        visible = kchunk[None, :] <= (qpos // CHUNK)[:, None]
        s = jnp.where(visible, s + bias, -jnp.inf)
        p = jax.nn.softmax(s, axis=-1)
        p = p[:, :, 0] - lam * p[:, :, 1]
        return jnp.einsum('bhqk,bkhd->bqhd', p, v)

    starts = jnp.arange(nblk) * QBLK
    o = lax.map(block, (qb, starts))
    o = jnp.moveaxis(o, 0, 1).reshape(B, S, H, DIFF_VDIM)
    o = rms_normalize(o) * subln.astype(F32) * (1.0 - lambda_init)
    return o.reshape(B, S, DIFF_WIDTH).astype(z.dtype)

def memory_cross_attention(xn, memn, wq, wk, wv, wo, q_norm, k_norm):
    B, S, _ = xn.shape
    M = memn.shape[1]
    q = rms_normalize((xn @ wq).reshape(B, S, XA_HEADS, XA_HEAD)) * q_norm.astype(F32)
    k = rms_normalize((memn @ wk).reshape(B, M, XA_HEADS, XA_HEAD)) * k_norm.astype(F32)
    v = (memn @ wv).reshape(B, M, XA_HEADS, XA_HEAD).astype(F32)
    s = jnp.einsum('bshd,bmhd->bhsm', q, k) * (XA_HEAD ** -0.5)
    p = jax.nn.softmax(s, axis=-1)
    o = jnp.einsum('bhsm,bmhd->bshd', p, v).reshape(B, S, D_MODEL).astype(xn.dtype)
    return o @ wo

def conv_ffn(xn, w_up, conv_w, conv_b, w_down):
    h = xn @ w_up
    a, b = jnp.split(h, 2, axis=-1)
    rhs = conv_w.reshape(CONV_W, 1, D_FF).astype(a.dtype)
    c = lax.conv_general_dilated(a, rhs, window_strides=(1,), padding=[(CONV_W - 1, 0)],
                                 dimension_numbers=('NWC', 'WIO', 'NWC'),
                                 feature_group_count=D_FF) + conv_b
    return (jax.nn.gelu(c, approximate=False) * b) @ w_down

def second_inputs(seed: int = 0) -> dict:
    key = jax.random.key(seed)
    ks = iter(jax.random.split(key, 40))
    nrm = lambda shape, s: jax.random.normal(next(ks), shape, F32) * s
    gain = lambda shape: 1.0 + 0.02 * jax.random.normal(next(ks), shape, F32)
    L = DEPTH_2
    return {
        "x": nrm((BATCH, SEQ, D_MODEL), 1.0),
        "mem": nrm((BATCH, MEM_LEN, D_MODEL), 1.0),
        "mix_norm_g": gain((L, D_MODEL)),
        "w_in": nrm((L, D_MODEL, P_IN), D_MODEL ** -0.5),
        "pool_w": nrm((L, POOL_GROUPS, POOL_GDIM, POOL_GDIM), POOL_GDIM ** -0.5),
        "pool_scale": gain((L, POOL_WIDTH)),
        "rwkv_mu": jax.random.uniform(next(ks), (L, RWKV_COLS), F32),
        "rwkv_w0": jax.random.uniform(next(ks), (L, RWKV_WIDTH), F32, -5.0, -1.0),
        "rwkv_w2": nrm((L, D_DECAY_LORA, RWKV_WIDTH), 0.5 * D_DECAY_LORA ** -0.5),
        "rwkv_a0": nrm((L, RWKV_WIDTH), 0.1),
        "rwkv_a2": nrm((L, D_AAA_LORA, RWKV_WIDTH), 0.5 * D_AAA_LORA ** -0.5),
        "rwkv_g2": nrm((L, D_GATE_LORA, RWKV_WIDTH), D_GATE_LORA ** -0.5),
        "rwkv_k_k": 0.85 + nrm((L, RWKV_WIDTH), 0.05),
        "rwkv_k_a": 1.0 + nrm((L, RWKV_WIDTH), 0.05),
        "rwkv_r_k": nrm((L, RWKV_HEADS, RWKV_HEAD), 0.1),
        "rwkv_ln_w": gain((L, RWKV_WIDTH)),
        "rwkv_ln_b": nrm((L, RWKV_WIDTH), 0.02),
        "diff_q_norm": gain((L, 2, DIFF_QK)),
        "diff_k_norm": gain((L, 2, DIFF_QK)),
        "diff_lq1": nrm((L, DIFF_QK), 0.1),
        "diff_lk1": nrm((L, DIFF_QK), 0.1),
        "diff_lq2": nrm((L, DIFF_QK), 0.1),
        "diff_lk2": nrm((L, DIFF_QK), 0.1),
        "diff_subln": gain((L, DIFF_VDIM)),
        "w_out": nrm((L, D_MODEL, D_MODEL), D_MODEL ** -0.5),
        "xa_norm_g": gain((L, D_MODEL)),
        "mem_norm_g": gain((L, D_MODEL)),
        "xa_wq": nrm((L, D_MODEL, D_MODEL), D_MODEL ** -0.5),
        "xa_wk": nrm((L, D_MODEL, D_MODEL), D_MODEL ** -0.5),
        "xa_wv": nrm((L, D_MODEL, D_MODEL), D_MODEL ** -0.5),
        "xa_wo": nrm((L, D_MODEL, D_MODEL), D_MODEL ** -0.5),
        "xa_q_norm": gain((L, XA_HEAD)),
        "xa_k_norm": gain((L, XA_HEAD)),
        "ffn_norm_g": gain((L, D_MODEL)),
        "ffn_w_up": nrm((L, D_MODEL, 2 * D_FF), D_MODEL ** -0.5),
        "ffn_conv_w": nrm((L, CONV_W, D_FF), CONV_W ** -0.5),
        "ffn_conv_b": nrm((L, D_FF), 0.02),
        "ffn_w_down": nrm((L, D_FF, D_MODEL), D_FF ** -0.5),
    }

def second_block(x, mem, mix_norm_g, w_in, pool_w, pool_scale,
              rwkv_mu, rwkv_w0, rwkv_w2, rwkv_a0, rwkv_a2, rwkv_g2,
              rwkv_k_k, rwkv_k_a, rwkv_r_k, rwkv_ln_w, rwkv_ln_b,
              diff_q_norm, diff_k_norm, diff_lq1, diff_lk1, diff_lq2, diff_lk2, diff_subln,
              w_out, xa_norm_g, mem_norm_g, xa_wq, xa_wk, xa_wv, xa_wo, xa_q_norm, xa_k_norm,
              ffn_norm_g, ffn_w_up, ffn_conv_w, ffn_conv_b, ffn_w_down):
    h = x
    for l in range(DEPTH_2):
        lambda_init = 0.8 - 0.6 * math.exp(-0.3 * l)
        z = rmsnorm(h, mix_norm_g[l]) @ w_in[l]
        z_pool = z[..., :POOL_WIDTH]
        z_rwkv = z[..., POOL_WIDTH:POOL_WIDTH + RWKV_COLS]
        z_diff = z[..., POOL_WIDTH + RWKV_COLS:]
        y_pool = pool_mixer(z_pool, pool_w[l], pool_scale[l])
        y_rwkv = rwkv7_mixer(z_rwkv, rwkv_mu[l], rwkv_w0[l], rwkv_w2[l], rwkv_a0[l],
                             rwkv_a2[l], rwkv_g2[l], rwkv_k_k[l], rwkv_k_a[l],
                             rwkv_r_k[l], rwkv_ln_w[l], rwkv_ln_b[l])
        y_diff = diff_attention(z_diff, diff_q_norm[l], diff_k_norm[l], diff_lq1[l],
                                diff_lk1[l], diff_lq2[l], diff_lk2[l], diff_subln[l],
                                lambda_init)
        y = jnp.concatenate([y_pool, y_rwkv, y_diff], axis=-1)
        h = h + y @ w_out[l]
        h = h + memory_cross_attention(rmsnorm(h, xa_norm_g[l]), rmsnorm(mem, mem_norm_g[l]),
                                       xa_wq[l], xa_wk[l], xa_wv[l], xa_wo[l],
                                       xa_q_norm[l], xa_k_norm[l])
        h = h + conv_ffn(rmsnorm(h, ffn_norm_g[l]), ffn_w_up[l], ffn_conv_w[l],
                         ffn_conv_b[l], ffn_w_down[l])
    return h


def setup_inputs(seed=0):
    out = dict(first_inputs(seed))
    for name, value in second_inputs(seed + 1).items():
        if name != "x":
            out[name + "_2"] = value
    return out


def reference(
    x, positions, ret_w_in, ret_log1m_decay, ret_gn_g, ret_gn_b, ret_w_out, mla_w_in,
    mla_q_norm, mla_kv_norm, mla_w_uq, mla_w_ukv, mla_w_out, peer_w_q, peer_sub_keys, peer_u,
    peer_v, ln_mix_g, ln_mix_b, ln_ffn_g, ln_ffn_b, mem_2, mix_norm_g_2, w_in_2, pool_w_2,
    pool_scale_2, rwkv_mu_2, rwkv_w0_2, rwkv_w2_2, rwkv_a0_2, rwkv_a2_2, rwkv_g2_2, rwkv_k_k_2,
    rwkv_k_a_2, rwkv_r_k_2, rwkv_ln_w_2, rwkv_ln_b_2, diff_q_norm_2, diff_k_norm_2, diff_lq1_2,
    diff_lk1_2, diff_lq2_2, diff_lk2_2, diff_subln_2, w_out_2, xa_norm_g_2, mem_norm_g_2,
    xa_wq_2, xa_wk_2, xa_wv_2, xa_wo_2, xa_q_norm_2, xa_k_norm_2, ffn_norm_g_2, ffn_w_up_2,
    ffn_conv_w_2, ffn_conv_b_2, ffn_w_down_2,
):
    x = first_block(
        x, positions, ret_w_in, ret_log1m_decay, ret_gn_g, ret_gn_b, ret_w_out, mla_w_in,
        mla_q_norm, mla_kv_norm, mla_w_uq, mla_w_ukv, mla_w_out, peer_w_q, peer_sub_keys,
        peer_u, peer_v, ln_mix_g, ln_mix_b, ln_ffn_g, ln_ffn_b,
    )
    return second_block(
        x, mem_2, mix_norm_g_2, w_in_2, pool_w_2, pool_scale_2, rwkv_mu_2, rwkv_w0_2, rwkv_w2_2,
        rwkv_a0_2, rwkv_a2_2, rwkv_g2_2, rwkv_k_k_2, rwkv_k_a_2, rwkv_r_k_2, rwkv_ln_w_2,
        rwkv_ln_b_2, diff_q_norm_2, diff_k_norm_2, diff_lq1_2, diff_lk1_2, diff_lq2_2,
        diff_lk2_2, diff_subln_2, w_out_2, xa_norm_g_2, mem_norm_g_2, xa_wq_2, xa_wk_2, xa_wv_2,
        xa_wo_2, xa_q_norm_2, xa_k_norm_2, ffn_norm_g_2, ffn_w_up_2, ffn_conv_w_2, ffn_conv_b_2,
        ffn_w_down_2,
    )


_drawn_inputs = setup_inputs


def setup_inputs(seed=0):
    import zlib

    import numpy as np

    out = dict(_drawn_inputs(seed))
    spreads = {}
    factors = {'ret_gn_g': 8.0,
     'ret_gn_b': 7.889,
     'mla_q_norm': 8.0,
     'mla_kv_norm': 8.0,
     'mix_norm_g_2': 2.836,
     'pool_scale_2': 7.436,
     'rwkv_w2_2': 7.55,
     'rwkv_a0_2': 5.796,
     'rwkv_k_k_2': 6.921,
     'rwkv_k_a_2': 4.163,
     'rwkv_ln_w_2': 8.0,
     'rwkv_ln_b_2': 8.0,
     'diff_q_norm_2': 6.175,
     'diff_k_norm_2': 6.185,
     'diff_lk1_2': 4.37,
     'diff_lk2_2': 4.976,
     'diff_subln_2': 5.862,
     'xa_norm_g_2': 8.0,
     'mem_norm_g_2': 8.0,
     'xa_q_norm_2': 8.0,
     'xa_k_norm_2': 8.0,
     'ffn_norm_g_2': 12.47,
     'ffn_conv_b_2': 17.614}
    for name, (base, spread) in spreads.items():
        noise = np.random.default_rng([zlib.crc32(name.encode()), seed]).standard_normal(out[name].shape)
        drawn = base * np.exp(spread * noise) if base else spread * noise
        out[name] = __import__('jax').numpy.asarray(drawn.astype(out[name].dtype))
    for name, factor in factors.items():
        out[name] = (out[name] * factor).astype(out[name].dtype)
    return out
```

```python
from contextlib import ExitStack

import numpy as np

import concourse.bass as bass
from concourse import mybir

F32 = mybir.dt.float32
I32 = mybir.dt.int32
U32 = mybir.dt.uint32
ALU = mybir.AluOpType
ACT = mybir.ActivationFunctionType
AX = mybir.AxisListType.X

P = 128
T = 256
TB = T // P
D = 1024
KD = D // P
BANK = 512
RING = 8
SLOT = 1024
ALPHA = 4.0 ** 0.25
LN_EPS = 1e-5
RMS_EPS = 1e-6

RET_HEADS, RET_DK, RET_DV = 4, 256, 512
RET_HV = RET_HEADS * RET_DV

MLA_HEADS, NOPE, ROPE, VDIM = 8, 128, 64, 128
Q_RANK, KV_RANK = 384, 256
MLA_IN = Q_RANK + KV_RANK + ROPE
MLA_SCALE = float((NOPE + ROPE) ** -0.5)

PH, NK, TOPK = 8, 128, 16
HC = 2 * PH

POOL_W, RWKV_W, DIFF_W = 256, 256, 512
POOL_WINDOWS = (2, 4, 8, 16)
RWKV_COLS = 1024
C = 64
NC_ = T // C
NH = 4
UN = NC_ * NH
LEVELS = 6
RWKV_EPS = 64e-5
LAMBDA_INIT = 0.2
XH, XD = 4, 256
D_FF = 2816
FF_TILES = D_FF // P

TWO_PI_HI = 6.28125
TWO_PI_LO = float(2 * np.pi - 6.28125)
ROUND = 12582912.0
PI_IN = 3.1415925
LOWEST = -3.0e38

PHASES = ("retention", "peer0", "mla", "peer1", "mixers", "cross", "ffn")


def rows(name, layer, k_tiles, c0, cols, k_rows=P, row0=0):
    return [(name, layer, row0 + k * k_rows, k_rows, ((c0, cols),)) for k in range(k_tiles)]


def weight_plan(phases):
    plan = []
    for phase in phases:
        if phase == "retention":
            for n in range(6):
                plan.append((f"ret_in{n}", rows("ret_w_in", 0, KD, n * 1024, 1024)))
            plan.append(("ret_out", rows("ret_w_out", 0, RET_HV // P, 0, D)))
        if phase.startswith("peer"):
            l = int(phase[-1])
            plan.append((phase + "_keys", [("sub_keys", l, n, P, ((0, 1024),)) for n in range(2)]))
            for n in range(2):
                plan.append((f"{phase}_q{n}", rows("peer_w_q", l, KD, n * 1024, 1024)))
            plan.append((phase + "_experts", [("experts", l, n, P, ((0, 1024),)) for n in range(2 * NK)]))
        if phase == "mla":
            plan.append(("mla_in", rows("mla_w_in", 0, KD, 0, MLA_IN)))
            for n in range(2):
                plan.append((f"mla_uq{n}", rows("mla_w_uq", 0, Q_RANK // P, n * 768, 768)))
            for n in range(2):
                plan.append((f"mla_ukv{n}", rows("mla_w_ukv", 0, KV_RANK // P, n * 1024, 1024)))
            plan.append(("mla_out", rows("mla_w_out", 0, MLA_HEADS, 0, D)))
        if phase == "mixers":
            for n in range(4):
                plan.append((f"slots{n}", rows("w_in_2", 0, KD, POOL_W + n * 512, 512)))
            plan.append(("diff_v", rows("w_in_2", 0, KD, POOL_W + 2048, DIFF_W)))
            plan.append(("pool_in", rows("w_in_2", 0, KD, 0, POOL_W)))
            plan.append(("mix_out", rows("w_out_2", 0, 8, 0, D, k_rows=64)
                         + rows("w_out_2", 0, 4, 0, D, row0=512)))
        if phase == "cross":
            for n, w in enumerate(("xa_wk_2", "xa_wv_2", "xa_wq_2", "xa_wo_2")):
                plan.append((w, rows(w, 0, KD, 0, D)))
        if phase == "ffn":
            for n in range(6):
                w = min(4, FF_TILES - 4 * n) * P
                plan.append((f"up{n}", [("ffn_w_up_2", 0, k * P, P, ((n * 512, w), (D_FF + n * 512, w)))
                                        for k in range(KD)]))
            plan.append(("down", rows("ffn_w_down_2", 0, FF_TILES, 0, D)))
    return plan


def constants():
    out = {}
    out["c_ident"] = np.eye(P, dtype=np.float32)
    out["c_iota"] = np.tile(np.arange(P, dtype=np.float32), (P, 1))
    f = (np.float32(10000.0) ** (-np.arange(0, RET_DK, 2, dtype=np.float32) / np.float32(RET_DK))).astype(np.float32)
    out["c_ret_freq"] = f[:, None].copy()
    f = (np.float32(10000.0) ** (-np.arange(0, ROPE, 2, dtype=np.float32) / np.float32(ROPE))).astype(np.float32)
    out["c_mla_freq"] = np.tile(f, (P, 1))
    m = np.arange(T).reshape(TB, P).T[:, :, None]
    n = np.arange(T)[None, None, :]
    d = (n - m).astype(np.float32)
    out["c_ahead"] = np.stack([np.maximum(d, 0), np.maximum(-d, 0)], 1).reshape(P, 2 * TB * T)
    slopes = 2.0 ** (-8.0 * (np.arange(4) + 1) / 4)
    seen = (n // C) <= (m // C)
    bias = np.where(seen[:, :, None, :], -slopes[None, None, :, None] * np.abs(d)[:, :, None, :], LOWEST)
    out["c_alibi"] = bias.astype(np.float32).reshape(P, TB * 4 * T)
    pool = np.zeros((P, TB, 4, T), np.float32)
    for g, w in enumerate(POOL_WINDOWS):
        count = np.minimum(n + 1, w)
        pool[:, :, g, :] = ((m <= n) & (m > n - w)) / count - (m == n)
    out["c_pool"] = pool.reshape(P, TB * 4 * T)
    s, t = np.arange(C)[:, None], np.arange(C)[None, :]
    before = np.concatenate([s < t, s <= t], 1).astype(np.float32)
    levels = [((s < t) & (s >> (b + 1) == t >> (b + 1)) & (s >> b != t >> b)) for b in range(LEVELS)]
    reset = np.tile((np.arange(T) % C != 0).astype(np.float32), (C, NH))
    out["c_rwkv"] = np.concatenate([before] + [x.astype(np.float32) for x in levels] + [reset], 1)
    return {k: np.ascontiguousarray(v, dtype=np.float32) for k, v in out.items()}


def columns(x):
    def cols(v, p):
        return np.asarray(v).reshape(-1, p).T

    rwkv = [cols(x[n], C) for n in ("rwkv_mu_2", "rwkv_w0_2", "rwkv_a0_2", "rwkv_k_k_2", "rwkv_k_a_2", "rwkv_r_k_2",
                                    "pool_scale_2", "diff_q_norm_2", "diff_k_norm_2")]
    return {"positions_cols": np.ascontiguousarray(cols(x["positions"], P)),
            "channel_cols": np.ascontiguousarray(np.concatenate(rwkv, 1)),
            "conv_cols": np.ascontiguousarray(np.concatenate([cols(x["ffn_conv_w_2"], P), cols(x["ffn_conv_b_2"], P)], 1))}


class Count:

    def __init__(self, n=0):
        self.n = n

    def up(self, by=1):
        self.n = self.n + by
        return self.n


class Last:

    def __init__(self, step):
        self.step, self.counts, self.last = step, {}, None

    def next(self):
        return self.mark(self.step)

    def mark(self, sem, by=1):
        n = self.counts.setdefault(id(sem), Count())
        self.last = (sem, n.up(by))
        return sem, by

    def set(self, sem, n):
        self.counts[id(sem)] = Count(n)
        self.last = (sem, n)


class Banks:

    def __init__(self, served):
        self.served = served
        self.lent = {who: Count() for who in served}
        self.of = {}

    def lend(self, banks, who):
        n = self.lent[who].up()
        for b in banks:
            self.of[b] = (self.served[who], n)
        return self.served[who], n


class Memory:

    def __init__(self, base, start, size):
        self.base, self.at, self.end = base, start, start + size

    def take(self, *dims, parts=P):
        n = int(np.prod(dims))
        assert self.at + n <= self.end, ("SBUF", dims, self.at, self.end)
        v = self.base[0:parts, self.at:self.at + n]
        self.at += n
        if len(dims) == 1:
            return v
        names = "abcde"[:len(dims)]
        return v.rearrange(f"p ({' '.join(names)}) -> p {' '.join(names)}", **dict(zip(names, dims)))


def bcast(ap, axis, n):
    v = ap.unsqueeze(axis)
    return v.broadcast_to([*v.shape[:axis], n, *v.shape[axis + 1:]])


def build(nc, x, out, phases=PHASES):
    ctx = ExitStack()
    with ctx:
        def sem(name):
            return ctx.enter_context(nc.semaphore(name))

        ARENA = 32768
        PERSIST = 4096 + 256 + RING * SLOT + 2048 + 3072 + 768 + 1024
        sb = ctx.enter_context(nc.sbuf_tensor("sb", [P, PERSIST + ARENA], F32))
        lasting = Memory(sb, 0, PERSIST)
        h = lasting.take(TB, D)
        hT = lasting.take(KD, T)
        ident = lasting.take(P)
        iota = lasting.take(P)
        ring = lasting.take(RING, SLOT)
        norm_gb = lasting.take(2, D)
        pair = lasting.take(3072)
        routes = lasting.take(3, T)
        small = Memory(sb, lasting.at, 1024)
        lasting_at = {"hT": TB * D, "norm_gb": TB * D + KD * T + 2 * P + RING * SLOT}
        lasting_at["pair"] = lasting_at["norm_gb"] + 2 * D
        lasting_at["routes"] = lasting_at["pair"] + 3072
        stats = small.take(4, 2, 6)
        mv = small.take(2, 2)
        var8 = small.take(8, 2)
        rstd = small.take(16)
        misc = small.take(512)

        def arena():
            return Memory(sb, PERSIST, ARENA)

        psum = ctx.enter_context(nc.psum_tensor("psum", [P, 8, BANK], F32))

        def ps(b0, n, parts=P):
            return psum[0:parts, b0:b0 + n, :].rearrange("p a b -> p (a b)")

        ring_loaded = [sem(f"ring_loaded{n}") for n in range(RING)]
        chunks_done = sem("chunks_done")
        psum_for_vec, psum_for_act = sem("psum_for_vec"), sem("psum_for_act")
        vec_served, act_served = sem("vec_served"), sem("act_served")
        vec_for_act, act_for_vec = sem("vec_for_act"), sem("act_for_vec")
        vec_for_pe, act_for_pe = sem("vec_for_pe"), sem("act_for_pe")
        vec_step, act_step = sem("vec_step"), sem("act_step")
        onehots_made, onehots_used = sem("onehots_made"), sem("onehots_used")
        gates_placed = sem("gates_placed")
        hidden_ready, gelu_done, weights_ready = sem("hidden_ready"), sem("gelu_done"), sem("weights_ready")
        expert_vec, expert_act = sem("expert_vec"), sem("expert_act")
        params_loaded, phase_done = sem("params_loaded"), sem("phase_done")
        stored = sem("stored")

        plan = weight_plan(phases)
        begin, end, n_chunks = {}, {}, 0
        for key, chunks in plan:
            begin[key] = n_chunks
            n_chunks += len(chunks)
            end[key] = n_chunks

        def whole(name):
            a = x[name]
            dims = "abcdef"[:len(a.shape)]
            return a.rearrange(f"{' '.join(dims)} -> ({' '.join(dims)})")

        params, A = {}, {}

        def param(phase, dst, src):
            params.setdefault(phase, []).append((dst, src))

        def everywhere(ap, parts=P):
            return ap.partition_broadcast(parts)

        def norm_params(phase, g, b, l):
            param(phase, norm_gb[:, 0, :], everywhere(x[g][l]))
            if b is not None:
                param(phase, norm_gb[:, 1, :], everywhere(x[b][l]))

        for phase in phases:
            m = arena()
            a = A[phase] = {}
            if phase == "retention":
                a["qT"], a["kT"] = m.take(8, T), m.take(8, T)
                a["v"], a["g"] = m.take(TB, RET_HV), m.take(TB, RET_HV)
                a["y"] = m.take(TB, RET_HV)
                a["decay"] = m.take(4, TB * T)
                a["s"] = m.take(4, TB, T)
                a["tmp"] = m.take(2, 4, T)
                a["gn"] = m.take(2, RET_HV)
                a["ahead"] = m.take(2, TB * T)
                a["cos"], a["sin"] = m.take(T), m.take(T)
                a["posi"], a["ang"], a["turn"] = m.take(T), m.take(T), m.take(T)
                a["lg"] = m.take(8)
                a["freq"] = m.take(1)
                a["yT"] = a["v"].rearrange("p a b -> p (a b)").rearrange("p (k t) -> p k t", t=T)
                param(phase, a["posi"].bitcast(I32), everywhere(x["positions"][0]))
                param(phase, a["freq"], x["c_ret_freq"])
                param(phase, a["ahead"].rearrange("p a b -> p (a b)"), x["c_ahead"])
                param(phase, a["lg"], everywhere(whole("ret_log1m_decay")))
                param(phase, a["gn"][:, 0, :], everywhere(x["ret_gn_g"][0]))
                param(phase, a["gn"][:, 1, :], everywhere(x["ret_gn_b"][0]))
                norm_params(phase, "ln_mix_g", "ln_mix_b", 0)
            if phase.startswith("peer"):
                l = int(phase[-1])
                a["keysT"], a["qT"] = m.take(HC, NK), m.take(HC, T)
                a["s"], a["s2"] = m.take(TB, HC, NK), m.take(TB, HC, NK)
                a["val"], a["idx"], a["idxf"] = (m.take(TB, HC, TOPK) for _ in range(3))
                a["cand"], a["cand2"] = m.take(TB, PH, TOPK * TOPK), m.take(TB, PH, TOPK * TOPK)
                a["top"], a["pos"], a["ab"], a["abf"] = m.take(TB, PH, TOPK), m.take(TB, PH, TOPK), m.take(2, TB, PH, TOPK), m.take(2, TB, PH, TOPK)
                a["sel"] = m.take(PH, TOPK, TOPK)
                a["ijg"] = m.take(3, TB, PH, TOPK)
                a["den"] = m.take(TB, PH)
                a["G"] = arena().take(T, NK)
                norm_params(phase, "ln_ffn_g", "ln_ffn_b", l)

            if phase == "mla":
                a["c"], a["sq"] = m.take(TB, MLA_IN), m.take(TB, Q_RANK + KV_RANK)
                a["cT"], a["krT"] = m.take(5, T), m.take(T, parts=ROPE)
                a["qnT"], a["knT"] = m.take(MLA_HEADS, T), m.take(MLA_HEADS, T)
                a["qr"], a["qrT"] = m.take(TB, MLA_HEADS, ROPE), m.take(MLA_HEADS, T, parts=ROPE)
                a["v"], a["oT"] = m.take(TB, MLA_HEADS * VDIM), m.take(MLA_HEADS, T)
                a["p"], a["pT"] = m.take(TB, 4, T), m.take(4, TB, T)
                a["tmp"] = m.take(4, TB * 4 * ROPE // 2)
                a["cos"], a["sin"], a["ang"], a["turn"] = (m.take(TB, ROPE // 2) for _ in range(4))
                a["freq"], a["posi"], a["pos"] = m.take(ROPE // 2), m.take(TB), m.take(TB)
                a["gain"] = m.take(Q_RANK + KV_RANK)
                param(phase, a["freq"], x["c_mla_freq"])
                param(phase, a["posi"].bitcast(I32), x["positions_cols"])
                param(phase, a["gain"][:, 0:Q_RANK], everywhere(x["mla_q_norm"][0]))
                param(phase, a["gain"][:, Q_RANK:], everywhere(x["mla_kv_norm"][0]))
                norm_params(phase, "ln_mix_g", "ln_mix_b", 1)
            if phase == "mixers":
                U = (UN, C)
                a["pv"] = m.take(TB, POOL_W + DIFF_W)
                a["qk"] = m.take(2, 8, T, parts=C)
                a["poolT"], a["oT"] = m.take(4, T, parts=C), m.take(4, T)
                a["alibi"] = m.take(TB, 4, T)
                late = Memory(sb, m.at, 2048)
                a["pool"] = m.take(TB, 4, T)
                a["rk"], a["X"] = late.take(*U, parts=C), late.take(*U, parts=C)
                a["pool_w"] = m.take(4, C, parts=C)
                a["masks"] = m.take(2 * C + LEVELS * C + NH * T, parts=C)
                a["w2"], a["a2"] = m.take(RWKV_W, parts=C), m.take(RWKV_W, parts=C)
                a["g2"] = m.take(2, RWKV_W, parts=C)
                a["ln"] = m.take(2, RWKV_W, parts=C)
                a["channels"] = m.take(16 + 6 * NH + 4, parts=C)
                a["mu"] = a["channels"][:, 0:16]
                a["cols"] = a["channels"][:, 16:16 + 6 * NH].rearrange("p (i h) -> p i h", h=NH)
                a["qk_gain"] = a["channels"][:, 16 + 6 * NH:].rearrange("p (w c) -> p w c", w=2)
                a["pend"] = m.take(UN, parts=C)
                a["lq"], a["lam"] = m.take(2, 2, C), m.take(8)
                a["ones"] = m.take(C, parts=C)
                late = Memory(sb, m.at, 2048)
                a["hn"] = m.take(TB, D)
                a["kk2"], a["kx"] = late.take(NH, T, parts=C), late.take(NH, T, parts=C)
                late = Memory(sb, late.at - 2048, 2048)
                a["Tm"], a["TmT"] = late.take(*U, parts=C), late.take(*U, parts=C)
                late = Memory(sb, late.at - 2048, 2048)
                a["o"], a["osq"] = late.take(TB, 4, P), late.take(TB, 4, P)
                late = Memory(sb, m.at, 4112)
                a["z"] = m.take(16, T + 1, parts=C)
                a["lw"], a["L"], a["Pd"], a["Pp"] = (late.take(NH, T, parts=C) for _ in range(4))
                late = Memory(sb, late.at - 4096, 4096)
                a["tm"] = late.take(4, *U, parts=C)
                a["rT"] = a["tm"][:, 0].rearrange("p u c -> p (u c)").rearrange("p (h t) -> p h t", h=NH)
                late = Memory(sb, m.at, 4096)
                a["zm"] = m.take(16, T, parts=C)
                a["Q"], a["Mt"], a["y"], a["ysq"] = (late.take(*U, parts=C) for _ in range(4))
                late = Memory(sb, late.at - 4096, 4096)
                a["rs"] = late.take(2, 8, T, parts=C)
                late = Memory(sb, m.at, 2048)
                a["ar"] = m.take(UN, 2, C, parts=C)
                a["pT"] = late.take(4, TB, T)
                late = Memory(sb, m.at, 4096)
                a["mab"], a["mak"] = m.take(UN, 2 * C, parts=C), m.take(UN, 2 * C, parts=C)
                a["p"] = late.take(2, TB, 4, T)
                late = Memory(sb, late.at - 4096, 4096)
                a["sq"] = late.take(2, 8, T, parts=C)
                late = Memory(sb, lasting_at["pair"], 3072)
                a["Pi"], a["a"], a["kk"] = (late.take(NH, T, parts=C) for _ in range(3))
                late = Memory(sb, late.at - 3072, 3072)
                a["aoff"], a["AkV"], a["G1"] = (late.take(*U, parts=C) for _ in range(3))
                a["U0"] = a["aoff"]
                late = Memory(sb, lasting_at["hT"], 2048)
                a["bt"], a["kt"] = late.take(*U, parts=C), late.take(*U, parts=C)
                late = Memory(sb, lasting_at["norm_gb"], 2048)
                a["g"], a["d"] = late.take(4, RWKV_W, parts=C), late.take(4, T, parts=C)
                a["S"] = Memory(sb, lasting_at["routes"], 768).take(3, NH, C, parts=C)
                norm_params(phase, "mix_norm_g_2", None, 0)
                param(phase, a["pool"].rearrange("p a b c -> p (a b c)"), x["c_pool"])
                param(phase, a["alibi"].rearrange("p a b c -> p (a b c)"), x["c_alibi"])
                param(phase, a["masks"], x["c_rwkv"])
                param(phase, a["pool_w"], x["pool_w_2"][0].rearrange("g c d -> c g d"))
                param(phase, a["w2"], x["rwkv_w2_2"][0])
                param(phase, a["a2"], x["rwkv_a2_2"][0])
                param(phase, a["g2"], x["rwkv_g2_2"][0].rearrange("(s p) c -> p s c", p=C))
                param(phase, a["ln"][:, 0, :], everywhere(x["rwkv_ln_w_2"][0], C))
                param(phase, a["ln"][:, 1, :], everywhere(x["rwkv_ln_b_2"][0], C))
                param(phase, a["channels"], x["channel_cols"])
                for i, name in enumerate(("diff_lq1_2", "diff_lk1_2", "diff_lq2_2", "diff_lk2_2")):
                    param(phase, a["lq"][:, i % 2, i // 2, :], everywhere(x[name][0]))
                param(phase, misc[:, 0:P], everywhere(x["diff_subln_2"][0]))
            if phase == "cross":
                a["mem"], a["mn"], a["hn"], a["mT"] = m.take(TB, D), m.take(TB, D), m.take(TB, D), m.take(KD, T)
                a["k"], a["q"], a["v"], a["sq"] = (m.take(TB, D) for _ in range(4))
                a["kT"], a["qT"] = m.take(KD, T), m.take(KD, T)
                a["p"], a["pT"], a["oT"] = m.take(TB, 4, T), m.take(4, TB, T), m.take(KD, T)
                a["gain"] = m.take(2, XD)
                param(phase, a["mem"], x["mem_2"][0].rearrange("(b p) d -> p b d", p=P))
                param(phase, norm_gb[:, 0, :], everywhere(x["mem_norm_g_2"][0]))
                param(phase, norm_gb[:, 1, :], everywhere(x["xa_norm_g_2"][0]))
                param(phase, a["gain"][:, 0, :], everywhere(x["xa_k_norm_2"][0]))
                param(phase, a["gain"][:, 1, :], everywhere(x["xa_q_norm_2"][0]))
            if phase == "ffn":
                a["hn"], a["hid"] = m.take(TB, D), m.take(FF_TILES, T)
                a["conv"] = m.take(2, 4, T)
                a["taps_bias"] = m.take(4 * FF_TILES)
                a["taps"] = a["taps_bias"][:, 0:3 * FF_TILES].rearrange("p (w t) -> p w t", w=3)
                a["bias"] = a["taps_bias"][:, 3 * FF_TILES:]
                norm_params(phase, "ffn_norm_g_2", None, 0)
                param(phase, a["taps_bias"], x["conv_cols"])

        gates_before, experts_before = {}, {}
        for n, phase in enumerate(p for p in phases if p.startswith("peer")):
            gates_before[phase], experts_before[phase] = n * T // 4, n * NK

        def onehot_views():
            v = pair[:, 0:2048].rearrange("p (w b q n) -> p w b q n", w=2, b=2, q=4)
            return v[:, 0], v[:, 1]

        def expert_views():
            return (pair[:, 0:2048].rearrange("p (b k e) -> p b k e", b=2, k=KD),
                    pair[:, 2048:2560].rearrange("p (b t) -> p b t", b=2),
                    pair[:, 2560:3072].rearrange("p (b t) -> p b t", b=2))

        block = ctx.enter_context(nc.Block())

        @block.sync
        def _(sync):
            def chunk_source(name, l, r0, k, runs):
                if name == "sub_keys":
                    return x["peer_sub_keys"][l].rearrange("h c k d -> k (h c) d")[:, r0 * 8:r0 * 8 + 8, :]
                c0, w = runs[0]
                if len(runs) == 2:
                    return x[name][l][r0:r0 + k, :].rearrange("k (two f) -> k two f", two=2)[:, :, c0:c0 + w]
                return x[name][l][r0:r0 + k, c0:c0 + w]

            def expert_rows(name, l):
                return x[name][l].rearrange("(i j) d -> i j d", j=NK)

            def load(n, k, src):
                if n >= RING:
                    sync.wait_ge(chunks_done, n - RING + 1)
                cols = src.shape[-1] * (src.shape[1] if len(src.shape) == 3 else 1)
                dst = ring[0:k, n % RING, 0:cols]
                if len(src.shape) == 3:
                    dst = dst.rearrange("p (a b) -> p a b", a=src.shape[1])
                sync.dma_start(dst, src).then_inc(ring_loaded[n % RING], 16)

            n = 0
            for key, chunks in plan:
                if not key.endswith("_experts"):
                    for name, l, r0, k, runs in chunks:
                        load(n, k, chunk_source(name, l, r0, k, runs))
                        n += 1
                    continue
                l = int(key[4])
                u, v = expert_rows("peer_u", l), expert_rows("peer_v", l)
                load(n, P, u[0])
                n += 1
                with sync.Fori(0, 31) as it:
                    for r in range(8):
                        m = n + r
                        src = (u[it * 4 + (1 + r // 2)] if r % 2 == 0 else v[it * 4 + r // 2])
                        sync.wait_ge(chunks_done, it * 8 + (m - RING + 1))
                        sync.dma_start(ring[:, m % RING, :], src).then_inc(ring_loaded[m % RING], 16)
                n += 31 * 8
                for j in range(125, NK + 1):
                    if j < NK:
                        load(n, P, u[j])
                        n += 1
                    load(n, P, v[j - 1])
                    n += 1
            sync.wait_ge(phase_done, len(phases))
            for tb in range(TB):
                sync.dma_start(out[0, tb * P:(tb + 1) * P, :], h[:, tb, :]).then_inc(stored, 16)
            sync.wait_ge(stored, 16 * TB)

        @block.gpsimd
        def _(gp):
            gp.dma_start(ident, x["c_ident"]).then_inc(params_loaded, 16)
            gp.dma_start(iota, x["c_iota"]).then_inc(params_loaded, 16)
            for tb in range(TB):
                gp.dma_start(h[:, tb, :], x["x"][0, tb * P:(tb + 1) * P, :]).then_inc(params_loaded, 16)
            for n, phase in enumerate(phases):
                if n:
                    gp.wait_ge(phase_done, n)
                for dst, src in params.get(phase, []):
                    gp.dma_start(dst, src).then_inc(params_loaded, 16)

        loads, at = {}, 4
        for phase in phases:
            at += len(params.get(phase, []))
            loads[phase] = 16 * at

        @block.tensor
        def _(pe):
            banks = Banks({"v": vec_served, "a": act_served})
            to_pe, act_to_pe = Count(), Count()

            def hold(bs):
                for who, served in banks.served.items():
                    owed = [banks.of[b][1] for b in bs if b in banks.of and banks.of[b][0] is served]
                    if owed:
                        pe.wait_ge(served, max(owed))

            def arrived(n):
                pe.wait_ge(ring_loaded[n % RING], 16 * (n // RING + 1))

            def panel(key, lhs, form, b0, tiles, free=None, widths=None, k_rows=None):
                kk = end[key] - begin[key]
                for k in range(kk):
                    n = begin[key] + k
                    rows_ = k_rows[k] if k_rows else P
                    arrived(n)
                    w = ring[0:rows_, n % RING, :]
                    if form == "tokens":
                        todo = [(ps(b0 + 2 * tb + c // BANK, 1)[:, 0:min(BANK, tiles - c)],
                                 lhs(k)[:, tb * P:(tb + 1) * P], w[:, c:min(c + BANK, tiles)], True)
                                for tb in range(TB) for c in range(0, tiles, BANK)]
                    else:
                        todo = []
                        at = 0
                        for i, wd in enumerate(tiles):
                            b = ps(b0 + i // 2, 1, wd)
                            todo.append((b[:, (i % 2) * T:(i % 2) * T + T], w[:, at:at + wd], lhs(k), i % 2 == 0))
                            at += wd
                    for o, a, b, first in todo:
                        mm = pe.matmul(o, a, b, start=(k == 0 and first), stop=(k == kk - 1), skip_group_check=True)
                    mm.then_inc(chunks_done, 1)

            def transpose_in(src, n_k, k_rows=P, b0=0):
                per = BANK // T
                nb = n_k // per
                for k in range(n_k):
                    for tb in range(TB):
                        mm = pe.transpose(ps(b0 + k // per, 1, k_rows)[:, (k % per) * T + tb * P:(k % per) * T + (tb + 1) * P],
                                          src(k, tb), ident)
                    if k == n_k // 2 - 1:
                        mm.then_inc(psum_for_vec, 1)
                mm.then_inc(psum_for_act, 1)
                return [banks.lend(range(b0, b0 + nb // 2), "v"), banks.lend(range(b0 + nb // 2, b0 + nb), "a")]

            def wait_all(tokens):
                for s, v in tokens:
                    pe.wait_ge(s, v)

            def stream_T(n, src=None):
                if src is not None:
                    pe.wait_ge(vec_for_pe, to_pe.up())
                elif n:
                    pe.wait_ge(phase_done, n)
                else:
                    pe.wait_ge(params_loaded, loads[phases[0]])
                src = h if src is None else src
                hold(range(4))
                wait_all(transpose_in(lambda k, tb: src[:, tb, k * P:(k + 1) * P], KD))

            def hk(k):
                return hT[:, k, :]

            def pe_retention(a):
                full = [P] * 8
                for n, who in enumerate("vvaaaa"):
                    b0 = 4 * ((n + 1) % 2)
                    hold(range(b0, b0 + 4))
                    if n < 2:
                        panel(f"ret_in{n}", hk, "features", b0, full)
                    else:
                        panel(f"ret_in{n}", hk, "tokens", b0, 1024)
                    tok = banks.lend(range(b0, b0 + 4), who)
                    if n == 1:
                        rotated = tok
                    if n == 3:
                        v_ready = tok
                pe.wait_ge(*rotated)
                hold(range(4, 8))
                for hd in range(RET_HEADS):
                    for mb in range(TB):
                        for d in range(2):
                            mm = pe.matmul(ps(4 + hd, 1)[:, mb * T:(mb + 1) * T],
                                           a["kT"][:, 2 * hd + d, mb * P:(mb + 1) * P], a["qT"][:, 2 * hd + d, :],
                                           start=(mb == 0 and d == 0), stop=(d == 1), skip_group_check=True)
                mm.then_inc(psum_for_vec, 1)
                decayed = banks.lend(range(4, 8), "v")
                pe.wait_ge(*decayed)
                pe.wait_ge(*v_ready)
                for tb in range(TB):
                    b0 = 4 * tb
                    hold(range(b0, b0 + 4))
                    for hd in range(RET_HEADS):
                        for mb in range(TB):
                            mm = pe.matmul(ps(b0 + hd, 1), a["s"][:, hd, mb, tb * P:(tb + 1) * P],
                                           a["v"][:, mb, hd * BANK:(hd + 1) * BANK], start=(mb == 0), stop=(mb == 1))
                    mm.then_inc(psum_for_vec, 1)
                    gated = banks.lend(range(b0, b0 + 4), "v")
                pe.wait_ge(*gated)
                toks = []
                for half in range(2):
                    toks += transpose_in(lambda k, tb: a["y"][:, tb, (8 * half + k) * P:(8 * half + k + 1) * P], 8, b0=4 * half)
                wait_all(toks)
                hold(range(4))
                panel("ret_out", lambda k: a["yT"][:, k, :], "tokens", 0, D)
                banks.lend(range(4), "v")

            def pe_peer(phase, a):
                hold(range(4, 8))
                for n in range(2):
                    c = begin[phase + "_keys"] + n
                    arrived(c)
                    for i in range(8):
                        hc = 8 * n + i
                        mm = pe.transpose(ps(4 + hc // 4, 1)[:, (hc % 4) * P:(hc % 4 + 1) * P],
                                          ring[:, c % RING, i * P:(i + 1) * P], ident)
                    mm.then_inc(chunks_done, 1)
                keys = [banks.lend(range(4, 6), "v"), banks.lend(range(6, 8), "a")]
                for n in range(2):
                    b0 = 4 * n
                    hold(range(b0, b0 + 4))
                    panel(f"{phase}_q{n}", hk, "features", b0, [P] * 8)
                    q = banks.lend(range(b0, b0 + 4), "a")
                    keys.append(q)
                wait_all(keys)
                for tb in range(TB):
                    b0 = 4 * tb
                    hold(range(b0, b0 + 4))
                    for hc in range(HC):
                        mm = pe.matmul(ps(b0 + hc // 4, 1)[:, (hc % 4) * P:(hc % 4 + 1) * P],
                                       a["qT"][:, hc, tb * P:(tb + 1) * P], a["keysT"][:, hc, :],
                                       start=(hc % 4 == 0), stop=True, skip_group_check=True)
                    mm.then_inc(psum_for_act, 1)
                    banks.lend(range(b0, b0 + 4), "a")
                pe.wait_ge(vec_for_pe, to_pe.up())
                hold([0, 1])
                for w in range(3):
                    for tb in range(TB):
                        mm = pe.transpose(ps(0, 2)[:, w * T + tb * P:w * T + (tb + 1) * P],
                                          a["ijg"][:, w, tb, :, :].rearrange("p a b -> p (a b)"), ident)
                mm.then_inc(psum_for_vec, 1)
                banks.lend([0, 1], "v")
                A_, B_ = onehot_views()
                for b in (2, 3):
                    hold([b])
                base = gates_before[phase]

                def gate_group(g, half, fresh):
                    if not fresh:
                        pe.wait_ge(gates_placed, g + (base - 1))
                    pe.wait_ge(onehots_made, g + (base + 1))
                    for q in range(4):
                        mm = pe.matmul(ps(2 + half, 1)[:, q * P:(q + 1) * P], B_[:, half, q, :], A_[:, half, q, :],
                                       start=(q == 0), stop=True, skip_group_check=True)
                    mm.then_inc(onehots_used, 1)

                gate_group(0, 0, True)
                gate_group(1, 1, True)
                with pe.Fori(1, T // 8) as it:
                    for half in range(2):
                        gate_group(it * 2 + half, half, False)
                uT, gel, w_ = expert_views()
                e0 = begin[phase + "_experts"]
                d0 = experts_before[phase]
                pe.wait_ge(gates_placed, base + T // 4)
                hold(range(0, 8))

                def T_(slot, round_, i, fresh=False):
                    pe.wait_ge(ring_loaded[slot], round_)
                    if not fresh:
                        pe.wait_ge(expert_vec, i)
                        pe.wait_ge(expert_act, i)
                    for k in range(KD):
                        mm = pe.transpose(ps(4 + k // 4, 1)[:, (k % 4) * P:(k % 4 + 1) * P],
                                          ring[:, slot, k * P:(k + 1) * P], ident)
                    mm.then_inc(chunks_done, 1)

                def H_(buf, i, fresh=False):
                    pe.wait_ge(expert_vec, i + 1)
                    pe.wait_ge(expert_act, i + 1)
                    if not fresh:
                        pe.wait_ge(gelu_done, i - 1)
                    for k in range(KD):
                        mm = pe.matmul(ps(6 + buf, 1)[:, 0:T], uT[:, buf, k, :], hT[:, k, :],
                                       start=(k == 0), stop=(k == KD - 1))
                    mm.then_inc(hidden_ready, 1)

                def Y_(slot, round_, buf, i, first=False, last=False):
                    pe.wait_ge(ring_loaded[slot], round_)
                    pe.wait_ge(weights_ready, i + 1)
                    for tb in range(TB):
                        for c in range(2):
                            mm = pe.matmul(ps(2 * tb + c, 1), w_[:, buf, tb * P:(tb + 1) * P],
                                           ring[:, slot, c * BANK:(c + 1) * BANK], start=first, stop=last,
                                           skip_group_check=True)
                    mm.then_inc(chunks_done, 1)

                def rv(n):
                    return 16 * (n // RING + 1)

                T_(e0 % RING, rv(e0), d0, fresh=True)
                H_(0, d0, fresh=True)
                n = e0 + 1

                def turn(i, n, buf, first=False):
                    T_(n[0] % RING, n[1], i)
                    Y_(n[2] % RING, n[3], 1 - buf, i - 1, first=first)
                    H_(buf, i, fresh=first)
                turn(d0 + 1, (n, rv(n), n + 1, rv(n + 1)), 1, first=True)
                n += 2
                with pe.Fori(0, 31) as it:
                    for r in range(4):
                        a0, a1 = n + 2 * r, n + 2 * r + 1
                        turn(it * 4 + (d0 + 2 + r), (a0, it * 16 + rv(a0), a1, it * 16 + rv(a1)), r % 2)
                n += 31 * 8
                for i in range(126, NK):
                    turn(d0 + i, (n, rv(n), n + 1, rv(n + 1)), i % 2)
                    n += 2
                Y_(n % RING, rv(n), 1, d0 + NK - 1, last=True)
                banks.lend(range(4), "v")

            def turn_p(p, b0):
                return transpose_in(lambda k, tb: p[:, tb, k // TB, (k % TB) * P:(k % TB + 1) * P], 8, b0=b0)

            def pe_mla(a):
                hold(range(4, 8))
                panel("mla_in", hk, "tokens", 4, MLA_IN)
                pe.wait_ge(*banks.lend(range(4, 8), "v"))
                hold(range(3))
                for k in range(5):
                    for tb in range(TB):
                        pe.transpose(ps(k // 2, 1)[:, (k % 2) * T + tb * P:(k % 2) * T + (tb + 1) * P],
                                     a["c"][:, tb, k * P:(k + 1) * P], ident)
                for tb in range(TB):
                    mm = pe.transpose(ps(2, 1, ROPE)[:, T + tb * P:T + (tb + 1) * P],
                                      a["c"][:, tb, Q_RANK + KV_RANK:MLA_IN], ident)
                mm.then_inc(psum_for_vec, 1)
                pe.wait_ge(*banks.lend(range(3), "v"))
                toks = []
                for n in range(2):
                    b0 = 4 * (1 - n)
                    hold(range(b0, b0 + 3))
                    for k in range(3):
                        c = begin[f"mla_uq{n}"] + k
                        arrived(c)
                        w = ring[:, c % RING, 0:768].rearrange("p (h e) -> p h e", h=4)
                        lat = a["cT"][:, k, :]
                        for hd in range(4):
                            pe.matmul(ps(b0 + hd // 2, 1)[:, (hd % 2) * T:(hd % 2 + 1) * T], w[:, hd, 0:NOPE], lat,
                                      start=(k == 0 and hd % 2 == 0), stop=(k == 2), skip_group_check=True)
                        for tb in range(TB):
                            mm = pe.matmul(ps(b0 + 2, 1)[:, tb * T:(tb + 1) * T].rearrange("p (h e) -> p h e", h=4),
                                           lat[:, tb * P:(tb + 1) * P], w[:, :, NOPE:],
                                           start=(k == 0 and tb == 0), stop=(k == 2), skip_group_check=True)
                        mm.then_inc(chunks_done, 1)
                    toks += [banks.lend([b0, b0 + 1], "a"), banks.lend([b0 + 2], "v")]
                for n in range(2):
                    b0 = 4 * (1 - n)
                    hold(range(b0, b0 + 4))
                    for k in range(2):
                        c = begin[f"mla_ukv{n}"] + k
                        arrived(c)
                        w = ring[:, c % RING, :].rearrange("p (h e) -> p h e", h=4)
                        lat = a["cT"][:, 3 + k, :]
                        for hd in range(4):
                            pe.matmul(ps(b0 + hd // 2, 1)[:, (hd % 2) * T:(hd % 2 + 1) * T], w[:, hd, 0:NOPE], lat,
                                      start=(k == 0 and hd % 2 == 0), stop=(k == 1), skip_group_check=True)
                        for tb in range(TB):
                            mm = pe.matmul(ps(b0 + 2 + tb, 1).rearrange("p (h e) -> p h e", h=4),
                                           lat[:, tb * P:(tb + 1) * P], w[:, :, NOPE:],
                                           start=(k == 0), stop=(k == 1), skip_group_check=True)
                        mm.then_inc(chunks_done, 1)
                    toks += [banks.lend([b0, b0 + 1], "a"), banks.lend([b0 + 2, b0 + 3], "v")]
                wait_all(toks[:4])
                hold(range(4, 8))
                for hd in range(MLA_HEADS):
                    for tb in range(TB):
                        mm = pe.transpose(ps(4 + hd // 2, 1, ROPE)[:, (hd % 2) * T + tb * P:(hd % 2) * T + (tb + 1) * P],
                                          a["qr"][:, tb, hd, :], ident)
                mm.then_inc(psum_for_act, 1)
                toks.append(banks.lend(range(4, 8), "a"))
                wait_all(toks[4:])
                for n in range(2):
                    hold(range(4))
                    for tb in range(TB):
                        for i in range(4):
                            hd = 4 * n + i
                            o = ps(2 * tb + i // 2, 1)[:, (i % 2) * T:(i % 2 + 1) * T]
                            pe.matmul(o, a["qnT"][:, hd, tb * P:(tb + 1) * P], a["knT"][:, hd, :],
                                      start=(i % 2 == 0), stop=False, skip_group_check=True)
                            mm = pe.matmul(o, a["qrT"][:, hd, tb * P:(tb + 1) * P], a["krT"],
                                           start=False, stop=True, skip_group_check=True)
                    mm.then_inc(psum_for_vec, 1)
                    pe.wait_ge(*banks.lend(range(4), "v"))
                    hold(range(4, 8))
                    wait_all(turn_p(a["p"], 4))
                    hold([0, 1])
                    for i in range(4):
                        for kb in range(TB):
                            mm = pe.matmul(ps(i // 2, 1)[:, (i % 2) * T:(i % 2 + 1) * T],
                                           a["v"][:, kb, (4 * n + i) * VDIM:(4 * n + i + 1) * VDIM], a["pT"][:, i, kb, :],
                                           start=(i % 2 == 0 and kb == 0), stop=(kb == 1), skip_group_check=True)
                    mm.then_inc(psum_for_act, 1)
                    o_ready = banks.lend([0, 1], "a")
                pe.wait_ge(*o_ready)
                hold(range(4, 8))
                panel("mla_out", lambda k: a["oT"][:, k, :], "tokens", 4, D)
                banks.lend(range(4, 8), "v")

            def pe_mixers(a):
                for n in range(4):
                    b0 = 4 * ((n + 1) % 2)
                    hold(range(b0, b0 + 4))
                    panel(f"slots{n}", hk, "features", b0, [C] * 8)
                    banks.lend(range(b0, b0 + 4), "a")
                hold(range(4, 8))
                panel("diff_v", hk, "tokens", 4, DIFF_W)
                banks.lend(range(4, 8), "a")
                hold(range(4))
                panel("pool_in", hk, "tokens", 0, POOL_W)
                pe.wait_ge(*banks.lend(range(4), "a"))
                hold([0, 1])
                for g in range(4):
                    for tb in range(TB):
                        mm = pe.matmul(ps(g // 2, 1, C)[:, (g % 2) * T:(g % 2 + 1) * T],
                                       a["pv"][:, tb, g * C:(g + 1) * C], a["pool"][:, tb, g, :],
                                       start=(g % 2 == 0 and tb == 0), stop=(tb == 1), skip_group_check=True)
                mm.then_inc(psum_for_vec, 1)
                pe.wait_ge(*banks.lend([0, 1], "v"))
                hold([2, 3])
                for g in range(4):
                    mm = pe.matmul(ps(2 + g // 2, 1, C)[:, (g % 2) * T:(g % 2 + 1) * T], a["pool_w"][:, g, :],
                                   a["d"][:, g, :], start=(g % 2 == 0), stop=True, skip_group_check=True)
                mm.then_inc(psum_for_vec, 1)
                banks.lend([2, 3], "v")
                pe.wait_ge(act_for_pe, act_to_pe.up())
                hold(range(6))
                for w, (wt, slot) in enumerate((("w2", 12), ("a2", 13))):
                    for hd in range(NH):
                        mm = pe.matmul(ps(2 * w + hd // 2, 1, C)[:, (hd % 2) * T:(hd % 2 + 1) * T],
                                       a[wt][:, hd * C:(hd + 1) * C], a["zm"][:, slot, :],
                                       start=(hd % 2 == 0), stop=True, skip_group_check=True)
                for c in range(NC_):
                    for s in range(2):
                        mm = pe.matmul(ps(4 + c // 2, 1, C)[:, (c % 2) * T:(c % 2 + 1) * T],
                                       a["zm"][:, 14 + s, c * C:(c + 1) * C], a["g2"][:, s, :],
                                       start=(c % 2 == 0 and s == 0), stop=(s == 1), skip_group_check=True)
                mm.then_inc(psum_for_act, 1)
                banks.lend(range(6), "a")
                pe.wait_ge(vec_for_pe, to_pe.up())
                hold([6, 7])
                for i in range(2):
                    mm = pe.matmul(ps(6 + i, 1, C), a["ones"], a["kk2"][:, 2 * i:2 * i + 2, :].rearrange("p h t -> p (h t)"),
                                   start=True, stop=True)
                mm.then_inc(psum_for_act, 1)
                banks.lend([6, 7], "a")
                pe.wait_ge(vec_for_pe, to_pe.up())
                hold(range(8))
                vz = a["zm"][:, 8:12, :].rearrange("p h (c t) -> p (h c) t", c=NC_)
                idc = ident[0:C, 0:C]
                for w in range(4):
                    for u in range(UN):
                        src = (a["ar"][:, u, 0, :], a["bt"][:, u, :], a["kt"][:, u, :], vz[:, u, :])[w]
                        mm = pe.transpose(ps(2 * w + u // 8, 1, C)[:, (u % 8) * C:(u % 8 + 1) * C], src, idc)
                    if w == 1:
                        mm.then_inc(psum_for_act, 1)
                mm.then_inc(psum_for_vec, 1)
                turned = [banks.lend(range(4), "a"), banks.lend(range(4, 8), "v")]
                for w, src in enumerate(("bt", "kt")):
                    hold(range(4 * w, 4 * w + 4))
                    for u in range(UN):
                        mm = pe.matmul(ps(4 * w + u // 4, 1, C)[:, (u % 4) * P:(u % 4 + 1) * P], a[src][:, u, :],
                                       a["ar"][:, u, :, :].rearrange("p w t -> p (w t)"), start=(u % 4 == 0), stop=True,
                                       skip_group_check=True)
                    mm.then_inc(psum_for_vec, 1)
                    masked = banks.lend(range(4 * w, 4 * w + 4), "v")
                pe.wait_ge(*masked)
                wait_all(turned)

                def units(b0, lhs, rhs, first=True, last=True, us=range(UN)):
                    for u in us:
                        mm = pe.matmul(ps(b0 + u // 8, 1, C)[:, (u % 8) * C:(u % 8 + 1) * C], lhs(u), rhs(u),
                                       start=(first and u % 8 == 0), stop=last, skip_group_check=True)
                    return mm

                def of(name):
                    return lambda u: a[name][:, u, :]

                def part(name, w):
                    return lambda u: a[name][:, u, w * C:(w + 1) * C]

                def tm(w):
                    return lambda u: a["tm"][:, w, u, :]

                for b in range(LEVELS):
                    pe.wait_ge(vec_for_pe, to_pe.up())
                    hold([0, 1])
                    units(0, of("aoff"), of("Tm")).then_inc(psum_for_vec, 1)
                    pe.wait_ge(*banks.lend([0, 1], "v"))
                    hold(range(2, 6))
                    units(2, of("TmT"), of("X"))
                    units(4, of("X"), of("TmT")).then_inc(psum_for_vec, 1)
                    inverse = banks.lend(range(2, 6), "v")
                hold([0, 1])
                units(0, part("mak", 0), tm(3)).then_inc(psum_for_act, 1)
                akv = banks.lend([0, 1], "a")
                pe.wait_ge(*inverse)
                hold([2, 3])
                units(2, of("TmT"), tm(0)).then_inc(psum_for_vec, 1)
                g1 = banks.lend([2, 3], "v")
                pe.wait_ge(*akv)
                hold([6, 7])
                units(6, of("TmT"), of("AkV")).then_inc(psum_for_act, 1)
                u0 = banks.lend([6, 7], "a")
                pe.wait_ge(*g1)
                hold(range(4))
                units(0, of("G1"), part("mab", 1))
                units(2, of("G1"), tm(1)).then_inc(psum_for_vec, 1)
                qm = banks.lend(range(4), "v")
                hold([4, 5])
                units(4, lambda u: a["rk"][:, u, :], lambda u: a["ones"]).then_inc(psum_for_act, 1)
                banks.lend([4, 5], "a")
                pe.wait_ge(*u0)
                pe.wait_ge(*qm)
                hold(range(0, 8))
                units(0, part("mab", 1), of("U0"), last=False)
                units(0, part("mak", 1), tm(3), first=False, last=False)
                for c in range(NC_):
                    mine = [hd * NC_ + c for hd in range(NH)]
                    if c:
                        pe.wait_ge(*state)
                        mm = units(0, of("Q"), lambda u: a["S"][:, c - 1, u // NC_, :], first=False, us=mine)
                    if c < NC_ - 1:
                        terms = [(tm(1), of("U0")), (tm(2), tm(3))]
                        if c:
                            terms.append((of("Mt"), lambda u: a["S"][:, c - 1, u // NC_, :]))
                        for i, (lhs, rhs) in enumerate(terms):
                            for u in mine:
                                hd = u // NC_
                                mm = pe.matmul(ps(2 + c, 1, C)[:, hd * C:(hd + 1) * C], lhs(u), rhs(u),
                                               start=(i == 0 and hd == 0), stop=(i == len(terms) - 1), skip_group_check=True)
                        mm.then_inc(psum_for_vec, 1)
                        state = banks.lend([2 + c], "v")
                mm.then_inc(psum_for_vec, 1)
                pe.wait_ge(*banks.lend([0, 1], "v"))
                hold([6, 7])
                for u in range(UN):
                    mm = pe.transpose(ps(6 + u // 8, 1, C)[:, (u % 8) * C:(u % 8 + 1) * C], a["y"][:, u, :], idc)
                mm.then_inc(psum_for_act, 1)
                rwkv = banks.lend([6, 7], "a")
                pe.wait_ge(act_for_pe, act_to_pe.up())
                pe.wait_ge(*rwkv)
                hold(range(8))
                for i in range(8):
                    mm = pe.matmul(ps(i, 1, C), a["ones"],
                                   a["sq"][:, i // 4, 2 * (i % 4):2 * (i % 4) + 2, :].rearrange("p s t -> p (s t)"),
                                   start=True, stop=True)
                mm.then_inc(psum_for_vec, 1)
                pe.wait_ge(*banks.lend(range(8), "v"))
                for c in range(2):
                    b0 = 4 * c
                    for tb in range(TB):
                        for hd in range(4):
                            mm = pe.matmul(ps(b0 + 2 * tb + hd // 2, 1)[:, (hd % 2) * T:(hd % 2 + 1) * T],
                                           a["qk"][:, 0, 2 * hd + c, tb * P:(tb + 1) * P], a["qk"][:, 1, 2 * hd + c, :],
                                           start=(hd % 2 == 0), stop=True, skip_group_check=True)
                    mm.then_inc(psum_for_vec, 1)
                    probs = banks.lend(range(b0, b0 + 4), "v")
                pe.wait_ge(*probs)
                wait_all(turn_p(a["p"][:, 0], 4))
                hold([0, 1])
                for tb in range(TB):
                    for hd in range(4):
                        for kb in range(TB):
                            mm = pe.matmul(ps(tb, 1)[:, hd * P:(hd + 1) * P], a["pT"][:, hd, kb, tb * P:(tb + 1) * P],
                                           a["pv"][:, kb, POOL_W + hd * P:POOL_W + (hd + 1) * P],
                                           start=(hd == 0 and kb == 0), stop=(kb == 1), skip_group_check=True)
                mm.then_inc(psum_for_vec, 1)
                pe.wait_ge(*banks.lend([0, 1], "v"))
                hold([2, 3])
                for hd in range(4):
                    for tb in range(TB):
                        mm = pe.transpose(ps(2 + hd // 2, 1)[:, (hd % 2) * T + tb * P:(hd % 2) * T + (tb + 1) * P],
                                          a["o"][:, tb, hd, :], ident)
                mm.then_inc(psum_for_act, 1)
                pe.wait_ge(*banks.lend([2, 3], "a"))
                hold(range(4, 8))
                lhs = [a["poolT"][:, i, :] for i in range(4)] + [a["rT"][:, i, :] for i in range(4)] + [a["oT"][:, i, :] for i in range(4)]
                panel("mix_out", lambda k: lhs[k], "tokens", 4, D, k_rows=[C] * 8 + [P] * 4)
                banks.lend(range(4, 8), "v")

            def pe_cross(a):
                pe.wait_ge(vec_for_pe, to_pe.up())
                hold(range(4, 8))
                wait_all(transpose_in(lambda k, tb: a["mn"][:, tb, k * P:(k + 1) * P], KD, b0=4))
                mk = lambda k: a["mT"][:, k, :]
                hold(range(4))
                panel("xa_wk_2", mk, "tokens", 0, D)
                kn = banks.lend(range(4), "v")
                hold(range(4, 8))
                panel("xa_wv_2", mk, "tokens", 4, D)
                vv = banks.lend(range(4, 8), "a")
                pe.wait_ge(*kn)
                hold(range(4))
                wait_all(transpose_in(lambda k, tb: a["k"][:, tb, k * P:(k + 1) * P], KD))
                stream_T(0, a["hn"])
                hold(range(4, 8))
                panel("xa_wq_2", hk, "tokens", 4, D)
                pe.wait_ge(*banks.lend(range(4, 8), "v"))
                hold(range(4))
                wait_all(transpose_in(lambda k, tb: a["q"][:, tb, k * P:(k + 1) * P], KD))
                hold(range(4, 8))
                for tb in range(TB):
                    for hd in range(XH):
                        for d in range(2):
                            mm = pe.matmul(ps(4 + 2 * tb + hd // 2, 1)[:, (hd % 2) * T:(hd % 2 + 1) * T],
                                           a["qT"][:, 2 * hd + d, tb * P:(tb + 1) * P], a["kT"][:, 2 * hd + d, :],
                                           start=(hd % 2 == 0 and d == 0), stop=(d == 1), skip_group_check=True)
                mm.then_inc(psum_for_vec, 1)
                pe.wait_ge(*banks.lend(range(4, 8), "v"))
                hold(range(4))
                wait_all(turn_p(a["p"], 0))
                pe.wait_ge(*vv)
                hold(range(4, 8))
                for i in range(8):
                    for kb in range(TB):
                        mm = pe.matmul(ps(4 + i // 2, 1)[:, (i % 2) * T:(i % 2 + 1) * T],
                                       a["v"][:, kb, i * P:(i + 1) * P], a["pT"][:, i // 2, kb, :],
                                       start=(i % 2 == 0 and kb == 0), stop=(kb == 1), skip_group_check=True)
                mm.then_inc(psum_for_act, 1)
                pe.wait_ge(*banks.lend(range(4, 8), "a"))
                hold(range(4))
                panel("xa_wo_2", lambda k: a["oT"][:, k, :], "tokens", 0, D)
                banks.lend(range(4), "v")

            def pe_ffn(a):
                for n in range(6):
                    b0 = 4 * ((n + 1) % 2)
                    hold(range(b0, b0 + 4))
                    panel(f"up{n}", hk, "features", b0, [P] * (2 * min(4, FF_TILES - 4 * n)))
                    hid = banks.lend(range(b0, b0 + 4), "v")
                pe.wait_ge(*hid)
                hold(range(4, 8))
                panel("down", lambda k: a["hid"][:, k, :], "tokens", 4, D)
                banks.lend(range(4, 8), "v")

            for n, phase in enumerate(phases):
                if phase in ("mixers", "ffn"):
                    stream_T(n, A[phase]["hn"])
                elif phase != "cross":
                    stream_T(n)
                if phase == "retention":
                    pe_retention(A[phase])
                if phase == "mla":
                    pe_mla(A[phase])
                if phase == "mixers":
                    pe_mixers(A[phase])
                if phase == "cross":
                    pe_cross(A[phase])
                if phase == "ffn":
                    pe_ffn(A[phase])
                if phase.startswith("peer"):
                    pe_peer(phase, A[phase])

        @block.vector
        def _(vec):
            own = Last(vec_step)
            psum_v, from_act = Count(), Count()

            def done():
                vec.wait_ge(*own.last)

            def ln_stream(key, b0, phase, n):
                flat = h.rearrange("p a b -> p (a b)")
                vec.wait_ge(chunks_done, end[key])
                vec.wait_ge(params_loaded, loads[phase])
                vec.scalar_tensor_tensor(flat, flat, ALPHA, ps(b0, 4), ALU.mult, ALU.add).then_inc(*own.mark(vec_served))
                done()
                for tb in range(TB):
                    for c in range(2):
                        vec.bn_stats(stats[:, 2 * tb + c, 0, :], h[:, tb, c * BANK:(c + 1) * BANK]).then_inc(*own.next())
                done()
                for tb in range(TB):
                    vec.bn_aggr(mv[:, tb, :], stats[:, 2 * tb:2 * tb + 2, 0, :]).then_inc(*own.next())
                done()
                vec.tensor_scalar(rstd[:, 0:TB], mv[:, :, 1], LN_EPS, None, ALU.add).then_inc(*own.mark(vec_for_act))
                vec.wait_ge(act_for_vec, from_act.up())
                vec.reciprocal(rstd[:, 0:TB], rstd[:, 0:TB]).then_inc(*own.next())
                done()
                for tb in range(TB):
                    vec.tensor_scalar(h[:, tb, :], h[:, tb, :], mv[:, tb, 0:1], rstd[:, tb:tb + 1],
                                      ALU.subtract, ALU.mult).then_inc(*own.next())
                done()
                vec.tensor_tensor(h, h, bcast(norm_gb[:, 0, :], 1, TB), ALU.mult).then_inc(*own.next())
                done()
                vec.tensor_tensor(h, h, bcast(norm_gb[:, 1, :], 1, TB), ALU.add).then_inc(*own.mark(phase_done))
                done()

            def take_turned(dst, b0):
                vec.wait_ge(psum_for_vec, psum_v.up())
                vec.tensor_copy(dst.rearrange("p a b -> p (a b)"), ps(b0, 2)).then_inc(*own.mark(vec_served))

            def reduced(dst, ang, turn, quarter):
                vec.tensor_scalar(turn, ang, 1.0 / (2 * np.pi), 0.25 if quarter else 0.0, ALU.mult, ALU.add).then_inc(*own.next())
                done()
                vec.tensor_scalar(turn, turn, ROUND, None, ALU.add).then_inc(*own.next())
                done()
                vec.tensor_scalar(turn, turn, -ROUND, None, ALU.add).then_inc(*own.next())
                done()
                vec.scalar_tensor_tensor(dst, turn, -TWO_PI_HI, ang, ALU.mult, ALU.add).then_inc(*own.next())
                done()
                vec.scalar_tensor_tensor(dst, turn, -TWO_PI_LO, dst, ALU.mult, ALU.add).then_inc(*own.next())
                done()
                if quarter:
                    vec.tensor_scalar(dst, dst, float(np.pi / 2), None, ALU.add).then_inc(*own.next())
                    done()
                vec.tensor_scalar(dst, dst, PI_IN, -PI_IN, ALU.min, ALU.max).then_inc(*own.next())
                done()

            def vec_retention(a, n, phase):
                vec.tensor_copy(a["ang"], a["posi"].bitcast(I32)).then_inc(*own.next())
                done()
                vec.tensor_scalar(a["ang"], a["ang"], a["freq"], None, ALU.mult).then_inc(*own.next())
                done()
                reduced(a["cos"], a["ang"], a["turn"], True)
                reduced(a["sin"], a["ang"], a["turn"], False)
                vec.tensor_copy(a["turn"], a["ang"]).then_inc(*own.mark(vec_for_act))
                vec.wait_ge(act_for_vec, from_act.up())
                for hd in range(RET_HEADS):
                    vec.tensor_scalar(a["decay"][:, hd, :], a["ahead"][:, 0, :], a["lg"][:, hd:hd + 1], None,
                                      ALU.mult).then_inc(*own.next())
                done()
                for hd in range(RET_HEADS):
                    vec.scalar_tensor_tensor(a["decay"][:, hd, :], a["ahead"][:, 1, :], a["lg"][:, 4 + hd:5 + hd],
                                             a["decay"][:, hd, :], ALU.mult, ALU.add).then_inc(
                        *(own.mark(vec_for_act) if hd == RET_HEADS - 1 else own.next()))
                vec.wait_ge(act_for_vec, from_act.up())
                cos, sin = bcast(a["cos"], 1, RET_HEADS), bcast(a["sin"], 1, RET_HEADS)
                for w, (dst, b0) in enumerate(((a["qT"], 4), (a["kT"], 0))):
                    vec.wait_ge(chunks_done, end[f"ret_in{w}"])
                    src = ps(b0, 4).rearrange("p (h two t) -> p h two t", two=2, t=T)
                    to = dst.rearrange("p (h two) t -> p h two t", two=2)
                    x1, x2 = src[:, :, 0, :], src[:, :, 1, :]
                    t1, t2 = a["tmp"][:, 0], a["tmp"][:, 1]
                    vec.tensor_tensor(t1, x1, cos, ALU.mult).then_inc(*own.next())
                    vec.tensor_tensor(t2, x2, sin, ALU.mult).then_inc(*own.next())
                    done()
                    vec.tensor_tensor(to[:, :, 0, :], t1, t2, ALU.subtract).then_inc(*own.next())
                    done()
                    vec.tensor_tensor(t1, x1, sin, ALU.mult).then_inc(*own.next())
                    vec.tensor_tensor(t2, x2, cos, ALU.mult).then_inc(*own.next())
                    done()
                    vec.tensor_tensor(to[:, :, 1, :], t1, t2, ALU.add).then_inc(*own.mark(vec_served))
                    done()
                vec.wait_ge(psum_for_vec, psum_v.up())
                vec.scalar_tensor_tensor(a["s"].rearrange("p a b c -> p (a b c)"), ps(4, 4), RET_DK ** -0.5,
                                         a["decay"].rearrange("p a b -> p (a b)"), ALU.mult, ALU.mult).then_inc(*own.mark(vec_served))
                for tb in range(TB):
                    vec.wait_ge(psum_for_vec, psum_v.up())
                    for hd in range(RET_HEADS):
                        vec.bn_stats(stats[:, hd, 0, :], ps(4 * tb + hd, 1)).then_inc(*own.next())
                    done()
                    for hd in range(RET_HEADS):
                        vec.bn_aggr(var8[:, 4 * tb + hd, :], stats[:, hd, 0, :]).then_inc(*own.next())
                    done()
                    r = rstd[:, 4 * tb:4 * tb + 4]
                    vec.tensor_scalar(r, var8[:, 4 * tb:4 * tb + 4, 1], LN_EPS, None, ALU.add).then_inc(*own.mark(vec_for_act))
                    vec.wait_ge(act_for_vec, from_act.up())
                    vec.reciprocal(r, r).then_inc(*own.next())
                    done()
                    for hd in range(RET_HEADS):
                        vec.tensor_scalar(a["y"][:, tb, hd * BANK:(hd + 1) * BANK], ps(4 * tb + hd, 1),
                                          var8[:, 4 * tb + hd, 0:1], r[:, hd:hd + 1], ALU.subtract, ALU.mult).then_inc(*own.next())
                    done()
                    y = a["y"][:, tb, :]
                    vec.tensor_tensor(y, y, a["gn"][:, 0, :], ALU.mult).then_inc(*own.next())
                    done()
                    vec.tensor_tensor(y, y, a["gn"][:, 1, :], ALU.add).then_inc(*own.next())
                    done()
                    vec.tensor_tensor(y, y, a["g"][:, tb, :], ALU.mult).then_inc(*own.mark(vec_served))
                    done()
                take_turned(a["yT"][:, 0:4, :], 0)
                take_turned(a["yT"][:, 8:12, :], 4)
                ln_stream("ret_out", 0, phase, n)

            def rms_stream(src, dst, gain, phase):
                vec.wait_ge(params_loaded, loads[phase])
                for tb in range(TB):
                    for c in range(2):
                        vec.bn_stats(stats[:, 2 * tb + c, 0, :], src[:, tb, c * BANK:(c + 1) * BANK]).then_inc(*own.next())
                done()
                for tb in range(TB):
                    vec.bn_aggr(mv[:, tb, :], stats[:, 2 * tb:2 * tb + 2, 0, :]).then_inc(*own.next())
                done()
                r = rstd[:, 0:TB]
                vec.tensor_tensor(r, mv[:, :, 0], mv[:, :, 0], ALU.mult).then_inc(*own.next())
                done()
                vec.scalar_tensor_tensor(r, r, RMS_EPS, mv[:, :, 1], ALU.add, ALU.add).then_inc(*own.mark(vec_for_act))
                vec.wait_ge(act_for_vec, from_act.up())
                vec.reciprocal(r, r).then_inc(*own.next())
                done()
                for tb in range(TB):
                    vec.scalar_tensor_tensor(dst[:, tb, :], src[:, tb, :], rstd[:, tb:tb + 1], gain, ALU.mult, ALU.mult).then_inc(
                        *(own.mark(vec_for_pe) if tb == TB - 1 else own.next()))
                done()

            def add_stream(key, b0):
                flat = h.rearrange("p a b -> p (a b)")
                vec.wait_ge(chunks_done, end[key])
                vec.tensor_tensor(flat, flat, ps(b0, 4), ALU.add).then_inc(*own.mark(vec_served))
                done()
                vec.tensor_copy(misc[:, 511:512], rstd[:, 0:1]).then_inc(*own.mark(phase_done))
                done()

            def softmax(src, p, top, total, last):
                rows_ = p.rearrange("p b h k -> p (b h) k")
                vec.tensor_reduce(top, src, AX, ALU.max).then_inc(*own.next())
                done()
                vec.tensor_tensor(rows_, src, bcast(top, 2, T), ALU.subtract).then_inc(*own.mark(vec_for_act))
                vec.wait_ge(act_for_vec, from_act.up())
                vec.tensor_reduce(total, rows_, AX, ALU.add).then_inc(*own.next())
                done()
                vec.reciprocal(total, total).then_inc(*own.next())
                done()
                vec.tensor_tensor(rows_, rows_, bcast(total, 2, T), ALU.mult).then_inc(*last())
                done()

            def served():
                return own.mark(vec_served)

            def from_psum():
                vec.wait_ge(psum_for_vec, psum_v.up())

            def rooted(v, scale, eps):
                vec.tensor_scalar(v, v, scale, eps, ALU.mult, ALU.add).then_inc(*own.mark(vec_for_act))
                vec.wait_ge(act_for_vec, from_act.up())
                vec.reciprocal(v, v).then_inc(*own.next())
                done()

            top8, sum8 = misc[:, 256:264], misc[:, 264:272]

            def vec_mla(a, n, phase):
                half = ROPE // 2
                vec.wait_ge(params_loaded, loads[phase])
                vec.tensor_copy(a["pos"], a["posi"].bitcast(I32)).then_inc(*own.next())
                done()
                for tb in range(TB):
                    vec.tensor_scalar(a["ang"][:, tb, :], a["freq"], a["pos"][:, tb:tb + 1], None, ALU.mult).then_inc(*own.next())
                done()
                reduced(a["cos"], a["ang"], a["turn"], True)
                reduced(a["sin"], a["ang"], a["turn"], False)
                vec.tensor_copy(a["turn"], a["ang"]).then_inc(*own.mark(vec_for_act))
                vec.wait_ge(chunks_done, end["mla_in"])
                c, r = a["c"], rstd[:, 0:4]
                vec.tensor_copy(c, ps(4, 4).rearrange("p (b c) -> p b c", b=TB)[:, :, 0:MLA_IN]).then_inc(*own.next())
                done()
                vec.tensor_tensor(a["sq"], c[:, :, 0:Q_RANK + KV_RANK], c[:, :, 0:Q_RANK + KV_RANK], ALU.mult).then_inc(*own.next())
                done()
                vec.tensor_reduce(r[:, 0:2], a["sq"][:, :, 0:Q_RANK], AX, ALU.add).then_inc(*own.next())
                vec.tensor_reduce(r[:, 2:4], a["sq"][:, :, Q_RANK:], AX, ALU.add).then_inc(*own.next())
                done()
                vec.tensor_scalar(r[:, 0:2], r[:, 0:2], 1.0 / Q_RANK, LN_EPS, ALU.mult, ALU.add).then_inc(*own.next())
                vec.wait_ge(act_for_vec, from_act.up())
                vec.tensor_scalar(r[:, 2:4], r[:, 2:4], 1.0 / KV_RANK, LN_EPS, ALU.mult, ALU.add).then_inc(*own.mark(vec_for_act))
                vec.wait_ge(act_for_vec, from_act.up())
                vec.reciprocal(r, r).then_inc(*own.next())
                done()
                for tb in range(TB):
                    for i, s in enumerate((slice(0, Q_RANK), slice(Q_RANK, Q_RANK + KV_RANK))):
                        vec.scalar_tensor_tensor(c[:, tb, s], c[:, tb, s], r[:, 2 * i + tb:2 * i + tb + 1], a["gain"][:, s],
                                                 ALU.mult, ALU.mult).then_inc(*own.next())

                def rotate(x1, x2, o1, o2, cos, sin, t):
                    vec.tensor_tensor(t[0], x1, cos, ALU.mult).then_inc(*own.next())
                    vec.tensor_tensor(t[1], x2, sin, ALU.mult).then_inc(*own.next())
                    vec.tensor_tensor(t[2], x1, sin, ALU.mult).then_inc(*own.next())
                    vec.tensor_tensor(t[3], x2, cos, ALU.mult).then_inc(*own.next())
                    done()
                    vec.tensor_tensor(o1, t[0], t[1], ALU.subtract).then_inc(*own.next())
                    vec.tensor_tensor(o2, t[2], t[3], ALU.add).then_inc(*own.mark(vec_served))
                    done()

                k1, k2 = c[:, :, MLA_IN - ROPE:MLA_IN - half], c[:, :, MLA_IN - half:]
                rotate(k1, k2, k1, k2, a["cos"], a["sin"],
                       [a["tmp"][:, i, 0:TB * half].rearrange("p (b e) -> p b e", b=TB) for i in range(4)])
                from_psum()
                vec.tensor_copy(a["cT"].rearrange("p a b -> p (a b)"), ps(0, 3)[:, 0:5 * T]).then_inc(*own.next())
                vec.tensor_copy(a["krT"], ps(2, 1, ROPE)[:, T:]).then_inc(*served())
                for i in range(2):
                    b0 = 4 * (1 - i)
                    vec.wait_ge(chunks_done, end[f"mla_uq{i}"])
                    q = ps(b0 + 2, 1).rearrange("p (b h e) -> p b h e", b=TB, h=4)
                    to = a["qr"][:, :, 4 * i:4 * i + 4, :]
                    rotate(q[:, :, :, 0:half], q[:, :, :, half:], to[:, :, :, 0:half], to[:, :, :, half:],
                           bcast(a["cos"], 2, 4), bcast(a["sin"], 2, 4),
                           [a["tmp"][:, j, :].rearrange("p (b h e) -> p b h e", b=TB, h=4) for j in range(4)])
                for i in range(2):
                    b0 = 4 * (1 - i)
                    vec.wait_ge(chunks_done, end[f"mla_ukv{i}"])
                    vec.tensor_copy(a["v"][:, :, i * BANK:(i + 1) * BANK],
                                    ps(b0 + 2, 2).rearrange("p (b c) -> p b c", b=TB)).then_inc(*served())
                for i in range(2):
                    from_psum()
                    softmax(ps(0, 4).rearrange("p (r k) -> p r k", k=T), a["p"], top8, sum8, served)
                    take_turned(a["pT"].rearrange("p h k t -> p (h k) t")[:, 0:4, :], 4)
                ln_stream("mla_out", 4, phase, n)

            def vec_mixers(a):
                cols, zm = a["cols"], a["zm"]

                def col(i):
                    return bcast(cols[:, i, :], 2, T)

                def u3(v):
                    return v.rearrange("p h (c t) -> p (h c) t", c=NC_)

                def flat(v):
                    return v.rearrange("p a b -> p (a b)")

                vec.memset(a["z"][:, :, 0:1], 0.0).then_inc(*own.next())
                vec.memset(a["ones"], 1.0).then_inc(*own.next())
                vec.wait_ge(act_for_vec, from_act.up())
                done()
                vec.tensor_tensor(zm, a["z"][:, :, 0:T], a["z"][:, :, 1:T + 1], ALU.subtract).then_inc(*own.next())
                done()
                vec.tensor_tensor(zm, zm, bcast(a["mu"], 2, T), ALU.mult).then_inc(*own.next())
                done()
                vec.tensor_tensor(zm, zm, a["z"][:, :, 1:T + 1], ALU.add).then_inc(*own.mark(vec_for_act))
                done()
                from_psum()
                vec.tensor_copy(flat(a["d"]), ps(0, 2, C)).then_inc(*served())
                from_psum()
                vec.tensor_tensor(a["poolT"], ps(2, 2, C).rearrange("p (h t) -> p h t", t=T), col(5), ALU.mult).then_inc(*served())
                r_, k_ = zm[:, 0:4, :], zm[:, 4:8, :]
                vec.tensor_tensor(a["kk"], k_, col(2), ALU.mult).then_inc(*own.next())
                vec.wait_ge(act_for_vec, from_act.up())
                vec.tensor_scalar(a["lw"], a["lw"], -float(np.exp(-0.5)), None, ALU.mult).then_inc(*own.next())
                done()
                vec.tensor_tensor_scan(flat(a["L"]), a["masks"][:, (2 + LEVELS) * C:], flat(a["lw"]), 0.0,
                                       ALU.mult, ALU.add).then_inc(*own.next())
                done()
                vec.tensor_tensor(a["Pp"], a["L"], a["lw"], ALU.subtract).then_inc(*own.mark(vec_for_act))
                done()
                vec.tensor_tensor(a["kk2"], a["kk"], a["kk"], ALU.mult).then_inc(*own.mark(vec_for_pe))
                kx = a["kx"]
                vec.tensor_scalar(kx, a["a"], -1.0, None, ALU.add).then_inc(*own.next())
                done()
                vec.tensor_tensor(kx, kx, col(3), ALU.mult).then_inc(*own.next())
                done()
                vec.scalar_tensor_tensor(kx, kx, 1.0, k_, ALU.add, ALU.mult).then_inc(*own.next())
                done()
                rk = a["rk"].rearrange("p (h c) t -> p h (c t)", h=NH)
                vec.tensor_tensor(rk, r_, kx, ALU.mult).then_inc(*own.next())
                done()
                vec.tensor_tensor(rk, rk, col(4), ALU.mult).then_inc(*own.next())
                vec.wait_ge(act_for_vec, from_act.up())
                vec.tensor_tensor(a["ar"][:, :, 1, :], u3(r_), u3(a["Pd"]), ALU.mult).then_inc(*own.next())
                vec.tensor_tensor(a["kt"], u3(kx), u3(a["Pi"]), ALU.mult).then_inc(*own.next())
                vec.tensor_copy(a["pend"], u3(a["Pd"])[:, :, C - 1]).then_inc(*own.next())
                vec.wait_ge(act_for_vec, from_act.up())
                n2 = a["kk2"]
                vec.tensor_scalar(n2, n2, 1e-12, None, ALU.max).then_inc(*own.next())
                done()
                vec.reciprocal(n2, n2).then_inc(*own.next())
                done()
                vec.tensor_tensor(a["kk"], a["kk"], n2, ALU.mult).then_inc(*own.next())
                done()
                vec.scalar_tensor_tensor(a["ar"][:, :, 0, :], u3(a["kk"]), -1.0, u3(a["Pp"]), ALU.mult, ALU.mult).then_inc(*own.next())
                done()
                vec.tensor_tensor(a["kk"], a["kk"], a["a"], ALU.mult).then_inc(*own.next())
                done()
                vec.tensor_tensor(a["bt"], u3(a["kk"]), u3(a["Pi"]), ALU.mult).then_inc(*own.mark(vec_for_pe))
                done()
                from_psum()
                vec.tensor_copy(a["tm"][:, 2:4].rearrange("p w u c -> p (w u c)"), ps(4, 4, C)).then_inc(*served())
                for i, name in enumerate(("mab", "mak")):
                    from_psum()
                    vec.tensor_tensor(a[name], ps(4 * i, 4, C).rearrange("p (u t) -> p u t", u=UN),
                                      bcast(a["masks"][:, 0:2 * C], 1, UN), ALU.mult).then_inc(*served())
                idc = bcast(ident[0:C, 0:C], 1, UN)
                vec.tensor_copy(a["Tm"], idc).then_inc(*own.next())
                vec.tensor_copy(a["TmT"], idc).then_inc(*own.next())
                done()

                def units(b0):
                    return ps(b0, 2, C).rearrange("p (u c) -> p u c", u=UN)

                for b in range(LEVELS):
                    vec.tensor_tensor(a["aoff"], a["mab"][:, :, 0:C], bcast(a["masks"][:, (2 + b) * C:(3 + b) * C], 1, UN),
                                      ALU.mult).then_inc(*own.mark(vec_for_pe))
                    from_psum()
                    vec.tensor_copy(a["X"], units(0)).then_inc(*served())
                    from_psum()
                    vec.tensor_tensor(a["Tm"], a["Tm"], units(2), ALU.add).then_inc(*own.next())
                    vec.tensor_tensor(a["TmT"], a["TmT"], units(4), ALU.add).then_inc(*served())
                    done()
                from_psum()
                vec.tensor_copy(a["G1"], units(2)).then_inc(*served())
                from_psum()
                vec.tensor_tensor(a["Q"], units(0), a["ar"][:, :, 1, :], ALU.add).then_inc(*own.next())
                vec.tensor_tensor(a["Mt"], units(2), idc, ALU.add).then_inc(*served())
                pend = a["pend"].rearrange("p (h c) -> p h c", h=NH)
                for c in range(NC_ - 1):
                    from_psum()
                    vec.tensor_tensor(a["S"][:, c], ps(2 + c, 1, C)[:, 0:NH * C].rearrange("p (h v) -> p h v", h=NH),
                                      bcast(pend[:, :, c], 2, C), ALU.mult).then_inc(*served())
                from_psum()
                y, ysq, mean, var = a["y"], a["ysq"], rstd[0:C, :], misc[0:C, 288:304]
                vec.tensor_reduce(mean, units(0), AX, ALU.add).then_inc(*own.next())
                done()
                vec.tensor_scalar(mean, mean, 1.0 / C, None, ALU.mult).then_inc(*own.next())
                done()
                vec.tensor_tensor(y, units(0), bcast(mean, 2, C), ALU.subtract).then_inc(*own.next())
                done()
                vec.tensor_tensor(ysq, y, y, ALU.mult).then_inc(*own.next())
                done()
                vec.tensor_reduce(var, ysq, AX, ALU.add).then_inc(*own.next())
                done()
                rooted(var, 1.0 / C, RWKV_EPS)
                vec.tensor_tensor(y, y, bcast(var, 2, C), ALU.mult).then_inc(*own.next())
                vec.tensor_tensor(a["X"], a["X"], a["tm"][:, 3], ALU.mult).then_inc(*own.next())
                done()
                y4 = y.rearrange("p (h c) v -> p h c v", h=NH)
                for i, op in enumerate((ALU.mult, ALU.add)):
                    for hd in range(NH):
                        vec.tensor_tensor(y4[:, hd], y4[:, hd], bcast(a["ln"][:, i, hd * C:(hd + 1) * C], 1, NC_), op).then_inc(*own.next())
                    done()
                vec.tensor_tensor(y, y, a["X"], ALU.add).then_inc(*own.next())
                done()
                g4 = a["g"].rearrange("p c (h v) -> p h c v", h=NH)
                for hd in range(NH):
                    vec.tensor_tensor(y4[:, hd], y4[:, hd], g4[:, hd], ALU.mult).then_inc(*(served() if hd == NH - 1 else own.next()))
                done()
                lq, lam = a["lq"], a["lam"]
                vec.tensor_tensor(lq[:, 0], lq[:, 0], lq[:, 1], ALU.mult).then_inc(*own.next())
                done()
                vec.tensor_reduce(lam[:, 0:2], lq[:, 0], AX, ALU.add).then_inc(*own.mark(vec_for_act))
                vec.wait_ge(act_for_vec, from_act.up())
                vec.tensor_tensor(lam[:, 2:3], lam[:, 1:2], lam[:, 0:1], ALU.subtract).then_inc(*own.next())
                done()
                vec.tensor_scalar(lam[:, 2:3], lam[:, 2:3], -LAMBDA_INIT, None, ALU.add).then_inc(*own.next())
                from_psum()
                rs = a["rs"].rearrange("p w s t -> p (w s t)")
                vec.tensor_scalar(rs, ps(0, 8, C), 1.0 / C, RMS_EPS, ALU.mult, ALU.add).then_inc(*own.mark(vec_for_act))
                vec.wait_ge(act_for_vec, from_act.up())
                vec.reciprocal(rs, rs).then_inc(*own.next())
                done()
                qk = a["qk"]
                vec.tensor_tensor(qk, qk, a["rs"], ALU.mult).then_inc(*own.next())
                done()
                for w in range(2):
                    for c in range(2):
                        v = qk[:, w].rearrange("p (h c) t -> p h c t", c=2)[:, :, c, :]
                        vec.tensor_scalar(v, v, a["qk_gain"][:, w, c:c + 1], None, ALU.mult).then_inc(
                            *(served() if w and c else own.next()))
                done()
                for c in range(2):
                    from_psum()
                    p = a["p"][:, c]
                    rows_ = p.rearrange("p b h k -> p (b h) k")
                    vec.scalar_tensor_tensor(p.rearrange("p b h k -> p (b h k)"), ps(4 * c, 4), C ** -0.5,
                                             a["alibi"].rearrange("p b h k -> p (b h k)"), ALU.mult, ALU.add).then_inc(*own.next())
                    done()
                    softmax(rows_, p, top8, sum8, own.next if c else served)
                p0 = a["p"][:, 0].rearrange("p b h k -> p (b h k)")
                vec.scalar_tensor_tensor(p0, a["p"][:, 1].rearrange("p b h k -> p (b h k)"), lam[:, 2:3], p0,
                                         ALU.mult, ALU.add).then_inc(*served())
                take_turned(a["pT"].rearrange("p h k t -> p (h k) t")[:, 0:4, :], 4)
                from_psum()
                o, osq = (a[w].rearrange("p b h v -> p (b h) v") for w in ("o", "osq"))
                vec.tensor_copy(o, ps(0, 2).rearrange("p (r v) -> p r v", v=P)).then_inc(*own.next())
                done()
                vec.tensor_tensor(osq, o, o, ALU.mult).then_inc(*own.next())
                done()
                vec.tensor_reduce(sum8, osq, AX, ALU.add).then_inc(*own.next())
                done()
                rooted(sum8, 1.0 / P, RMS_EPS)
                vec.tensor_tensor(o, o, bcast(sum8, 2, P), ALU.mult).then_inc(*own.next())
                done()
                vec.scalar_tensor_tensor(o, o, 1.0 - LAMBDA_INIT, bcast(misc[:, 0:P], 1, 8), ALU.mult, ALU.mult).then_inc(*served())
                add_stream("mix_out", 4)

            def vec_cross(a, phase):
                rms_stream(a["mem"], a["mn"], norm_gb[:, 0, :], phase)
                rms_stream(h, a["hn"], norm_gb[:, 1, :], phase)
                take_turned(a["mT"][:, 0:4, :], 4)

                def head_norm(key, b0, dst, gain):
                    vec.wait_ge(chunks_done, end[key])
                    d8, s8 = (v.rearrange("p b (h e) -> p (b h) e", h=XH) for v in (dst, a["sq"]))
                    vec.tensor_copy(d8, ps(b0, 4).rearrange("p (r e) -> p r e", e=XD)).then_inc(*own.next())
                    done()
                    vec.tensor_tensor(s8, d8, d8, ALU.mult).then_inc(*own.next())
                    done()
                    vec.tensor_reduce(sum8, s8, AX, ALU.add).then_inc(*own.next())
                    done()
                    rooted(sum8, 1.0 / XD, RMS_EPS)
                    vec.tensor_tensor(d8, d8, bcast(sum8, 2, XD), ALU.mult).then_inc(*own.next())
                    done()
                    vec.tensor_tensor(d8, d8, bcast(gain, 1, 8), ALU.mult).then_inc(*served())

                head_norm("xa_wk_2", 0, a["k"], a["gain"][:, 0, :])
                take_turned(a["kT"][:, 0:4, :], 0)
                take_turned(hT[:, 0:4, :], 0)
                head_norm("xa_wq_2", 4, a["q"], a["gain"][:, 1, :])
                take_turned(a["qT"][:, 0:4, :], 0)
                from_psum()
                softmax(ps(4, 4).rearrange("p (r k) -> p r k", k=T), a["p"], top8, sum8, served)
                take_turned(a["pT"].rearrange("p h k t -> p (h k) t")[:, 0:4, :], 0)
                add_stream("xa_wo_2", 0)

            def vec_ffn(a):
                for n in range(6):
                    b0, w = 4 * ((n + 1) % 2), min(4, FF_TILES - 4 * n)
                    vec.wait_ge(chunks_done, end[f"up{n}"])
                    v = ps(b0, 4).rearrange("p (i t) -> p i t", t=T)
                    c = a["conv"][:, n % 2]
                    for i in range(w):
                        f = 4 * n + i
                        vec.tensor_scalar(c[:, i, :], v[:, i, :], a["taps"][:, 2, f:f + 1], a["bias"][:, f:f + 1],
                                          ALU.mult, ALU.add).then_inc(*own.next())
                    done()
                    for tap in (1, 0):
                        back = 2 - tap
                        for i in range(w):
                            f = 4 * n + i
                            vec.scalar_tensor_tensor(c[:, i, back:], v[:, i, 0:T - back], a["taps"][:, tap, f:f + 1],
                                                     c[:, i, back:], ALU.mult, ALU.add).then_inc(
                                *(own.mark(vec_for_act) if tap == 0 and i == w - 1 else own.next()))
                        done()
                    vec.wait_ge(act_for_vec, from_act.up())
                    vec.tensor_tensor(a["hid"][:, 4 * n:4 * n + w, :], c[:, 0:w, :], v[:, w:2 * w, :], ALU.mult).then_inc(*served())
                add_stream("down", 4)

            def top_sixteen(n, src, spare, val, idx):
                for i in range(n):
                    vec.max(val(i)[:, 0:8], src(i)).then_inc(*own.next())
                done()
                for i in range(n):
                    vec.max_index(idx(i)[:, 0:8], val(i)[:, 0:8], src(i)).then_inc(*own.next())
                for i in range(n):
                    vec.match_replace(spare(i), val(i)[:, 0:8], src(i), LOWEST).then_inc(*own.next())
                done()
                for i in range(n):
                    vec.max(val(i)[:, 8:16], spare(i)).then_inc(*own.next())
                done()
                for i in range(n):
                    vec.max_index(idx(i)[:, 8:16], val(i)[:, 8:16], spare(i)).then_inc(*own.next())
                done()

            def vec_peer(a, n, phase):
                vec.wait_ge(chunks_done, end[phase + "_keys"])
                vec.tensor_copy(a["keysT"][:, 0:8, :].rearrange("p a b -> p (a b)"), ps(4, 2)).then_inc(*own.mark(vec_served))
                vec.wait_ge(act_for_vec, from_act.up(TB))
                for tb in range(TB):
                    s, s2, val, idx = a["s"][:, tb], a["s2"][:, tb], a["val"][:, tb], a["idx"][:, tb].bitcast(U32)
                    top_sixteen(HC, lambda i: s[:, i, :], lambda i: s2[:, i, :], lambda i: val[:, i, :], lambda i: idx[:, i, :])
                    idxf = a["idxf"][:, tb]
                    vec.tensor_copy(idxf, idx).then_inc(*own.next())
                    v1 = val.rearrange("p (h c) k -> p h c k", c=2)
                    cand, cand2 = a["cand"][:, tb], a["cand2"][:, tb]
                    c4 = cand.rearrange("p h (a b) -> p h a b", a=TOPK)
                    for hd in range(PH):
                        vec.tensor_tensor(c4[:, hd], bcast(v1[:, hd, 0, :], 2, TOPK), bcast(v1[:, hd, 1, :], 1, TOPK),
                                          ALU.add).then_inc(*own.next())
                    done()
                    top, pos = a["top"][:, tb], a["pos"][:, tb].bitcast(U32)
                    top_sixteen(PH, lambda i: cand[:, i, :], lambda i: cand2[:, i, :], lambda i: top[:, i, :], lambda i: pos[:, i, :])
                    ab = a["ab"][:, :, tb].bitcast(U32)
                    vec.tensor_scalar(ab[:, 0], pos, 4, None, ALU.logical_shift_right).then_inc(*own.next())
                    vec.tensor_scalar(ab[:, 1], pos, 15, None, ALU.bitwise_and).then_inc(*own.next())
                    done()
                    abf = a["abf"][:, :, tb]
                    vec.tensor_copy(abf, ab).then_inc(*own.next())
                    done()
                    i1 = idxf.rearrange("p (h c) k -> p h c k", c=2)
                    sel = a["sel"]
                    for w in range(2):
                        for hd in range(PH):
                            vec.tensor_tensor(sel[:, hd], bcast(abf[:, w, hd, :], 2, TOPK), bcast(iota[:, 0:TOPK], 1, TOPK),
                                              ALU.is_equal).then_inc(*own.next())
                        done()
                        for hd in range(PH):
                            vec.tensor_tensor(sel[:, hd], sel[:, hd], bcast(i1[:, hd, w, :], 1, TOPK), ALU.mult).then_inc(*own.next())
                        done()
                        vec.tensor_reduce(a["ijg"][:, w, tb], sel, AX, ALU.add).then_inc(*own.next())
                        done()
                    gate = a["ijg"][:, 2, tb]
                    vec.tensor_tensor(gate, top, top[:, :, 0:1].broadcast_to([P, PH, TOPK]), ALU.subtract).then_inc(*own.mark(vec_for_act))
                    vec.wait_ge(act_for_vec, from_act.up())
                    den = a["den"][:, tb]
                    vec.tensor_reduce(den, gate, AX, ALU.add).then_inc(*own.next())
                    done()
                    vec.reciprocal(den, den).then_inc(*own.next())
                    done()
                    vec.tensor_tensor(gate, gate, bcast(den, 2, TOPK), ALU.mult).then_inc(
                        *(own.mark(vec_for_pe) if tb == TB - 1 else own.next()))
                    done()
                vec.wait_ge(psum_for_vec, psum_v.up())
                vec.tensor_copy(routes.rearrange("p a b -> p (a b)"), ps(0, 2)[:, 0:3 * T]).then_inc(*own.mark(vec_served))
                done()
                A_, B_ = onehot_views()
                base = gates_before[phase]

                def onehots(g, half, fresh):
                    if not fresh:
                        vec.wait_ge(onehots_used, g + (base - 1))
                    for q in range(4):
                        vec.tensor_scalar(A_[:, half, q, :], iota, routes[:, 0, bass.ds(g * 4 + q, 1)],
                                          routes[:, 2, bass.ds(g * 4 + q, 1)], ALU.is_equal, ALU.mult)
                    for q in range(4):
                        mm = vec.tensor_scalar(B_[:, half, q, :], iota, routes[:, 1, bass.ds(g * 4 + q, 1)],
                                               None, ALU.is_equal)
                    mm.then_inc(onehots_made, 1)

                onehots(0, 0, True)
                onehots(1, 1, True)
                with vec.Fori(1, T // 8) as it:
                    for half in range(2):
                        onehots(it * 2 + half, half, False)
                uT, gel, w_ = expert_views()
                e0, d0 = begin[phase + "_experts"], experts_before[phase]
                G = a["G"]

                def turned(chunk, i, buf):
                    vec.wait_ge(chunks_done, chunk + 1)
                    vec.tensor_copy(uT[:, buf, 0:4, :].rearrange("p a b -> p (a b)"), ps(4, 1)).then_inc(expert_vec, 1)

                def weigh(i, tile, buf):
                    vec.wait_ge(gelu_done, i + 1)
                    vec.tensor_tensor(w_[:, buf, :], gel[:, buf, :], G[:, :, bass.ds(tile, 1)].rearrange("p t o -> p (t o)"),
                                      ALU.mult).then_inc(weights_ready, 1)

                turned(e0, d0, 0)
                weigh(d0, 0, 0)
                turned(e0 + 1, d0 + 1, 1)
                weigh(d0 + 1, 1, 1)
                with vec.Fori(0, 31) as it:
                    for r in range(4):
                        turned(it * 8 + (e0 + 3 + 2 * r), it * 4 + (d0 + 2 + r), r % 2)
                        weigh(it * 4 + (d0 + 2 + r), it * 4 + (2 + r), r % 2)
                for i in range(126, NK):
                    turned(e0 + 2 * i - 1, d0 + i, i % 2)
                    weigh(d0 + i, i, i % 2)
                ln_stream(phase + "_experts", 0, phase, n)

            for n, phase in enumerate(phases):
                if n == 0:
                    vec.wait_ge(params_loaded, loads[phase])
                if phase in ("mixers", "ffn"):
                    rms_stream(h, A[phase]["hn"], norm_gb[:, 0, :], phase)
                if phase != "cross":
                    take_turned(hT[:, 0:4, :], 0)
                if phase == "retention":
                    vec_retention(A[phase], n, phase)
                if phase == "mla":
                    vec_mla(A[phase], n, phase)
                if phase == "mixers":
                    vec_mixers(A[phase])
                if phase == "cross":
                    vec_cross(A[phase], phase)
                if phase == "ffn":
                    vec_ffn(A[phase])
                if phase.startswith("peer"):
                    vec_peer(A[phase], n, phase)

        @block.scalar
        def _(act):
            own = Last(act_step)
            psum_a, from_vec = Count(), Count()

            def done():
                act.wait_ge(*own.last)

            def copy_turned(dst, b0, nb=2):
                act.wait_ge(psum_for_act, psum_a.up())
                act.activation(dst.rearrange("p a b -> p (a b)"), ps(b0, nb), ACT.Copy).then_inc(*own.mark(act_served))

            def root(v):
                act.wait_ge(vec_for_act, from_vec.up())
                act.activation(v, v, ACT.Sqrt).then_inc(*own.mark(act_for_vec))

            def act_retention(a):
                lg = a["lg"]
                act.activation(lg, lg, ACT.Exp).then_inc(*own.next())
                done()
                act.activation(lg, lg, ACT.Ln, scale=-1.0, bias=1.0).then_inc(*own.mark(act_for_vec))
                act.wait_ge(vec_for_act, from_vec.up())
                act.activation(a["cos"], a["cos"], ACT.Sin).then_inc(*own.next())
                act.activation(a["sin"], a["sin"], ACT.Sin).then_inc(*own.next())
                act.wait_ge(vec_for_act, from_vec.up())
                dec = a["decay"].rearrange("p a b -> p (a b)")
                act.activation(dec, dec, ACT.Exp).then_inc(*own.mark(act_for_vec))
                for n in range(4):
                    b0 = 4 * ((n + 3) % 2)
                    act.wait_ge(chunks_done, end[f"ret_in{n + 2}"])
                    dst = (a["v"], a["g"])[n // 2][:, :, (n % 2) * 1024:(n % 2 + 1) * 1024]
                    for tb in range(TB):
                        i = act.activation(dst[:, tb, :], ps(b0 + 2 * tb, 2), ACT.Copy if n < 2 else ACT.Silu)
                        i.then_inc(*(own.mark(act_served) if tb else own.next()))
                root(rstd[:, 0:4])
                root(rstd[:, 4:8])
                copy_turned(a["yT"][:, 4:8, :], 2)
                copy_turned(a["yT"][:, 12:16, :], 6)
                root(rstd[:, 0:TB])

            def in_place(v, func, **kw):
                act.wait_ge(vec_for_act, from_vec.up())
                act.activation(v, v, func, **kw).then_inc(*own.mark(act_for_vec))

            def tell_vec():
                done()
                act.activation(misc[:, 508:509], iota[:, 0:1], ACT.Copy).then_inc(*own.mark(act_for_vec))

            def rows8(p):
                return p.rearrange("p b h k -> p (b h k)")

            def turned_p(pT, b0):
                copy_turned(pT.rearrange("p h k t -> p (h k) t")[:, 4:8, :], b0)

            def act_mla(a):
                act.wait_ge(vec_for_act, from_vec.up())
                act.activation(a["cos"], a["cos"], ACT.Sin).then_inc(*own.next())
                act.activation(a["sin"], a["sin"], ACT.Sin).then_inc(*own.mark(act_for_vec))
                root(rstd[:, 0:4])
                for key, dst in (("mla_uq", "qnT"), ("mla_ukv", "knT")):
                    for n in range(2):
                        act.wait_ge(chunks_done, end[f"{key}{n}"])
                        act.activation(a[dst][:, 4 * n:4 * n + 4, :].rearrange("p a b -> p (a b)"), ps(4 * (1 - n), 2),
                                       ACT.Copy).then_inc(*own.mark(act_served))
                act.wait_ge(psum_for_act, psum_a.up())
                act.activation(a["qrT"].rearrange("p a b -> p (a b)"), ps(4, 4, ROPE), ACT.Copy).then_inc(*own.mark(act_served))
                for n in range(2):
                    in_place(rows8(a["p"]), ACT.Exp, scale=MLA_SCALE)
                    turned_p(a["pT"], 6)
                    copy_turned(a["oT"][:, 4 * n:4 * n + 4, :], 0)
                root(rstd[:, 0:TB])

            def act_mixers(a):
                def flat(v):
                    return v.rearrange("p a b -> p (a b)")

                for n in range(4):
                    b0 = 4 * ((n + 1) % 2)
                    act.wait_ge(chunks_done, end[f"slots{n}"])
                    src = ps(b0, 4, C).rearrange("p (s t) -> p s t", t=T)
                    dst = a["z"][:, 8 * n:8 * n + 8, 1:T + 1] if n < 2 else a["qk"][:, n - 2]
                    act.activation(dst, src, ACT.Copy).then_inc(*own.mark(act_served))
                    if n == 1:
                        tell_vec()
                for key, b0, c in (("diff_v", 4, slice(POOL_W, POOL_W + DIFF_W)), ("pool_in", 0, slice(0, POOL_W))):
                    act.wait_ge(chunks_done, end[key])
                    act.activation(a["pv"][:, :, c], ps(b0, 4).rearrange("p (b c) -> p b c", b=TB)[:, :, 0:c.stop - c.start],
                                   ACT.Copy).then_inc(*own.mark(act_served))
                act.wait_ge(vec_for_act, from_vec.up())
                act.activation(a["zm"][:, 12, :], a["zm"][:, 12, :], ACT.Tanh).then_inc(*own.next())
                act.activation(a["zm"][:, 14:16, :], a["zm"][:, 14:16, :], ACT.Sigmoid).then_inc(*own.mark(act_for_pe))
                act.wait_ge(psum_for_act, psum_a.up())
                for w, dst in enumerate(("lw", "a")):
                    for hd in range(NH):
                        act.activation(a[dst][:, hd, :], ps(2 * w + hd // 2, 1, C)[:, (hd % 2) * T:(hd % 2 + 1) * T],
                                       ACT.Sigmoid, bias=a["cols"][:, w, hd:hd + 1]).then_inc(*own.next())
                act.activation(flat(a["g"]), ps(4, 2, C), ACT.Copy).then_inc(*own.mark(act_served))
                tell_vec()
                act.wait_ge(vec_for_act, from_vec.up())
                act.activation(flat(a["Pd"]), flat(a["L"]), ACT.Exp).then_inc(*own.next())
                act.activation(flat(a["Pi"]), flat(a["L"]), ACT.Exp, scale=-1.0).then_inc(*own.next())
                act.activation(flat(a["Pp"]), flat(a["Pp"]), ACT.Exp).then_inc(*own.mark(act_for_vec))
                act.wait_ge(psum_for_act, psum_a.up())
                act.activation(flat(a["kk2"]), ps(6, 2, C), ACT.Sqrt).then_inc(*own.mark(act_served))
                tell_vec()
                act.wait_ge(psum_for_act, psum_a.up())
                act.activation(a["tm"][:, 0:2].rearrange("p w u c -> p (w u c)"), ps(0, 4, C), ACT.Copy).then_inc(*own.mark(act_served))
                for dst, b0 in (("AkV", 0), ("U0", 6), ("X", 4)):
                    act.wait_ge(psum_for_act, psum_a.up())
                    act.activation(flat(a[dst]), ps(b0, 2, C), ACT.Copy).then_inc(*own.mark(act_served))
                root(misc[0:C, 288:304])
                act.wait_ge(psum_for_act, psum_a.up())
                act.activation(flat(a["rT"]), ps(6, 2, C), ACT.Copy).then_inc(*own.mark(act_served))
                sq, qk = (a[w].rearrange("p w s t -> p (w s t)") for w in ("sq", "qk"))
                act.activation(sq, qk, ACT.Square).then_inc(*own.mark(act_for_pe))
                in_place(a["lam"][:, 0:2], ACT.Exp)
                root(a["rs"].rearrange("p w s t -> p (w s t)"))
                for c in range(2):
                    in_place(rows8(a["p"][:, c]), ACT.Exp)
                turned_p(a["pT"], 6)
                root(sum8_)
                copy_turned(a["oT"], 2)

            sum8_ = misc[:, 264:272]

            def act_cross(a):
                root(rstd[:, 0:TB])
                root(rstd[:, 0:TB])
                copy_turned(a["mT"][:, 4:8, :], 6)
                root(sum8_)
                act.wait_ge(chunks_done, end["xa_wv_2"])
                act.activation(a["v"].rearrange("p a b -> p (a b)"), ps(4, 4), ACT.Copy).then_inc(*own.mark(act_served))
                copy_turned(a["kT"][:, 4:8, :], 2)
                copy_turned(hT[:, 4:8, :], 2)
                root(sum8_)
                copy_turned(a["qT"][:, 4:8, :], 2)
                in_place(rows8(a["p"]), ACT.Exp, scale=XD ** -0.5)
                turned_p(a["pT"], 2)
                act.wait_ge(psum_for_act, psum_a.up())
                act.activation(a["oT"].rearrange("p a b -> p (a b)"), ps(4, 4), ACT.Copy).then_inc(*own.mark(act_served))

            def act_ffn(a):
                for n in range(6):
                    w = min(4, FF_TILES - 4 * n)
                    in_place(a["conv"][:, n % 2, 0:w, :].rearrange("p a b -> p (a b)"), ACT.Gelu)

            def act_peer(a, phase):
                act.wait_ge(chunks_done, end[phase + "_keys"])
                act.activation(a["keysT"][:, 8:16, :].rearrange("p a b -> p (a b)"), ps(6, 2), ACT.Copy).then_inc(*own.mark(act_served))
                for n in range(2):
                    act.wait_ge(chunks_done, end[f"{phase}_q{n}"])
                    act.activation(a["qT"][:, 8 * n:8 * n + 8, :].rearrange("p a b -> p (a b)"), ps(4 * n, 4), ACT.Copy).then_inc(*own.mark(act_served))
                for tb in range(TB):
                    act.wait_ge(psum_for_act, psum_a.up())
                    act.activation(a["s"][:, tb].rearrange("p a b -> p (a b)"), ps(4 * tb, 4), ACT.Copy).then_inc(*own.mark(act_served))
                    done()
                    act.activation(misc[:, 0:1], iota[:, 0:1], ACT.Copy).then_inc(*own.mark(act_for_vec))
                for tb in range(TB):
                    act.wait_ge(vec_for_act, from_vec.up())
                    g = a["ijg"][:, 2, tb]
                    act.activation(g, g, ACT.Exp).then_inc(*own.mark(act_for_vec))
                G, base = a["G"], gates_before[phase]

                def place(g, half):
                    act.wait_ge(onehots_used, g + (base + 1))
                    act.activation(G[:, bass.ds(g * 4, 4), :], ps(2 + half, 1).rearrange("p (q n) -> p q n", q=4),
                                   ACT.Copy).then_inc(gates_placed, 1)

                with act.Fori(0, T // 8) as it:
                    for half in range(2):
                        place(it * 2 + half, half)
                uT, gel, w_ = expert_views()
                e0, d0 = begin[phase + "_experts"], experts_before[phase]

                def tile_(chunk, i, buf, fresh=False):
                    act.wait_ge(chunks_done, chunk + 1)
                    act.activation(uT[:, buf, 4:8, :].rearrange("p a b -> p (a b)"), ps(5, 1), ACT.Copy).then_inc(expert_act, 1)
                    act.wait_ge(hidden_ready, i + 1)
                    if not fresh:
                        act.wait_ge(weights_ready, i - 1)
                    act.activation(gel[:, buf, :], ps(6 + buf, 1)[:, 0:T], ACT.Gelu).then_inc(gelu_done, 1)

                tile_(e0, d0, 0, True)
                tile_(e0 + 1, d0 + 1, 1, True)
                with act.Fori(0, 31) as it:
                    for r in range(4):
                        tile_(it * 8 + (e0 + 3 + 2 * r), it * 4 + (d0 + 2 + r), r % 2)
                for i in range(126, NK):
                    tile_(e0 + 2 * i - 1, d0 + i, i % 2)
                root(rstd[:, 0:TB])

            for n, phase in enumerate(phases):
                if n == 0:
                    act.wait_ge(params_loaded, loads[phase])
                if phase in ("mixers", "ffn"):
                    root(rstd[:, 0:TB])
                if phase != "cross":
                    copy_turned(hT[:, 4:8, :], 2)
                if phase == "retention":
                    act_retention(A[phase])
                if phase == "mla":
                    act_mla(A[phase])
                if phase == "mixers":
                    act_mixers(A[phase])
                if phase == "cross":
                    act_cross(A[phase])
                if phase == "ffn":
                    act_ffn(A[phase])
                if phase.startswith("peer"):
                    act_peer(A[phase], phase)


def kernel(**inputs):
    import numpy as _np
    import concourse.bacc as _bacc
    from concourse import mybir as _mybir
    from concourse.bass_utils import run_bass_kernel_spmd as _run

    nc = _bacc.Bacc("TRN2", target_bir_lowering=False, num_devices=1)
    arrays, x = {}, {}
    for name, value in {**inputs, **constants(), **columns(inputs)}.items():
        a = _np.ascontiguousarray(value)
        arrays[f"in_{name}"] = a
        x[name] = nc.dram_tensor(f"in_{name}", a.shape, _mybir.dt.from_np(a.dtype), kind="ExternalInput").ap()
    out = nc.dram_tensor("out", (1, T, D), F32, kind="ExternalOutput").ap()
    build(nc, x, out)
    return _run(nc, [arrays], core_ids=[0]).results[0]["out"]
```

```python
from contextlib import ExitStack

import numpy as np

import concourse.bass as bass
from concourse import mybir

F32 = mybir.dt.float32
F32R = mybir.dt.float32r
I32 = mybir.dt.int32
U32 = mybir.dt.uint32
ALU = mybir.AluOpType
ACT = mybir.ActivationFunctionType
AX = mybir.AxisListType.X

P = 128
T = 256
TB = T // P
D = 1024
KD = D // P
BANK = 512
RING = 4
SPLIT = 2
SLOT = 1024
ALPHA = 4.0 ** 0.25
LN_EPS = 1e-5
RMS_EPS = 1e-6

RET_HEADS, RET_DK, RET_DV = 4, 256, 512
RET_HV = RET_HEADS * RET_DV

MLA_HEADS, NOPE, ROPE, VDIM = 8, 128, 64, 128
Q_RANK, KV_RANK = 384, 256
MLA_IN = Q_RANK + KV_RANK + ROPE
MLA_SCALE = float((NOPE + ROPE) ** -0.5)

PH, NK, TOPK = 8, 128, 16
HC = 2 * PH

POOL_W, RWKV_W, DIFF_W = 256, 256, 512
POOL_WINDOWS = (2, 4, 8, 16)
RWKV_COLS = 1024
C = 64
NC_ = T // C
NH = 4
UN = NC_ * NH
LEVELS = 6
RWKV_EPS = 64e-5
LAMBDA_INIT = 0.2
XH, XD = 4, 256
D_FF = 2816
FF_TILES = D_FF // P

TWO_PI_HI = 6.28125
TWO_PI_LO = float(2 * np.pi - 6.28125)
ROUND = 12582912.0
PI_IN = 3.1415925
LOWEST = -3.0e38

WHOLE = ("mix_out", "peer0_keys", "peer1_keys")

PHASES = ("retention", "peer0", "mla", "peer1", "mixers", "cross", "ffn")


def rows(name, layer, k_tiles, c0, cols, k_rows=P, row0=0):
    return [(name, layer, row0 + k * k_rows, k_rows, ((c0, cols),)) for k in range(k_tiles)]


def weight_plan(phases):
    plan = []
    for phase in phases:
        if phase == "retention":
            for n in range(6):
                plan.append((f"ret_in{n}", rows("ret_w_in", 0, KD, n * 1024, 1024)))
            plan.append(("ret_out", rows("ret_w_out", 0, RET_HV // P, 0, D)))
        if phase.startswith("peer"):
            l = int(phase[-1])
            for n in range(2):
                plan.append((f"{phase}_q{n}", rows("peer_w_q", l, KD, n * 1024, 1024)))
            plan.append((phase + "_keys", [("keys_turned", l, n, P, ((0, 1024),)) for n in range(2)]))
            plan.append((phase + "_u", [("u_turned", l, n, P, ((0, 1024),)) for n in range(NK)]))
            plan.append((phase + "_v", [("peer_v", l, n, P, ((0, 1024),)) for n in range(NK)]))
        if phase == "mla":
            plan.append(("mla_in", rows("mla_w_in", 0, KD, 0, MLA_IN)))
            for n in range(2):
                plan.append((f"mla_uq{n}", rows("mla_w_uq", 0, Q_RANK // P, n * 768, 768)))
            for n in range(2):
                plan.append((f"mla_ukv{n}", rows("mla_w_ukv", 0, KV_RANK // P, n * 1024, 1024)))
            plan.append(("mla_out", rows("mla_w_out", 0, MLA_HEADS, 0, D)))
        if phase == "mixers":
            for n in range(4):
                plan.append((f"slots{n}", rows("w_in_2", 0, KD, POOL_W + n * 512, 512)))
            plan.append(("diff_v", rows("w_in_2", 0, KD, POOL_W + 2048, DIFF_W)))
            plan.append(("pool_in", rows("w_in_2", 0, KD, 0, POOL_W)))
            plan.append(("mix_out", rows("w_out_2", 0, 8, 0, D, k_rows=64)
                         + rows("w_out_2", 0, 4, 0, D, row0=512)))
        if phase == "cross":
            for n, w in enumerate(("xa_wk_2", "xa_wv_2", "xa_wq_2", "xa_wo_2")):
                plan.append((w, rows(w, 0, KD, 0, D)))
        if phase == "ffn":
            for n in range(6):
                w = min(4, FF_TILES - 4 * n) * P
                plan.append((f"up{n}", [("ffn_w_up_2", 0, k * P, P, ((n * 512, w), (D_FF + n * 512, w)))
                                        for k in range(KD)]))
            plan.append(("down", rows("ffn_w_down_2", 0, FF_TILES, 0, D)))
    return plan


def constants():
    out = {}
    out["c_ident"] = np.eye(P, dtype=np.float32)
    out["c_iota"] = np.tile(np.arange(P, dtype=np.float32), (P, 1))
    f = (np.float32(10000.0) ** (-np.arange(0, RET_DK, 2, dtype=np.float32) / np.float32(RET_DK))).astype(np.float32)
    out["c_ret_freq"] = f[:, None].copy()
    f = (np.float32(10000.0) ** (-np.arange(0, ROPE, 2, dtype=np.float32) / np.float32(ROPE))).astype(np.float32)
    out["c_mla_freq"] = np.tile(f, (P, 1))
    m = np.arange(T).reshape(TB, P).T[:, :, None]
    n = np.arange(T)[None, None, :]
    d = (n - m).astype(np.float32)
    out["c_ahead"] = np.stack([np.maximum(d, 0), np.maximum(-d, 0)], 1).reshape(P, 2 * TB * T)
    slopes = 2.0 ** (-8.0 * (np.arange(4) + 1) / 4)
    seen = (n // C) <= (m // C)
    bias = np.where(seen[:, :, None, :], -slopes[None, None, :, None] * np.abs(d)[:, :, None, :], LOWEST)
    out["c_alibi"] = bias.astype(np.float32).reshape(P, TB * 4 * T)
    pool = np.zeros((P, TB, 4, T), np.float32)
    for g, w in enumerate(POOL_WINDOWS):
        count = np.minimum(n + 1, w)
        pool[:, :, g, :] = ((m <= n) & (m > n - w)) / count - (m == n)
    out["c_pool"] = pool.reshape(P, TB * 4 * T)
    s, t = np.arange(C)[:, None], np.arange(C)[None, :]
    before = np.concatenate([s < t, s <= t], 1).astype(np.float32)
    levels = [((s < t) & (s >> (b + 1) == t >> (b + 1)) & (s >> b != t >> b)) for b in range(LEVELS)]
    reset = np.tile((np.arange(T) % C != 0).astype(np.float32), (C, NH))
    out["c_rwkv"] = np.concatenate([before] + [x.astype(np.float32) for x in levels] + [reset], 1)
    return {k: np.ascontiguousarray(v, dtype=np.float32) for k, v in out.items()}


def columns(x):
    def cols(v, p):
        return np.asarray(v).reshape(-1, p).T

    rwkv = [cols(x[n], C) for n in ("rwkv_mu_2", "rwkv_w0_2", "rwkv_a0_2", "rwkv_k_k_2", "rwkv_k_a_2", "rwkv_r_k_2",
                                    "pool_scale_2", "diff_q_norm_2", "diff_k_norm_2")]
    return {"positions_cols": np.ascontiguousarray(cols(x["positions"], P)),
            "channel_cols": np.ascontiguousarray(np.concatenate(rwkv, 1)),
            "conv_cols": np.ascontiguousarray(np.concatenate([cols(x["ffn_conv_w_2"], P), cols(x["ffn_conv_b_2"], P)], 1))}


def turned(x):
    u = np.asarray(x["peer_u"]).reshape(-1, NK, NK, KD, P)
    keys = np.asarray(x["peer_sub_keys"]).reshape(-1, 2, PH, NK, P)
    return {"u_turned": np.ascontiguousarray(u.transpose(0, 1, 4, 3, 2)),
            "keys_turned": np.ascontiguousarray(keys.transpose(0, 1, 4, 2, 3))}


class Count:

    def __init__(self, n=0):
        self.n = n

    def up(self, by=1):
        self.n = self.n + by
        return self.n


class Last:

    def __init__(self, step):
        self.step, self.counts, self.last = step, {}, None

    def next(self):
        return self.mark(self.step)

    def mark(self, sem, by=1):
        n = self.counts.setdefault(id(sem), Count())
        self.last = (sem, n.up(by))
        return sem, by

    def set(self, sem, n):
        self.counts[id(sem)] = Count(n)
        self.last = (sem, n)


class Banks:

    def __init__(self, served):
        self.served = served
        self.lent = {who: Count() for who in served}
        self.of = {}

    def lend(self, banks, who):
        n = self.lent[who].up()
        for b in banks:
            self.of[b] = (self.served[who], n)
        return self.served[who], n


class Memory:

    def __init__(self, base, start, size):
        self.base, self.at, self.end = base, start, start + size

    def take(self, *dims, parts=P):
        n = int(np.prod(dims))
        assert self.at + n <= self.end, ("SBUF", dims, self.at, self.end)
        v = self.base[0:parts, self.at:self.at + n]
        self.at += n
        if len(dims) == 1:
            return v
        names = "abcde"[:len(dims)]
        return v.rearrange(f"p ({' '.join(names)}) -> p {' '.join(names)}", **dict(zip(names, dims)))


def bcast(ap, axis, n):
    v = ap.unsqueeze(axis)
    return v.broadcast_to([*v.shape[:axis], n, *v.shape[axis + 1:]])


def build(nc, x, out, phases=PHASES):
    ctx = ExitStack()
    with ctx:
        def sem(name):
            return ctx.enter_context(nc.semaphore(name))

        ARENA = 32768
        LASTING = TB * D + 2 * P + RING * SLOT + 3072 + 3 * T + 640
        sb = ctx.enter_context(nc.sbuf_tensor("sb", [P, LASTING + ARENA], F32))
        lasting = Memory(sb, 0, LASTING)
        h = lasting.take(TB, D)
        ident = lasting.take(P)
        iota = lasting.take(P)
        ring = lasting.take(RING, SLOT)
        pair_at = lasting.at
        pair = lasting.take(3072)
        routes_at = lasting.at
        routes = lasting.take(3, T)
        stats = lasting.take(4, 2, 6)
        mv = lasting.take(2, 2)
        var8 = lasting.take(8, 2)
        rstd = lasting.take(16)
        misc = lasting.take(512)

        rounded = ctx.enter_context(nc.sbuf_tensor("rounded", [P, 2 * KD * T + 2 * SPLIT * SLOT + 4 * T], F32R))
        split_parts = Memory(rounded, 0, 2 * KD * T + 2 * SPLIT * SLOT + 4 * T)
        hT = split_parts.take(2, KD, T)
        ring_hi = split_parts.take(SPLIT, SLOT)
        ring_lo = split_parts.take(SPLIT, SLOT)
        tile_w = split_parts.take(2, 2, T)

        def arena():
            return Memory(sb, LASTING, ARENA)

        psum = ctx.enter_context(nc.psum_tensor("psum", [P, 8, BANK], F32))

        def ps(b0, n, parts=P):
            return psum[0:parts, b0:b0 + n, :].rearrange("p a b -> p (a b)")

        ring_loaded = [sem(f"ring_loaded{n}") for n in range(RING)]
        chunks_done = sem("chunks_done")
        psum_for_vec, psum_for_act = sem("psum_for_vec"), sem("psum_for_act")
        vec_served, act_served = sem("vec_served"), sem("act_served")
        vec_for_act, act_for_vec = sem("vec_for_act"), sem("act_for_vec")
        vec_for_pe, act_for_pe = sem("vec_for_pe"), sem("act_for_pe")
        vec_step, act_step = sem("vec_step"), sem("act_step")
        onehots_made, onehots_used = sem("onehots_made"), sem("onehots_used")
        gates_placed, routes_ready = sem("gates_placed"), sem("routes_ready")
        j_less, j_apart, j_onehots = sem("j_less"), sem("j_apart"), sem("j_onehots")
        gelu_done, weights_hi, weights_ready = sem("gelu_done"), sem("weights_hi"), sem("weights_ready")
        chunk_hi, chunk_split = sem("chunk_hi"), sem("chunk_split")
        alibi_loaded = sem("alibi_loaded")
        input_loaded, params_loaded, phase_done = sem("input_loaded"), sem("params_loaded"), sem("phase_done")
        stored = sem("stored")

        plan = weight_plan(phases)
        begin, end, n_chunks = {}, {}, 0
        for key, chunks in plan:
            begin[key] = n_chunks
            n_chunks += len(chunks)
            end[key] = n_chunks
        chunk_size = {begin[key] + i: (k, sum(w for _, w in runs))
                      for key, chunks in plan for i, (_, _, _, k, runs) in enumerate(chunks)}
        split_count = {}
        for key, chunks in plan:
            if key not in WHOLE:
                for n in range(begin[key], end[key]):
                    split_count[n] = len(split_count) + 1

        def whole(name):
            a = x[name]
            dims = "abcdef"[:len(a.shape)]
            return a.rearrange(f"{' '.join(dims)} -> ({' '.join(dims)})")

        params, A = {}, {}

        def param(phase, dst, src):
            params.setdefault(phase, []).append((dst, src))

        def everywhere(ap, parts=P):
            return ap.partition_broadcast(parts)

        def norm_params(phase, place, g, b, l):
            A[phase]["norm"] = place
            param(phase, place[:, 0, :], everywhere(x[g][l]))
            if b is not None:
                param(phase, place[:, 1, :], everywhere(x[b][l]))

        for phase in phases:
            m = arena()
            a = A[phase] = {}
            if phase == "retention":
                a["qT"], a["kT"] = m.take(8, T), m.take(8, T)
                a["v"], a["g"] = m.take(TB, RET_HV), m.take(TB, RET_HV)
                a["y"] = m.take(TB, RET_HV)
                a["decay"] = m.take(4, TB * T)
                a["s"] = m.take(4, TB, T)
                a["tmp"] = m.take(2, 4, T)
                a["gn"] = m.take(2, RET_HV)
                a["ahead"] = m.take(2, TB * T)
                a["cos"], a["sin"] = m.take(T), m.take(T)
                a["posi"], a["ang"], a["turn"] = m.take(T), m.take(T), m.take(T)
                a["lg"] = m.take(8)
                a["freq"] = m.take(1)
                a["yT"] = a["v"].rearrange("p a b -> p (a b)").rearrange("p (k t) -> p k t", t=T)
                param(phase, a["posi"].bitcast(I32), everywhere(x["positions"][0]))
                param(phase, a["freq"], x["c_ret_freq"])
                param(phase, a["ahead"].rearrange("p a b -> p (a b)"), x["c_ahead"])
                param(phase, a["lg"], everywhere(whole("ret_log1m_decay")))
                param(phase, a["gn"][:, 0, :], everywhere(x["ret_gn_g"][0]))
                param(phase, a["gn"][:, 1, :], everywhere(x["ret_gn_b"][0]))
                norm_params(phase, m.take(2, D), "ln_mix_g", "ln_mix_b", 0)
            if phase.startswith("peer"):
                l = int(phase[-1])
                a["G"] = m.take(NK, T)
                up = Memory(sb, LASTING + NK // 2 * T, NK // 2 * T)
                a["s"] = up.take(TB, HC, NK)
                late = Memory(sb, up.at, 8192)
                a["qT"] = up.take(HC, T)
                up.take(8192 - HC * T)
                a["s2"], a["cand"], a["cand2"] = late.take(HC, NK), late.take(PH, TOPK * TOPK), late.take(PH, TOPK * TOPK)
                a["sel"] = late.take(PH, TOPK, TOPK)
                a["val"], a["idx"], a["idxf"] = (up.take(HC, TOPK) for _ in range(3))
                a["top"], a["pos"] = up.take(PH, TOPK), up.take(PH, TOPK)
                a["ab"], a["abf"] = up.take(2, PH, TOPK), up.take(2, PH, TOPK)
                late = Memory(sb, pair_at + 2048, 1024)
                a["ijg"], a["den"] = late.take(3, TB, PH, TOPK), late.take(TB, PH)
                norm_params(phase, arena().take(2, D), "ln_ffn_g", "ln_ffn_b", l)
            if phase == "mla":
                a["c"], a["sq"] = m.take(TB, MLA_IN), m.take(TB, Q_RANK + KV_RANK)
                a["krT"] = m.take(T, parts=ROPE)
                a["qnT"], a["knT"] = m.take(MLA_HEADS, T), m.take(MLA_HEADS, T)
                a["qr"], a["qrT"] = m.take(TB, MLA_HEADS, ROPE), m.take(MLA_HEADS, T, parts=ROPE)
                a["v"] = m.take(TB, MLA_HEADS * VDIM)
                a["p"], a["pT"] = m.take(TB, 4, T), m.take(4, TB, T)
                a["tmp"] = m.take(4, TB * 4 * ROPE // 2)
                a["cos"], a["sin"], a["ang"], a["turn"] = (m.take(TB, ROPE // 2) for _ in range(4))
                a["freq"], a["posi"], a["pos"] = m.take(ROPE // 2), m.take(TB), m.take(TB)
                a["gain"] = m.take(Q_RANK + KV_RANK)
                param(phase, a["freq"], x["c_mla_freq"])
                param(phase, a["posi"].bitcast(I32), x["positions_cols"])
                param(phase, a["gain"][:, 0:Q_RANK], everywhere(x["mla_q_norm"][0]))
                param(phase, a["gain"][:, Q_RANK:], everywhere(x["mla_kv_norm"][0]))
                norm_params(phase, m.take(2, D), "ln_mix_g", "ln_mix_b", 1)
            if phase == "mixers":
                U = (UN, C)
                a["pv"] = m.take(TB, POOL_W + DIFF_W)
                a["qk"] = m.take(2, 8, T, parts=C)
                a["poolT"], a["oT"] = m.take(4, T, parts=C), m.take(4, T)
                a["g"] = a["oT"][0:C]
                late = Memory(sb, m.at, 2048)
                a["alibi"] = m.take(TB, 4, T)
                a["bt"], a["kt"] = late.take(*U, parts=C), late.take(*U, parts=C)
                late = Memory(sb, m.at, 2048)
                a["pool"] = m.take(TB, 4, T)
                a["rk"], a["X"] = late.take(*U, parts=C), late.take(*U, parts=C)
                a["pool_w"] = m.take(4, C, parts=C)
                a["masks"] = m.take(2 * C + LEVELS * C + NH * T, parts=C)
                a["w2"], a["a2"] = m.take(RWKV_W, parts=C), m.take(RWKV_W, parts=C)
                a["g2"] = m.take(2, RWKV_W, parts=C)
                a["ln"] = m.take(2, RWKV_W, parts=C)
                a["channels"] = m.take(16 + 6 * NH + 4, parts=C)
                a["mu"] = a["channels"][:, 0:16]
                a["cols"] = a["channels"][:, 16:16 + 6 * NH].rearrange("p (i h) -> p i h", h=NH)
                a["qk_gain"] = a["channels"][:, 16 + 6 * NH:].rearrange("p (w c) -> p w c", w=2)
                a["pend"] = m.take(UN, parts=C)
                a["lq"], a["lam"] = m.take(2, 2, C), m.take(8)
                a["ones"] = m.take(C, parts=C)
                late = Memory(sb, m.at, 2048)
                a["hn"] = m.take(TB, D)
                a["kk2"], a["kx"] = late.take(NH, T, parts=C), late.take(NH, T, parts=C)
                a["d"] = a["kk2"]
                late = Memory(sb, late.at - 2048, 2048)
                a["Tm"], a["TmT"] = late.take(*U, parts=C), late.take(*U, parts=C)
                late = Memory(sb, late.at - 2048, 2048)
                a["o"], a["osq"] = late.take(TB, 4, P), late.take(TB, 4, P)
                late = Memory(sb, m.at, 4112)
                a["z"] = m.take(16, T + 1, parts=C)
                a["lw"], a["L"], a["Pd"], a["Pp"] = (late.take(NH, T, parts=C) for _ in range(4))
                late = Memory(sb, late.at - 4096, 4096)
                a["tm"] = late.take(4, *U, parts=C)
                a["rT"] = a["tm"][:, 0].rearrange("p u c -> p (u c)").rearrange("p (h t) -> p h t", h=NH)
                late, zm_at = Memory(sb, m.at, 4096), m.at
                a["zm"] = m.take(16, T, parts=C)
                a["Q"], a["Mt"], a["y"], a["ysq"] = (late.take(*U, parts=C) for _ in range(4))
                late = Memory(sb, late.at - 4096, 4096)
                a["rs"] = late.take(2, 8, T, parts=C)
                late = Memory(sb, m.at, 2048)
                a["ar"] = m.take(UN, 2, C, parts=C)
                a["pT"] = late.take(4, TB, T)
                late = Memory(sb, m.at, 4096)
                a["mab"], a["mak"] = m.take(UN, 2 * C, parts=C), m.take(UN, 2 * C, parts=C)
                a["p"] = late.take(2, TB, 4, T)
                late = Memory(sb, late.at - 4096, 4096)
                a["sq"] = late.take(2, 8, T, parts=C)
                late = Memory(sb, pair_at, 3072)
                a["Pi"], a["a"], a["kk"] = (late.take(NH, T, parts=C) for _ in range(3))
                late = Memory(sb, late.at - 3072, 3072)
                a["aoff"], a["AkV"], a["G1"] = (late.take(*U, parts=C) for _ in range(3))
                a["U0"] = a["aoff"]
                a["S"] = Memory(sb, routes_at, 768).take(3, NH, C, parts=C)
                norm_params(phase, Memory(sb, zm_at, D).take(1, D), "mix_norm_g_2", None, 0)
                param(phase, a["pool"].rearrange("p a b c -> p (a b c)"), x["c_pool"])
                param(phase, a["masks"], x["c_rwkv"])
                param(phase, a["pool_w"], x["pool_w_2"][0].rearrange("g c d -> c g d"))
                param(phase, a["w2"], x["rwkv_w2_2"][0])
                param(phase, a["a2"], x["rwkv_a2_2"][0])
                param(phase, a["g2"], x["rwkv_g2_2"][0].rearrange("(s p) c -> p s c", p=C))
                param(phase, a["ln"][:, 0, :], everywhere(x["rwkv_ln_w_2"][0], C))
                param(phase, a["ln"][:, 1, :], everywhere(x["rwkv_ln_b_2"][0], C))
                param(phase, a["channels"], x["channel_cols"])
                for i, name in enumerate(("diff_lq1_2", "diff_lk1_2", "diff_lq2_2", "diff_lk2_2")):
                    param(phase, a["lq"][:, i % 2, i // 2, :], everywhere(x[name][0]))
                param(phase, misc[:, 0:P], everywhere(x["diff_subln_2"][0]))
            if phase == "cross":
                a["mem"], a["mn"], a["hn"] = m.take(TB, D), m.take(TB, D), m.take(TB, D)
                a["k"], a["q"], a["v"], a["sq"] = (m.take(TB, D) for _ in range(4))
                a["kT"], a["qT"] = m.take(KD, T), m.take(KD, T)
                a["p"], a["pT"] = m.take(TB, 4, T), m.take(4, TB, T)
                a["gain"] = m.take(2, XD)
                param(phase, a["mem"], x["mem_2"][0].rearrange("(b p) d -> p b d", p=P))
                a["norm"] = a["v"]
                param(phase, a["norm"][:, 0, :], everywhere(x["mem_norm_g_2"][0]))
                param(phase, a["norm"][:, 1, :], everywhere(x["xa_norm_g_2"][0]))
                param(phase, a["gain"][:, 0, :], everywhere(x["xa_k_norm_2"][0]))
                param(phase, a["gain"][:, 1, :], everywhere(x["xa_q_norm_2"][0]))
            if phase == "ffn":
                a["hn"], a["hid"] = m.take(TB, D), m.take(FF_TILES, T)
                a["conv"] = m.take(2, 4, T)
                a["taps_bias"] = m.take(4 * FF_TILES)
                a["taps"] = a["taps_bias"][:, 0:3 * FF_TILES].rearrange("p (w t) -> p w t", w=3)
                a["bias"] = a["taps_bias"][:, 3 * FF_TILES:]
                norm_params(phase, m.take(1, D), "ffn_norm_g_2", None, 0)
                param(phase, a["taps_bias"], x["conv_cols"])

        gates_before, experts_before = {}, {}
        for n, phase in enumerate(p for p in phases if p.startswith("peer")):
            gates_before[phase], experts_before[phase] = n * T // 4, n * NK

        def onehot_views():
            v = pair[:, 0:2048].rearrange("p (w b q n) -> p w b q n", w=2, b=2, q=4)
            return v[:, 0], v[:, 1]

        less_j = pair[:, 2048:3072].rearrange("p (b q n) -> p b q n", b=2, q=4)

        block = ctx.enter_context(nc.Block())

        def gp_less_j(gp, phase):
            base = gates_before[phase]
            gp.wait_ge(routes_ready, 1 + base * 4 // T)

            def group(g, half, fresh):
                if not fresh:
                    gp.wait_ge(j_onehots, g + (base - 1))
                gp.tensor_tensor(less_j[:, half], bcast(iota, 1, 4), bcast(routes[:, 1, bass.ds(g * 4, 4)], 2, P),
                                 ALU.subtract).then_inc(j_less, 1)

            group(0, 0, True)
            group(1, 1, True)
            with gp.Fori(1, T // 8) as it:
                for half in range(2):
                    group(it * 2 + half, half, False)

        @block.sync
        def _(sync):
            def chunk_source(name, l, r0, k, runs):
                if name in ("keys_turned", "u_turned"):
                    return x[name][l][r0].rearrange("p a b -> p (a b)")
                c0, w = runs[0]
                if len(runs) == 2:
                    return x[name][l][r0:r0 + k, :].rearrange("k (two f) -> k two f", two=2)[:, :, c0:c0 + w]
                return x[name][l][r0:r0 + k, c0:c0 + w]

            def load(n, k, src):
                if n - RING in split_count:
                    sync.wait_ge(chunk_split, split_count[n - RING])
                elif n >= RING:
                    sync.wait_ge(chunks_done, n - RING + 1)
                cols = src.shape[-1] * (src.shape[1] if len(src.shape) == 3 else 1)
                dst = ring[0:k, n % RING, 0:cols]
                if len(src.shape) == 3:
                    dst = dst.rearrange("p (a b) -> p a b", a=src.shape[1])
                sync.dma_start(dst, src).then_inc(ring_loaded[n % RING], 16)

            n = 0
            for key, chunks in plan:
                if not key.startswith("peer") or not key.endswith(("_u", "_v")):
                    for name, l, r0, k, runs in chunks:
                        load(n, k, chunk_source(name, l, r0, k, runs))
                        n += 1
                    continue
                l = int(key[4])
                if key.endswith("_u"):
                    src = x["u_turned"][l].rearrange("i p k j -> i p (k j)")
                else:
                    src = x["peer_v"][l].rearrange("(i j) d -> i j d", j=NK)
                for r in range(RING):
                    load(n + r, P, src[r])
                with sync.Fori(1, NK // RING) as it:
                    for r in range(RING):
                        sync.wait_ge(chunk_split, it * RING + (split_count[n + r] - RING))
                        sync.dma_start(ring[:, (n + r) % RING, :], src[it * RING + r]).then_inc(ring_loaded[(n + r) % RING], 16)
                n += NK
            sync.wait_ge(phase_done, len(phases))
            for tb in range(TB):
                sync.dma_start(out[0, tb * P:(tb + 1) * P, :], h[:, tb, :]).then_inc(stored, 16)
            sync.wait_ge(stored, 16 * TB)

        @block.gpsimd
        def _(gp):
            for phase in phases:
                if phase.startswith("peer"):
                    gp_less_j(gp, phase)

        loads, at = {}, 0
        for phase in phases:
            at += len(params.get(phase, []))
            loads[phase] = 16 * at

        @block.tensor
        def _(pe):
            banks = Banks({"v": vec_served, "a": act_served})
            to_pe, act_to_pe = Count(), Count()

            def hold(bs):
                for who, served in banks.served.items():
                    owed = [banks.of[b][1] for b in bs if b in banks.of and banks.of[b][0] is served]
                    if owed:
                        pe.wait_ge(served, max(owed))

            def arrived(n):
                if n in split_count:
                    pe.wait_ge(chunk_split, split_count[n])
                else:
                    pe.wait_ge(ring_loaded[n % RING], 16 * (n // RING + 1))

            def parts(n, rows_=P):
                return ring_hi[0:rows_, n % SPLIT, :], ring_lo[0:rows_, n % SPLIT, :]

            def passes(o, a, b, first, last):
                for i, (p, q) in enumerate(((0, 0), (0, 1), (1, 0))):
                    mm = pe.matmul(o, a[p], b[q], start=(first and i == 0),
                                   stop=(last and i == 2), skip_group_check=True)
                return mm

            def panel(key, lhs, form, b0, tiles, k_rows=None, fed=None):
                kk = end[key] - begin[key]
                for k in range(kk):
                    if fed is not None and k >= fed and k % 4 == 0:
                        pe.wait_ge(vec_for_pe, to_pe.up())
                    n = begin[key] + k
                    rows_ = k_rows[k] if k_rows else P
                    arrived(n)
                    w = parts(n, rows_) if n in split_count else (ring[0:rows_, n % RING, :],)
                    act_ = lhs(k) if n in split_count else (lhs(k),)
                    todo = []
                    if form == "tokens":
                        for tb in range(TB):
                            for c in range(0, tiles, BANK):
                                todo.append((ps(b0 + 2 * tb + c // BANK, 1)[:, 0:min(BANK, tiles - c)],
                                             [v[:, tb * P:(tb + 1) * P] for v in act_],
                                             [v[:, c:min(c + BANK, tiles)] for v in w], True))
                    else:
                        for i in range(tiles):
                            todo.append((ps(b0 + i // 2, 1)[:, (i % 2) * T:(i % 2) * T + T],
                                         [v[:, i * P:(i + 1) * P] for v in w], act_, i % 2 == 0))
                    for o, a, b, first in todo:
                        if len(a) == 1:
                            mm = pe.matmul(o, a[0], b[0], start=(k == 0 and first), stop=(k == kk - 1), skip_group_check=True)
                        else:
                            mm = passes(o, a, b, k == 0 and first, k == kk - 1)
                    mm.then_inc(chunks_done, 1)

            def transpose_in(src, n_k, k_rows=P, b0=0, who="vv"):
                per = BANK // T
                nb = n_k // per
                for k in range(n_k):
                    for tb in range(TB):
                        mm = pe.transpose(ps(b0 + k // per, 1, k_rows)[:, (k % per) * T + tb * P:(k % per) * T + (tb + 1) * P],
                                          src(k, tb), ident)
                    if k == n_k // 2 - 1:
                        mm.then_inc(psum_for_vec, 1)
                mm.then_inc(psum_for_act if who == "va" else psum_for_vec, 1)
                return [banks.lend(range(b0, b0 + nb // 2), "v"), banks.lend(range(b0 + nb // 2, b0 + nb), who[1])]

            def wait_all(tokens):
                for s, v in tokens:
                    pe.wait_ge(s, v)

            def stream_T(n, src=None):
                if src is not None:
                    pe.wait_ge(vec_for_pe, to_pe.up())
                elif n:
                    pe.wait_ge(phase_done, n)
                else:
                    pe.wait_ge(input_loaded, 64)
                src = h if src is None else src
                hold(range(4))
                wait_all(transpose_in(lambda k, tb: src[:, tb, k * P:(k + 1) * P], KD))

            def split_of(v):
                return lambda k: (v[:, 0, k, :], v[:, 1, k, :])

            hk = split_of(hT)

            def four_by_four(k):
                return hk(k % KD)

            def pe_retention(a):
                for n, who in enumerate("vvaaaa"):
                    b0 = 4 * ((n + 1) % 2)
                    hold(range(b0, b0 + 4))
                    if n < 2:
                        panel(f"ret_in{n}", hk, "features", b0, 8)
                    else:
                        panel(f"ret_in{n}", hk, "tokens", b0, 1024)
                    tok = banks.lend(range(b0, b0 + 4), who)
                    if n == 1:
                        rotated = tok
                    if n == 3:
                        v_ready = tok
                pe.wait_ge(*rotated)
                hold(range(4, 8))
                for hd in range(RET_HEADS):
                    for mb in range(TB):
                        for d in range(2):
                            mm = pe.matmul(ps(4 + hd, 1)[:, mb * T:(mb + 1) * T],
                                           a["kT"][:, 2 * hd + d, mb * P:(mb + 1) * P], a["qT"][:, 2 * hd + d, :],
                                           start=(mb == 0 and d == 0), stop=(d == 1), skip_group_check=True)
                mm.then_inc(psum_for_vec, 1)
                decayed = banks.lend(range(4, 8), "v")
                pe.wait_ge(*decayed)
                pe.wait_ge(*v_ready)
                for tb in range(TB):
                    b0 = 4 * tb
                    hold(range(b0, b0 + 4))
                    for hd in range(RET_HEADS):
                        for mb in range(TB):
                            mm = pe.matmul(ps(b0 + hd, 1), a["s"][:, hd, mb, tb * P:(tb + 1) * P],
                                           a["v"][:, mb, hd * BANK:(hd + 1) * BANK], start=(mb == 0), stop=(mb == 1))
                    mm.then_inc(psum_for_vec, 1)
                    gated = banks.lend(range(b0, b0 + 4), "v")
                pe.wait_ge(*gated)
                toks = []
                for half in range(2):
                    toks += transpose_in(lambda k, tb: a["y"][:, tb, (8 * half + k) * P:(8 * half + k + 1) * P], 8, b0=4 * half)
                wait_all(toks)
                hold(range(4))
                panel("ret_out", four_by_four, "tokens", 0, D, fed=8)
                banks.lend(range(4), "v")

            def pe_peer(phase, a):
                for n in range(2):
                    b0 = 4 * (1 - n)
                    hold(range(b0, b0 + 4))
                    panel(f"{phase}_q{n}", hk, "features", b0, 8)
                    q = banks.lend(range(b0, b0 + 4), "v")
                pe.wait_ge(*q)
                hold(range(8))
                for n in range(2):
                    c = begin[phase + "_keys"] + n
                    arrived(c)
                    for tb in range(TB):
                        for i in range(8):
                            hc = 8 * n + i
                            mm = pe.matmul(ps(4 * tb + hc // 4, 1)[:, (hc % 4) * P:(hc % 4 + 1) * P],
                                           a["qT"][:, hc, tb * P:(tb + 1) * P], ring[:, c % RING, i * P:(i + 1) * P],
                                           start=(hc % 4 == 0), stop=True, skip_group_check=True)
                    mm.then_inc(chunks_done, 1)
                banks.lend(range(8), "a")

                hold([6, 7])
                n, d0 = begin[phase + "_u"], experts_before[phase]

                def hidden(n, split, i, buf, fresh=False):
                    pe.wait_ge(chunk_split, split)
                    if not fresh:
                        pe.wait_ge(gelu_done, i - 1)
                    u = parts(n)
                    for k in range(KD):
                        for w, (p, q) in enumerate(((0, 0), (0, 1), (1, 0))):
                            mm = pe.matmul(ps(6 + buf, 1)[:, 0:T], u[p][:, k * P:(k + 1) * P], hT[:, q, k, :], start=(k == 0 and w == 0),
                                           stop=(k == KD - 1 and w == 2))
                    mm.then_inc(chunks_done, 1)

                for r in range(RING):
                    hidden(n + r, split_count[n + r], d0 + r, r % 2, fresh=r < 2)
                with pe.Fori(1, NK // RING) as it:
                    for r in range(RING):
                        hidden(n + r, it * RING + split_count[n + r], it * RING + (d0 + r), r % 2)

                pe.wait_ge(vec_for_pe, to_pe.up())
                hold([0, 1])
                for w in range(3):
                    for tb in range(TB):
                        mm = pe.transpose(ps(0, 2)[:, w * T + tb * P:w * T + (tb + 1) * P],
                                          a["ijg"][:, w, tb, :, :].rearrange("p a b -> p (a b)"), ident)
                mm.then_inc(psum_for_vec, 1)
                banks.lend([0, 1], "v")
                A_, B_ = onehot_views()
                hold([2, 3])
                base = gates_before[phase]

                def gate_group(g, half, fresh):
                    if not fresh:
                        pe.wait_ge(gates_placed, g + (base - 1))
                    pe.wait_ge(onehots_made, g + (base + 1))
                    pe.wait_ge(j_onehots, g + (base + 1))
                    for q in range(4):
                        mm = pe.matmul(ps(2 + half, 1)[:, q * P:(q + 1) * P], B_[:, half, q, :], A_[:, half, q, :],
                                       start=(q == 0), stop=True, skip_group_check=True)
                    mm.then_inc(onehots_used, 1)

                gate_group(0, 0, True)
                gate_group(1, 1, True)
                with pe.Fori(1, T // 8) as it:
                    for half in range(2):
                        gate_group(it * 2 + half, half, False)

                pe.wait_ge(gates_placed, base + T // 4)
                hold(range(4))
                n = begin[phase + "_v"]

                def output(n, split, i, buf, first=False, last=False):
                    pe.wait_ge(chunk_split, split)
                    pe.wait_ge(weights_ready, i + 1)
                    v = parts(n)
                    for tb in range(TB):
                        for c in range(2):
                            for w, (p, q) in enumerate(((0, 0), (0, 1), (1, 0))):
                                mm = pe.matmul(ps(2 * tb + c, 1), tile_w[:, buf, p, tb * P:(tb + 1) * P],
                                               v[q][:, c * BANK:(c + 1) * BANK],
                                               start=(first and w == 0), stop=(last and w == 2), skip_group_check=True)
                    mm.then_inc(chunks_done, 1)

                for r in range(RING):
                    output(n + r, split_count[n + r], d0 + r, r % 2, first=(r == 0))
                with pe.Fori(1, NK // RING - 1) as it:
                    for r in range(RING):
                        output(n + r, it * RING + split_count[n + r], it * RING + (d0 + r), r % 2)
                for r in range(NK - RING, NK):
                    output(n + r, split_count[n + r], d0 + r, r % 2, last=(r == NK - 1))
                banks.lend(range(4), "v")

            def turn_p(p, b0):
                return transpose_in(lambda k, tb: p[:, tb, k // TB, (k % TB) * P:(k % TB + 1) * P], 8, b0=b0, who="va")

            def pe_mla(a):
                hold(range(4, 8))
                panel("mla_in", hk, "tokens", 4, MLA_IN)
                pe.wait_ge(*banks.lend(range(4, 8), "v"))
                hold(range(3))
                for k in range(5):
                    for tb in range(TB):
                        pe.transpose(ps(k // 2, 1)[:, (k % 2) * T + tb * P:(k % 2) * T + (tb + 1) * P],
                                     a["c"][:, tb, k * P:(k + 1) * P], ident)
                for tb in range(TB):
                    mm = pe.transpose(ps(2, 1, ROPE)[:, T + tb * P:T + (tb + 1) * P],
                                      a["c"][:, tb, Q_RANK + KV_RANK:MLA_IN], ident)
                mm.then_inc(psum_for_vec, 1)
                pe.wait_ge(*banks.lend(range(3), "v"))
                toks = []
                for n in range(2):
                    b0 = 4 * (1 - n)
                    hold(range(b0, b0 + 3))
                    for k in range(3):
                        c = begin[f"mla_uq{n}"] + k
                        arrived(c)
                        w = [v[:, 0:768].rearrange("p (h e) -> p h e", h=4) for v in parts(c)]
                        lat = hk(k)
                        for hd in range(4):
                            passes(ps(b0 + hd // 2, 1)[:, (hd % 2) * T:(hd % 2 + 1) * T], [v[:, hd, 0:NOPE] for v in w], lat,
                                   k == 0 and hd % 2 == 0, k == 2)
                        for tb in range(TB):
                            mm = passes(ps(b0 + 2, 1)[:, tb * T:(tb + 1) * T].rearrange("p (h e) -> p h e", h=4),
                                        [v[:, tb * P:(tb + 1) * P] for v in lat], [v[:, :, NOPE:] for v in w],
                                        k == 0 and tb == 0, k == 2)
                        mm.then_inc(chunks_done, 1)
                    toks += [banks.lend([b0, b0 + 1], "a"), banks.lend([b0 + 2], "v")]
                for n in range(2):
                    b0 = 4 * (1 - n)
                    hold(range(b0, b0 + 4))
                    for k in range(2):
                        c = begin[f"mla_ukv{n}"] + k
                        arrived(c)
                        w = [v.rearrange("p (h e) -> p h e", h=4) for v in parts(c)]
                        lat = hk(3 + k)
                        for hd in range(4):
                            passes(ps(b0 + hd // 2, 1)[:, (hd % 2) * T:(hd % 2 + 1) * T], [v[:, hd, 0:NOPE] for v in w], lat,
                                   k == 0 and hd % 2 == 0, k == 1)
                        for tb in range(TB):
                            mm = passes(ps(b0 + 2 + tb, 1).rearrange("p (h e) -> p h e", h=4),
                                        [v[:, tb * P:(tb + 1) * P] for v in lat], [v[:, :, NOPE:] for v in w],
                                        k == 0, k == 1)
                        mm.then_inc(chunks_done, 1)
                    toks += [banks.lend([b0, b0 + 1], "a"), banks.lend([b0 + 2, b0 + 3], "v")]
                wait_all(toks[:4])
                hold(range(4, 8))
                for hd in range(MLA_HEADS):
                    for tb in range(TB):
                        mm = pe.transpose(ps(4 + hd // 2, 1, ROPE)[:, (hd % 2) * T + tb * P:(hd % 2) * T + (tb + 1) * P],
                                          a["qr"][:, tb, hd, :], ident)
                mm.then_inc(psum_for_act, 1)
                toks.append(banks.lend(range(4, 8), "a"))
                wait_all(toks[4:])
                for n in range(2):
                    hold(range(4))
                    for tb in range(TB):
                        for i in range(4):
                            hd = 4 * n + i
                            o = ps(2 * tb + i // 2, 1)[:, (i % 2) * T:(i % 2 + 1) * T]
                            pe.matmul(o, a["qnT"][:, hd, tb * P:(tb + 1) * P], a["knT"][:, hd, :],
                                      start=(i % 2 == 0), stop=False, skip_group_check=True)
                            mm = pe.matmul(o, a["qrT"][:, hd, tb * P:(tb + 1) * P], a["krT"],
                                           start=False, stop=True, skip_group_check=True)
                    mm.then_inc(psum_for_vec, 1)
                    pe.wait_ge(*banks.lend(range(4), "v"))
                    hold(range(4, 8))
                    wait_all(turn_p(a["p"], 4))
                    hold([0, 1])
                    for i in range(4):
                        for kb in range(TB):
                            mm = pe.matmul(ps(i // 2, 1)[:, (i % 2) * T:(i % 2 + 1) * T],
                                           a["v"][:, kb, (4 * n + i) * VDIM:(4 * n + i + 1) * VDIM], a["pT"][:, i, kb, :],
                                           start=(i % 2 == 0 and kb == 0), stop=(kb == 1), skip_group_check=True)
                    mm.then_inc(psum_for_vec, 1)
                    o_ready = banks.lend([0, 1], "v")
                pe.wait_ge(*o_ready)
                hold(range(4, 8))
                panel("mla_out", hk, "tokens", 4, D)
                banks.lend(range(4, 8), "v")

            def pe_mixers(a):
                for n in range(4):
                    b0 = 4 * ((n + 1) % 2)
                    hold(range(b0, b0 + 4))
                    panel(f"slots{n}", hk, "features", b0, 4)
                    banks.lend(range(b0, b0 + 4), "a")
                hold(range(4, 8))
                panel("diff_v", hk, "tokens", 4, DIFF_W)
                banks.lend(range(4, 8), "a")
                hold(range(4))
                panel("pool_in", hk, "tokens", 0, POOL_W)
                pe.wait_ge(*banks.lend(range(4), "a"))
                hold([0, 1])
                for g in range(4):
                    for tb in range(TB):
                        mm = pe.matmul(ps(g // 2, 1, C)[:, (g % 2) * T:(g % 2 + 1) * T],
                                       a["pv"][:, tb, g * C:(g + 1) * C], a["pool"][:, tb, g, :],
                                       start=(g % 2 == 0 and tb == 0), stop=(tb == 1), skip_group_check=True)
                mm.then_inc(psum_for_vec, 1)
                pe.wait_ge(*banks.lend([0, 1], "v"))
                hold([2, 3])
                for g in range(4):
                    mm = pe.matmul(ps(2 + g // 2, 1, C)[:, (g % 2) * T:(g % 2 + 1) * T], a["pool_w"][:, g, :],
                                   a["d"][:, g, :], start=(g % 2 == 0), stop=True, skip_group_check=True)
                mm.then_inc(psum_for_vec, 1)
                banks.lend([2, 3], "v")
                pe.wait_ge(act_for_pe, act_to_pe.up())
                hold(range(6))
                for w, (wt, slot) in enumerate((("w2", 12), ("a2", 13))):
                    for hd in range(NH):
                        mm = pe.matmul(ps(2 * w + hd // 2, 1, C)[:, (hd % 2) * T:(hd % 2 + 1) * T],
                                       a[wt][:, hd * C:(hd + 1) * C], a["zm"][:, slot, :],
                                       start=(hd % 2 == 0), stop=True, skip_group_check=True)
                for c in range(NC_):
                    for s in range(2):
                        mm = pe.matmul(ps(4 + c // 2, 1, C)[:, (c % 2) * T:(c % 2 + 1) * T],
                                       a["zm"][:, 14 + s, c * C:(c + 1) * C], a["g2"][:, s, :],
                                       start=(c % 2 == 0 and s == 0), stop=(s == 1), skip_group_check=True)
                mm.then_inc(psum_for_act, 1)
                banks.lend(range(6), "a")
                pe.wait_ge(vec_for_pe, to_pe.up())
                hold([6, 7])
                for i in range(2):
                    mm = pe.matmul(ps(6 + i, 1, C), a["ones"], a["kk2"][:, 2 * i:2 * i + 2, :].rearrange("p h t -> p (h t)"),
                                   start=True, stop=True)
                mm.then_inc(psum_for_act, 1)
                banks.lend([6, 7], "a")
                pe.wait_ge(vec_for_pe, to_pe.up())
                hold(range(8))
                vz = a["zm"][:, 8:12, :].rearrange("p h (c t) -> p (h c) t", c=NC_)
                idc = ident[0:C, 0:C]
                for w in range(4):
                    for u in range(UN):
                        src = (a["ar"][:, u, 0, :], a["bt"][:, u, :], a["kt"][:, u, :], vz[:, u, :])[w]
                        mm = pe.transpose(ps(2 * w + u // 8, 1, C)[:, (u % 8) * C:(u % 8 + 1) * C], src, idc)
                    if w == 1:
                        mm.then_inc(psum_for_act, 1)
                mm.then_inc(psum_for_vec, 1)
                turned = [banks.lend(range(4), "a"), banks.lend(range(4, 8), "v")]
                for w, src in enumerate(("bt", "kt")):
                    hold(range(4 * w, 4 * w + 4))
                    for u in range(UN):
                        mm = pe.matmul(ps(4 * w + u // 4, 1, C)[:, (u % 4) * P:(u % 4 + 1) * P], a[src][:, u, :],
                                       a["ar"][:, u, :, :].rearrange("p w t -> p (w t)"), start=(u % 4 == 0), stop=True,
                                       skip_group_check=True)
                    mm.then_inc(psum_for_vec, 1)
                    masked = banks.lend(range(4 * w, 4 * w + 4), "v")
                pe.wait_ge(*masked)
                wait_all(turned)

                def units(b0, lhs, rhs, first=True, last=True, us=range(UN)):
                    for u in us:
                        mm = pe.matmul(ps(b0 + u // 8, 1, C)[:, (u % 8) * C:(u % 8 + 1) * C], lhs(u), rhs(u),
                                       start=(first and u % 8 == 0), stop=last, skip_group_check=True)
                    return mm

                def of(name):
                    return lambda u: a[name][:, u, :]

                def part(name, w):
                    return lambda u: a[name][:, u, w * C:(w + 1) * C]

                def tm(w):
                    return lambda u: a["tm"][:, w, u, :]

                for b in range(LEVELS):
                    pe.wait_ge(vec_for_pe, to_pe.up())
                    hold([0, 1])
                    units(0, of("aoff"), of("Tm")).then_inc(psum_for_vec, 1)
                    pe.wait_ge(*banks.lend([0, 1], "v"))
                    hold(range(2, 6))
                    units(2, of("TmT"), of("X"))
                    units(4, of("X"), of("TmT")).then_inc(psum_for_vec, 1)
                    inverse = banks.lend(range(2, 6), "v")
                hold([0, 1])
                units(0, part("mak", 0), tm(3)).then_inc(psum_for_act, 1)
                akv = banks.lend([0, 1], "a")
                pe.wait_ge(*inverse)
                hold([2, 3])
                units(2, of("TmT"), tm(0)).then_inc(psum_for_vec, 1)
                g1 = banks.lend([2, 3], "v")
                pe.wait_ge(*akv)
                hold([6, 7])
                units(6, of("TmT"), of("AkV")).then_inc(psum_for_act, 1)
                u0 = banks.lend([6, 7], "a")
                pe.wait_ge(*g1)
                hold(range(4))
                units(0, of("G1"), part("mab", 1))
                units(2, of("G1"), tm(1)).then_inc(psum_for_vec, 1)
                qm = banks.lend(range(4), "v")
                hold([4, 5])
                units(4, lambda u: a["rk"][:, u, :], lambda u: a["ones"]).then_inc(psum_for_act, 1)
                banks.lend([4, 5], "a")
                pe.wait_ge(*u0)
                pe.wait_ge(*qm)
                hold(range(0, 8))
                units(0, part("mab", 1), of("U0"), last=False)
                units(0, part("mak", 1), tm(3), first=False, last=False)
                for c in range(NC_):
                    mine = [hd * NC_ + c for hd in range(NH)]
                    if c:
                        pe.wait_ge(*state)
                        mm = units(0, of("Q"), lambda u: a["S"][:, c - 1, u // NC_, :], first=False, us=mine)
                    if c < NC_ - 1:
                        terms = [(tm(1), of("U0")), (tm(2), tm(3))]
                        if c:
                            terms.append((of("Mt"), lambda u: a["S"][:, c - 1, u // NC_, :]))
                        for i, (lhs, rhs) in enumerate(terms):
                            for u in mine:
                                hd = u // NC_
                                mm = pe.matmul(ps(2 + c, 1, C)[:, hd * C:(hd + 1) * C], lhs(u), rhs(u),
                                               start=(i == 0 and hd == 0), stop=(i == len(terms) - 1), skip_group_check=True)
                        mm.then_inc(psum_for_vec, 1)
                        state = banks.lend([2 + c], "v")
                mm.then_inc(psum_for_vec, 1)
                pe.wait_ge(*banks.lend([0, 1], "v"))
                hold([6, 7])
                for u in range(UN):
                    mm = pe.transpose(ps(6 + u // 8, 1, C)[:, (u % 8) * C:(u % 8 + 1) * C], a["y"][:, u, :], idc)
                mm.then_inc(psum_for_act, 1)
                rwkv = banks.lend([6, 7], "a")
                pe.wait_ge(act_for_pe, act_to_pe.up())
                pe.wait_ge(*rwkv)
                hold(range(8))
                for i in range(8):
                    mm = pe.matmul(ps(i, 1, C), a["ones"],
                                   a["sq"][:, i // 4, 2 * (i % 4):2 * (i % 4) + 2, :].rearrange("p s t -> p (s t)"),
                                   start=True, stop=True)
                mm.then_inc(psum_for_vec, 1)
                pe.wait_ge(*banks.lend(range(8), "v"))
                for c in range(2):
                    b0 = 4 * c
                    for tb in range(TB):
                        for hd in range(4):
                            mm = pe.matmul(ps(b0 + 2 * tb + hd // 2, 1)[:, (hd % 2) * T:(hd % 2 + 1) * T],
                                           a["qk"][:, 0, 2 * hd + c, tb * P:(tb + 1) * P], a["qk"][:, 1, 2 * hd + c, :],
                                           start=(hd % 2 == 0), stop=True, skip_group_check=True)
                    mm.then_inc(psum_for_vec, 1)
                    probs = banks.lend(range(b0, b0 + 4), "v")
                pe.wait_ge(*probs)
                wait_all(turn_p(a["p"][:, 0], 4))
                hold([0, 1])
                for tb in range(TB):
                    for hd in range(4):
                        for kb in range(TB):
                            mm = pe.matmul(ps(tb, 1)[:, hd * P:(hd + 1) * P], a["pT"][:, hd, kb, tb * P:(tb + 1) * P],
                                           a["pv"][:, kb, POOL_W + hd * P:POOL_W + (hd + 1) * P],
                                           start=(hd == 0 and kb == 0), stop=(kb == 1), skip_group_check=True)
                mm.then_inc(psum_for_vec, 1)
                pe.wait_ge(*banks.lend([0, 1], "v"))
                hold([2, 3])
                for hd in range(4):
                    for tb in range(TB):
                        mm = pe.transpose(ps(2 + hd // 2, 1)[:, (hd % 2) * T + tb * P:(hd % 2) * T + (tb + 1) * P],
                                          a["o"][:, tb, hd, :], ident)
                mm.then_inc(psum_for_act, 1)
                pe.wait_ge(*banks.lend([2, 3], "a"))
                hold(range(4, 8))
                lhs = [a["poolT"][:, i, :] for i in range(4)] + [a["rT"][:, i, :] for i in range(4)] + [a["oT"][:, i, :] for i in range(4)]
                panel("mix_out", lambda k: lhs[k], "tokens", 4, D, k_rows=[C] * 8 + [P] * 4)
                banks.lend(range(4, 8), "v")

            def pe_cross(a):
                pe.wait_ge(vec_for_pe, to_pe.up())
                hold(range(4, 8))
                wait_all(transpose_in(lambda k, tb: a["mn"][:, tb, k * P:(k + 1) * P], KD, b0=4))
                hold(range(4))
                panel("xa_wk_2", hk, "tokens", 0, D)
                kn = banks.lend(range(4), "v")
                hold(range(4, 8))
                panel("xa_wv_2", hk, "tokens", 4, D)
                vv = banks.lend(range(4, 8), "a")
                pe.wait_ge(*kn)
                hold(range(4))
                wait_all(transpose_in(lambda k, tb: a["k"][:, tb, k * P:(k + 1) * P], KD, who="va"))
                stream_T(0, a["hn"])
                hold(range(4, 8))
                panel("xa_wq_2", hk, "tokens", 4, D)
                pe.wait_ge(*banks.lend(range(4, 8), "v"))
                hold(range(4))
                wait_all(transpose_in(lambda k, tb: a["q"][:, tb, k * P:(k + 1) * P], KD, who="va"))
                hold(range(4, 8))
                for tb in range(TB):
                    for hd in range(XH):
                        for d in range(2):
                            mm = pe.matmul(ps(4 + 2 * tb + hd // 2, 1)[:, (hd % 2) * T:(hd % 2 + 1) * T],
                                           a["qT"][:, 2 * hd + d, tb * P:(tb + 1) * P], a["kT"][:, 2 * hd + d, :],
                                           start=(hd % 2 == 0 and d == 0), stop=(d == 1), skip_group_check=True)
                mm.then_inc(psum_for_vec, 1)
                pe.wait_ge(*banks.lend(range(4, 8), "v"))
                hold(range(4))
                wait_all(turn_p(a["p"], 0))
                pe.wait_ge(*vv)
                hold(range(4, 8))
                for i in range(8):
                    for kb in range(TB):
                        mm = pe.matmul(ps(4 + i // 2, 1)[:, (i % 2) * T:(i % 2 + 1) * T],
                                       a["v"][:, kb, i * P:(i + 1) * P], a["pT"][:, i // 2, kb, :],
                                       start=(i % 2 == 0 and kb == 0), stop=(kb == 1), skip_group_check=True)
                mm.then_inc(psum_for_vec, 1)
                pe.wait_ge(*banks.lend(range(4, 8), "v"))
                hold(range(4))
                panel("xa_wo_2", hk, "tokens", 0, D)
                banks.lend(range(4), "v")

            def pe_ffn(a):
                for n in range(6):
                    b0 = 4 * ((n + 1) % 2)
                    hold(range(b0, b0 + 4))
                    panel(f"up{n}", hk, "features", b0, 2 * min(4, FF_TILES - 4 * n))
                    hid = banks.lend(range(b0, b0 + 4), "v")
                pe.wait_ge(*hid)
                hold(range(4, 8))
                panel("down", four_by_four, "tokens", 4, D, fed=0)
                banks.lend(range(4, 8), "v")

            for n, phase in enumerate(phases):
                if phase in ("mixers", "ffn"):
                    stream_T(n, A[phase]["hn"])
                elif phase != "cross":
                    stream_T(n)
                if phase == "retention":
                    pe_retention(A[phase])
                if phase == "mla":
                    pe_mla(A[phase])
                if phase == "mixers":
                    pe_mixers(A[phase])
                if phase == "cross":
                    pe_cross(A[phase])
                if phase == "ffn":
                    pe_ffn(A[phase])
                if phase.startswith("peer"):
                    pe_peer(phase, A[phase])

        @block.vector
        def _(vec):
            own = Last(vec_step)
            psum_v, from_act = Count(), Count()

            def done():
                vec.wait_ge(*own.last)

            n_split = Count()

            def round_to(hi, src):
                return vec.tensor_copy(hi, src)

            def split_chunk(slot, part, loaded, read, count, k=P, wide=SLOT):
                vec.wait_ge(ring_loaded[slot], loaded)
                if read is not None:
                    vec.wait_ge(chunks_done, read)
                whole, top = ring[0:k, slot, 0:wide], ring_hi[0:k, part, 0:wide]
                round_to(top, whole).then_inc(chunk_hi, 1)
                vec.wait_ge(chunk_hi, count)
                vec.tensor_tensor(ring_lo[0:k, part, 0:wide], whole, top.bitcast(F32), ALU.subtract).then_inc(chunk_split, 1)
                own.last = (chunk_split, count)

            def split_to(end_):
                while n_split.n < min(end_, n_chunks):
                    n = n_split.n
                    if n in split_count:
                        k, wide = chunk_size[n]
                        split_chunk(n % RING, n % SPLIT, 16 * (n // RING + 1), n - 1 if n >= SPLIT else None,
                                    split_count[n], k, wide)
                    n_split.up()

            def more(k, key):
                split_to(min(n_split.n + k, end[key] + SPLIT))

            def panel_done(key):
                split_to(end[key] + SPLIT)
                vec.wait_ge(chunks_done, end[key])

            def ln_stream(key, b0, phase):
                flat, norm = h.rearrange("p a b -> p (a b)"), A[phase]["norm"]
                panel_done(key)
                vec.scalar_tensor_tensor(flat, flat, ALPHA, ps(b0, 4), ALU.mult, ALU.add).then_inc(*own.mark(vec_served))
                done()
                for tb in range(TB):
                    for c in range(2):
                        vec.bn_stats(stats[:, 2 * tb + c, 0, :], h[:, tb, c * BANK:(c + 1) * BANK]).then_inc(*own.next())
                done()
                for tb in range(TB):
                    vec.bn_aggr(mv[:, tb, :], stats[:, 2 * tb:2 * tb + 2, 0, :]).then_inc(*own.next())
                done()
                vec.tensor_scalar(rstd[:, 0:TB], mv[:, :, 1], LN_EPS, None, ALU.add).then_inc(*own.mark(vec_for_act))
                more(2, key)
                vec.wait_ge(act_for_vec, from_act.up())
                vec.reciprocal(rstd[:, 0:TB], rstd[:, 0:TB]).then_inc(*own.next())
                done()
                vec.wait_ge(params_loaded, loads[phase])
                for tb in range(TB):
                    vec.tensor_scalar(h[:, tb, :], h[:, tb, :], mv[:, tb, 0:1], rstd[:, tb:tb + 1],
                                      ALU.subtract, ALU.mult).then_inc(*own.next())
                done()
                vec.tensor_tensor(h, h, bcast(norm[:, 0, :], 1, TB), ALU.mult).then_inc(*own.next())
                done()
                vec.tensor_tensor(h, h, bcast(norm[:, 1, :], 1, TB), ALU.add).then_inc(*own.mark(phase_done))
                done()

            def take_turned(dst, b0):
                vec.wait_ge(psum_for_vec, psum_v.up())
                vec.tensor_copy(dst.rearrange("p a b -> p (a b)"), ps(b0, 2)).then_inc(*own.mark(vec_served))

            def take_split(hi, lo, b0, nb, wide=None):
                hi, lo = (v.rearrange("p a b -> p (a b)") for v in (hi, lo))
                src = ps(b0, nb)[:, 0:wide or nb * BANK]
                round_to(hi, src).then_inc(*own.next())
                done()
                vec.tensor_tensor(lo, src, hi.bitcast(F32), ALU.subtract).then_inc(*own.mark(vec_served))
                done()

            def feed(key, src, first=0):
                for k in range(first, end[key] - begin[key], 4):
                    if k >= KD:
                        split_to(begin[key] + k - 2)
                        vec.wait_ge(chunks_done, begin[key] + k - 4)
                    w = min(4, end[key] - begin[key] - k)
                    hi, lo = (hT[:, i, k % KD:k % KD + w, :] for i in range(2))
                    round_to(hi, src[:, k:k + w, :]).then_inc(*own.next())
                    done()
                    vec.tensor_tensor(lo, src[:, k:k + w, :], hi.bitcast(F32), ALU.subtract).then_inc(*own.mark(vec_for_pe))
                    done()

            def take_matrix(dst, b0=0):
                for i in range(2):
                    vec.wait_ge(psum_for_vec, psum_v.up())
                    take_split(dst[:, 0, 4 * i:4 * i + 4, :], dst[:, 1, 4 * i:4 * i + 4, :], b0 + 2 * i, 2)

            def reduced(dst, ang, turn, quarter):
                vec.tensor_scalar(turn, ang, 1.0 / (2 * np.pi), 0.25 if quarter else 0.0, ALU.mult, ALU.add).then_inc(*own.next())
                done()
                vec.tensor_scalar(turn, turn, ROUND, None, ALU.add).then_inc(*own.next())
                done()
                vec.tensor_scalar(turn, turn, -ROUND, None, ALU.add).then_inc(*own.next())
                done()
                vec.scalar_tensor_tensor(dst, turn, -TWO_PI_HI, ang, ALU.mult, ALU.add).then_inc(*own.next())
                done()
                vec.scalar_tensor_tensor(dst, turn, -TWO_PI_LO, dst, ALU.mult, ALU.add).then_inc(*own.next())
                done()
                if quarter:
                    vec.tensor_scalar(dst, dst, float(np.pi / 2), None, ALU.add).then_inc(*own.next())
                    done()
                vec.tensor_scalar(dst, dst, PI_IN, -PI_IN, ALU.min, ALU.max).then_inc(*own.next())
                done()

            def vec_retention(a, phase):
                split_to(2)
                vec.wait_ge(params_loaded, loads[phase])
                vec.tensor_copy(a["ang"], a["posi"].bitcast(I32)).then_inc(*own.next())
                done()
                vec.tensor_scalar(a["ang"], a["ang"], a["freq"], None, ALU.mult).then_inc(*own.next())
                done()
                reduced(a["cos"], a["ang"], a["turn"], True)
                reduced(a["sin"], a["ang"], a["turn"], False)
                vec.tensor_copy(a["turn"], a["ang"]).then_inc(*own.mark(vec_for_act))
                vec.wait_ge(act_for_vec, from_act.up())
                for hd in range(RET_HEADS):
                    vec.tensor_scalar(a["decay"][:, hd, :], a["ahead"][:, 0, :], a["lg"][:, hd:hd + 1], None,
                                      ALU.mult).then_inc(*own.next())
                done()
                for hd in range(RET_HEADS):
                    vec.scalar_tensor_tensor(a["decay"][:, hd, :], a["ahead"][:, 1, :], a["lg"][:, 4 + hd:5 + hd],
                                             a["decay"][:, hd, :], ALU.mult, ALU.add).then_inc(
                        *(own.mark(vec_for_act) if hd == RET_HEADS - 1 else own.next()))
                vec.wait_ge(act_for_vec, from_act.up())
                cos, sin = bcast(a["cos"], 1, RET_HEADS), bcast(a["sin"], 1, RET_HEADS)
                for w, (dst, b0) in enumerate(((a["qT"], 4), (a["kT"], 0))):
                    panel_done(f"ret_in{w}")
                    src = ps(b0, 4).rearrange("p (h two t) -> p h two t", two=2, t=T)
                    to = dst.rearrange("p (h two) t -> p h two t", two=2)
                    x1, x2 = src[:, :, 0, :], src[:, :, 1, :]
                    t1, t2 = a["tmp"][:, 0], a["tmp"][:, 1]
                    vec.tensor_tensor(t1, x1, cos, ALU.mult).then_inc(*own.next())
                    vec.tensor_tensor(t2, x2, sin, ALU.mult).then_inc(*own.next())
                    done()
                    vec.tensor_tensor(to[:, :, 0, :], t1, t2, ALU.subtract).then_inc(*own.next())
                    done()
                    vec.tensor_tensor(t1, x1, sin, ALU.mult).then_inc(*own.next())
                    vec.tensor_tensor(t2, x2, cos, ALU.mult).then_inc(*own.next())
                    done()
                    vec.tensor_tensor(to[:, :, 1, :], t1, t2, ALU.add).then_inc(*own.mark(vec_served))
                    done()
                split_to(end["ret_in5"] + SPLIT)
                vec.wait_ge(psum_for_vec, psum_v.up())
                vec.scalar_tensor_tensor(a["s"].rearrange("p a b c -> p (a b c)"), ps(4, 4), RET_DK ** -0.5,
                                         a["decay"].rearrange("p a b -> p (a b)"), ALU.mult, ALU.mult).then_inc(*own.mark(vec_served))
                for tb in range(TB):
                    vec.wait_ge(psum_for_vec, psum_v.up())
                    for hd in range(RET_HEADS):
                        vec.bn_stats(stats[:, hd, 0, :], ps(4 * tb + hd, 1)).then_inc(*own.next())
                    done()
                    for hd in range(RET_HEADS):
                        vec.bn_aggr(var8[:, 4 * tb + hd, :], stats[:, hd, 0, :]).then_inc(*own.next())
                    done()
                    r = rstd[:, 4 * tb:4 * tb + 4]
                    vec.tensor_scalar(r, var8[:, 4 * tb:4 * tb + 4, 1], LN_EPS, None, ALU.add).then_inc(*own.mark(vec_for_act))
                    vec.wait_ge(act_for_vec, from_act.up())
                    vec.reciprocal(r, r).then_inc(*own.next())
                    done()
                    for hd in range(RET_HEADS):
                        vec.tensor_scalar(a["y"][:, tb, hd * BANK:(hd + 1) * BANK], ps(4 * tb + hd, 1),
                                          var8[:, 4 * tb + hd, 0:1], r[:, hd:hd + 1], ALU.subtract, ALU.mult).then_inc(*own.next())
                    done()
                    y = a["y"][:, tb, :]
                    vec.tensor_tensor(y, y, a["gn"][:, 0, :], ALU.mult).then_inc(*own.next())
                    done()
                    vec.tensor_tensor(y, y, a["gn"][:, 1, :], ALU.add).then_inc(*own.next())
                    done()
                    vec.tensor_tensor(y, y, a["g"][:, tb, :], ALU.mult).then_inc(*own.mark(vec_served))
                    done()
                for i in range(4):
                    from_psum()
                    if i < 2:
                        take_split(hT[:, 0, 4 * i:4 * i + 4, :], hT[:, 1, 4 * i:4 * i + 4, :], 2 * i, 2)
                    else:
                        vec.tensor_copy(a["yT"][:, 4 * i:4 * i + 4, :].rearrange("p a b -> p (a b)"), ps(2 * i, 2)).then_inc(*served())
                done()
                feed("ret_out", a["yT"], KD)
                ln_stream("ret_out", 0, phase)

            def rms_stream(src, dst, gain, phase):
                for tb in range(TB):
                    for c in range(2):
                        vec.bn_stats(stats[:, 2 * tb + c, 0, :], src[:, tb, c * BANK:(c + 1) * BANK]).then_inc(*own.next())
                done()
                for tb in range(TB):
                    vec.bn_aggr(mv[:, tb, :], stats[:, 2 * tb:2 * tb + 2, 0, :]).then_inc(*own.next())
                done()
                r = rstd[:, 0:TB]
                vec.tensor_tensor(r, mv[:, :, 0], mv[:, :, 0], ALU.mult).then_inc(*own.next())
                done()
                vec.scalar_tensor_tensor(r, r, RMS_EPS, mv[:, :, 1], ALU.add, ALU.add).then_inc(*own.mark(vec_for_act))
                vec.wait_ge(act_for_vec, from_act.up())
                vec.reciprocal(r, r).then_inc(*own.next())
                done()
                vec.wait_ge(params_loaded, loads[phase])
                for tb in range(TB):
                    vec.scalar_tensor_tensor(dst[:, tb, :], src[:, tb, :], rstd[:, tb:tb + 1], gain, ALU.mult, ALU.mult).then_inc(
                        *(own.mark(vec_for_pe) if tb == TB - 1 else own.next()))
                done()

            def add_stream(key, b0):
                flat = h.rearrange("p a b -> p (a b)")
                panel_done(key)
                vec.tensor_tensor(flat, flat, ps(b0, 4), ALU.add).then_inc(*own.mark(vec_served))
                done()
                vec.tensor_copy(misc[:, 511:512], iota[:, 0:1]).then_inc(*own.mark(phase_done))
                done()

            def softmax(src, p, top, total, last):
                rows_ = p.rearrange("p b h k -> p (b h) k")
                vec.tensor_reduce(top, src, AX, ALU.max).then_inc(*own.next())
                done()
                vec.tensor_tensor(rows_, src, bcast(top, 2, T), ALU.subtract).then_inc(*own.mark(vec_for_act))
                vec.wait_ge(act_for_vec, from_act.up())
                vec.tensor_reduce(total, rows_, AX, ALU.add).then_inc(*own.next())
                done()
                vec.reciprocal(total, total).then_inc(*own.next())
                done()
                vec.tensor_tensor(rows_, rows_, bcast(total, 2, T), ALU.mult).then_inc(*last())
                done()

            def served():
                return own.mark(vec_served)

            def from_psum():
                vec.wait_ge(psum_for_vec, psum_v.up())

            def rooted(v, scale, eps):
                vec.tensor_scalar(v, v, scale, eps, ALU.mult, ALU.add).then_inc(*own.mark(vec_for_act))
                vec.wait_ge(act_for_vec, from_act.up())
                vec.reciprocal(v, v).then_inc(*own.next())
                done()

            top8, sum8 = misc[:, 256:264], misc[:, 264:272]

            def vec_mla(a, phase):
                half = ROPE // 2
                vec.wait_ge(params_loaded, loads[phase])
                vec.tensor_copy(a["pos"], a["posi"].bitcast(I32)).then_inc(*own.next())
                done()
                for tb in range(TB):
                    vec.tensor_scalar(a["ang"][:, tb, :], a["freq"], a["pos"][:, tb:tb + 1], None, ALU.mult).then_inc(*own.next())
                done()
                reduced(a["cos"], a["ang"], a["turn"], True)
                reduced(a["sin"], a["ang"], a["turn"], False)
                vec.tensor_copy(a["turn"], a["ang"]).then_inc(*own.mark(vec_for_act))
                panel_done("mla_in")
                c, r = a["c"], rstd[:, 0:4]
                vec.tensor_copy(c, ps(4, 4).rearrange("p (b c) -> p b c", b=TB)[:, :, 0:MLA_IN]).then_inc(*own.next())
                done()
                vec.tensor_tensor(a["sq"], c[:, :, 0:Q_RANK + KV_RANK], c[:, :, 0:Q_RANK + KV_RANK], ALU.mult).then_inc(*own.next())
                done()
                vec.tensor_reduce(r[:, 0:2], a["sq"][:, :, 0:Q_RANK], AX, ALU.add).then_inc(*own.next())
                vec.tensor_reduce(r[:, 2:4], a["sq"][:, :, Q_RANK:], AX, ALU.add).then_inc(*own.next())
                done()
                vec.tensor_scalar(r[:, 0:2], r[:, 0:2], 1.0 / Q_RANK, LN_EPS, ALU.mult, ALU.add).then_inc(*own.next())
                vec.wait_ge(act_for_vec, from_act.up())
                vec.tensor_scalar(r[:, 2:4], r[:, 2:4], 1.0 / KV_RANK, LN_EPS, ALU.mult, ALU.add).then_inc(*own.mark(vec_for_act))
                vec.wait_ge(act_for_vec, from_act.up())
                vec.reciprocal(r, r).then_inc(*own.next())
                done()
                for tb in range(TB):
                    for i, s in enumerate((slice(0, Q_RANK), slice(Q_RANK, Q_RANK + KV_RANK))):
                        vec.scalar_tensor_tensor(c[:, tb, s], c[:, tb, s], r[:, 2 * i + tb:2 * i + tb + 1], a["gain"][:, s],
                                                 ALU.mult, ALU.mult).then_inc(*own.next())

                def rotate(x1, x2, o1, o2, cos, sin, t):
                    vec.tensor_tensor(t[0], x1, cos, ALU.mult).then_inc(*own.next())
                    vec.tensor_tensor(t[1], x2, sin, ALU.mult).then_inc(*own.next())
                    vec.tensor_tensor(t[2], x1, sin, ALU.mult).then_inc(*own.next())
                    vec.tensor_tensor(t[3], x2, cos, ALU.mult).then_inc(*own.next())
                    done()
                    vec.tensor_tensor(o1, t[0], t[1], ALU.subtract).then_inc(*own.next())
                    vec.tensor_tensor(o2, t[2], t[3], ALU.add).then_inc(*own.mark(vec_served))
                    done()

                k1, k2 = c[:, :, MLA_IN - ROPE:MLA_IN - half], c[:, :, MLA_IN - half:]
                rotate(k1, k2, k1, k2, a["cos"], a["sin"],
                       [a["tmp"][:, i, 0:TB * half].rearrange("p (b e) -> p b e", b=TB) for i in range(4)])
                from_psum()
                vec.tensor_copy(a["krT"], ps(2, 1, ROPE)[:, T:]).then_inc(*own.next())
                take_split(hT[:, 0, 0:5, :], hT[:, 1, 0:5, :], 0, 3, 5 * T)
                for i in range(2):
                    b0 = 4 * (1 - i)
                    panel_done(f"mla_uq{i}")
                    q = ps(b0 + 2, 1).rearrange("p (b h e) -> p b h e", b=TB, h=4)
                    to = a["qr"][:, :, 4 * i:4 * i + 4, :]
                    rotate(q[:, :, :, 0:half], q[:, :, :, half:], to[:, :, :, 0:half], to[:, :, :, half:],
                           bcast(a["cos"], 2, 4), bcast(a["sin"], 2, 4),
                           [a["tmp"][:, j, :].rearrange("p (b h e) -> p b h e", b=TB, h=4) for j in range(4)])
                for i in range(2):
                    b0 = 4 * (1 - i)
                    panel_done(f"mla_ukv{i}")
                    vec.tensor_copy(a["v"][:, :, i * BANK:(i + 1) * BANK],
                                    ps(b0 + 2, 2).rearrange("p (b c) -> p b c", b=TB)).then_inc(*served())
                for i in range(2):
                    from_psum()
                    softmax(ps(0, 4).rearrange("p (r k) -> p r k", k=T), a["p"], top8, sum8, served)
                    take_turned(a["pT"].rearrange("p h k t -> p (h k) t")[:, 0:4, :], 4)
                    from_psum()
                    take_split(hT[:, 0, 4 * i:4 * i + 4, :], hT[:, 1, 4 * i:4 * i + 4, :], 0, 2)
                ln_stream("mla_out", 4, phase)

            def vec_mixers(a):
                cols, zm = a["cols"], a["zm"]

                def col(i):
                    return bcast(cols[:, i, :], 2, T)

                def u3(v):
                    return v.rearrange("p h (c t) -> p (h c) t", c=NC_)

                def flat(v):
                    return v.rearrange("p a b -> p (a b)")

                vec.memset(a["z"][:, :, 0:1], 0.0).then_inc(*own.next())
                vec.memset(a["ones"], 1.0).then_inc(*own.next())
                split_to(end["slots1"] + SPLIT)
                vec.wait_ge(act_for_vec, from_act.up())
                done()
                vec.tensor_tensor(zm, a["z"][:, :, 0:T], a["z"][:, :, 1:T + 1], ALU.subtract).then_inc(*own.next())
                more(6, "slots3")
                done()
                vec.tensor_tensor(zm, zm, bcast(a["mu"], 2, T), ALU.mult).then_inc(*own.next())
                more(6, "slots3")
                done()
                vec.tensor_tensor(zm, zm, a["z"][:, :, 1:T + 1], ALU.add).then_inc(*own.mark(vec_for_act))
                split_to(end["pool_in"])
                done()
                from_psum()
                vec.tensor_copy(flat(a["d"]), ps(0, 2, C)).then_inc(*served())
                from_psum()
                vec.tensor_tensor(a["poolT"], ps(2, 2, C).rearrange("p (h t) -> p h t", t=T), col(5), ALU.mult).then_inc(*served())
                r_, k_ = zm[:, 0:4, :], zm[:, 4:8, :]
                vec.tensor_tensor(a["kk"], k_, col(2), ALU.mult).then_inc(*own.next())
                vec.wait_ge(act_for_vec, from_act.up())
                vec.tensor_scalar(a["lw"], a["lw"], -float(np.exp(-0.5)), None, ALU.mult).then_inc(*own.next())
                done()
                vec.tensor_tensor_scan(flat(a["L"]), a["masks"][:, (2 + LEVELS) * C:], flat(a["lw"]), 0.0,
                                       ALU.mult, ALU.add).then_inc(*own.next())
                done()
                vec.tensor_tensor(a["Pp"], a["L"], a["lw"], ALU.subtract).then_inc(*own.mark(vec_for_act))
                done()
                vec.tensor_tensor(a["kk2"], a["kk"], a["kk"], ALU.mult).then_inc(*own.mark(vec_for_pe))
                kx = a["kx"]
                vec.tensor_scalar(kx, a["a"], -1.0, None, ALU.add).then_inc(*own.next())
                done()
                vec.tensor_tensor(kx, kx, col(3), ALU.mult).then_inc(*own.next())
                done()
                vec.scalar_tensor_tensor(kx, kx, 1.0, k_, ALU.add, ALU.mult).then_inc(*own.next())
                done()
                rk = a["rk"].rearrange("p (h c) t -> p h (c t)", h=NH)
                vec.tensor_tensor(rk, r_, kx, ALU.mult).then_inc(*own.next())
                done()
                vec.tensor_tensor(rk, rk, col(4), ALU.mult).then_inc(*own.next())
                vec.wait_ge(act_for_vec, from_act.up())
                vec.tensor_tensor(a["ar"][:, :, 1, :], u3(r_), u3(a["Pd"]), ALU.mult).then_inc(*own.next())
                vec.tensor_tensor(a["kt"], u3(kx), u3(a["Pi"]), ALU.mult).then_inc(*own.next())
                vec.tensor_copy(a["pend"], u3(a["Pd"])[:, :, C - 1]).then_inc(*own.next())
                vec.wait_ge(act_for_vec, from_act.up())
                n2 = a["kk2"]
                vec.tensor_scalar(n2, n2, 1e-12, None, ALU.max).then_inc(*own.next())
                done()
                vec.reciprocal(n2, n2).then_inc(*own.next())
                done()
                vec.tensor_tensor(a["kk"], a["kk"], n2, ALU.mult).then_inc(*own.next())
                done()
                vec.scalar_tensor_tensor(a["ar"][:, :, 0, :], u3(a["kk"]), -1.0, u3(a["Pp"]), ALU.mult, ALU.mult).then_inc(*own.next())
                done()
                vec.tensor_tensor(a["kk"], a["kk"], a["a"], ALU.mult).then_inc(*own.next())
                done()
                vec.tensor_tensor(a["bt"], u3(a["kk"]), u3(a["Pi"]), ALU.mult).then_inc(*own.mark(vec_for_pe))
                done()
                from_psum()
                vec.tensor_copy(a["tm"][:, 2:4].rearrange("p w u c -> p (w u c)"), ps(4, 4, C)).then_inc(*served())
                for i, name in enumerate(("mab", "mak")):
                    from_psum()
                    vec.tensor_tensor(a[name], ps(4 * i, 4, C).rearrange("p (u t) -> p u t", u=UN),
                                      bcast(a["masks"][:, 0:2 * C], 1, UN), ALU.mult).then_inc(*served())
                idc = bcast(ident[0:C, 0:C], 1, UN)
                vec.tensor_copy(a["Tm"], idc).then_inc(*own.next())
                vec.tensor_copy(a["TmT"], idc).then_inc(*own.next())
                done()

                def units(b0):
                    return ps(b0, 2, C).rearrange("p (u c) -> p u c", u=UN)

                for b in range(LEVELS):
                    vec.tensor_tensor(a["aoff"], a["mab"][:, :, 0:C], bcast(a["masks"][:, (2 + b) * C:(3 + b) * C], 1, UN),
                                      ALU.mult).then_inc(*own.mark(vec_for_pe))
                    from_psum()
                    vec.tensor_copy(a["X"], units(0)).then_inc(*served())
                    from_psum()
                    vec.tensor_tensor(a["Tm"], a["Tm"], units(2), ALU.add).then_inc(*own.next())
                    vec.tensor_tensor(a["TmT"], a["TmT"], units(4), ALU.add).then_inc(*served())
                    done()
                from_psum()
                vec.tensor_copy(a["G1"], units(2)).then_inc(*served())
                from_psum()
                vec.tensor_tensor(a["Q"], units(0), a["ar"][:, :, 1, :], ALU.add).then_inc(*own.next())
                vec.tensor_tensor(a["Mt"], units(2), idc, ALU.add).then_inc(*served())
                pend = a["pend"].rearrange("p (h c) -> p h c", h=NH)
                for c in range(NC_ - 1):
                    from_psum()
                    vec.tensor_tensor(a["S"][:, c], ps(2 + c, 1, C)[:, 0:NH * C].rearrange("p (h v) -> p h v", h=NH),
                                      bcast(pend[:, :, c], 2, C), ALU.mult).then_inc(*served())
                from_psum()
                y, ysq, mean, var = a["y"], a["ysq"], rstd[0:C, :], misc[0:C, 288:304]
                vec.tensor_reduce(mean, units(0), AX, ALU.add).then_inc(*own.next())
                done()
                vec.tensor_scalar(mean, mean, 1.0 / C, None, ALU.mult).then_inc(*own.next())
                done()
                vec.tensor_tensor(y, units(0), bcast(mean, 2, C), ALU.subtract).then_inc(*own.next())
                done()
                vec.tensor_tensor(ysq, y, y, ALU.mult).then_inc(*own.next())
                done()
                vec.tensor_reduce(var, ysq, AX, ALU.add).then_inc(*own.next())
                done()
                rooted(var, 1.0 / C, RWKV_EPS)
                vec.tensor_tensor(y, y, bcast(var, 2, C), ALU.mult).then_inc(*own.next())
                vec.tensor_tensor(a["X"], a["X"], a["tm"][:, 3], ALU.mult).then_inc(*own.next())
                done()
                y4 = y.rearrange("p (h c) v -> p h c v", h=NH)
                for i, op in enumerate((ALU.mult, ALU.add)):
                    for hd in range(NH):
                        vec.tensor_tensor(y4[:, hd], y4[:, hd], bcast(a["ln"][:, i, hd * C:(hd + 1) * C], 1, NC_), op).then_inc(*own.next())
                    done()
                vec.tensor_tensor(y, y, a["X"], ALU.add).then_inc(*own.next())
                done()
                g4 = a["g"].rearrange("p c (h v) -> p h c v", h=NH)
                for hd in range(NH):
                    vec.tensor_tensor(y4[:, hd], y4[:, hd], g4[:, hd], ALU.mult).then_inc(*(served() if hd == NH - 1 else own.next()))
                done()
                lq, lam = a["lq"], a["lam"]
                vec.tensor_tensor(lq[:, 0], lq[:, 0], lq[:, 1], ALU.mult).then_inc(*own.next())
                done()
                vec.tensor_reduce(lam[:, 0:2], lq[:, 0], AX, ALU.add).then_inc(*own.mark(vec_for_act))
                vec.wait_ge(act_for_vec, from_act.up())
                vec.tensor_tensor(lam[:, 2:3], lam[:, 1:2], lam[:, 0:1], ALU.subtract).then_inc(*own.next())
                done()
                vec.tensor_scalar(lam[:, 2:3], lam[:, 2:3], -LAMBDA_INIT, None, ALU.add).then_inc(*own.next())
                from_psum()
                rs = a["rs"].rearrange("p w s t -> p (w s t)")
                vec.tensor_scalar(rs, ps(0, 8, C), 1.0 / C, RMS_EPS, ALU.mult, ALU.add).then_inc(*own.mark(vec_for_act))
                vec.wait_ge(act_for_vec, from_act.up())
                vec.reciprocal(rs, rs).then_inc(*own.next())
                done()
                qk = a["qk"]
                vec.tensor_tensor(qk, qk, a["rs"], ALU.mult).then_inc(*own.next())
                done()
                for w in range(2):
                    for c in range(2):
                        v = qk[:, w].rearrange("p (h c) t -> p h c t", c=2)[:, :, c, :]
                        vec.tensor_scalar(v, v, a["qk_gain"][:, w, c:c + 1], None, ALU.mult).then_inc(
                            *(served() if w and c else own.next()))
                done()
                vec.wait_ge(alibi_loaded, 16)
                for c in range(2):
                    from_psum()
                    p = a["p"][:, c]
                    rows_ = p.rearrange("p b h k -> p (b h) k")
                    vec.scalar_tensor_tensor(p.rearrange("p b h k -> p (b h k)"), ps(4 * c, 4), C ** -0.5,
                                             a["alibi"].rearrange("p b h k -> p (b h k)"), ALU.mult, ALU.add).then_inc(*own.next())
                    done()
                    softmax(rows_, p, top8, sum8, own.next if c else served)
                p0 = a["p"][:, 0].rearrange("p b h k -> p (b h k)")
                vec.scalar_tensor_tensor(p0, a["p"][:, 1].rearrange("p b h k -> p (b h k)"), lam[:, 2:3], p0,
                                         ALU.mult, ALU.add).then_inc(*served())
                take_turned(a["pT"].rearrange("p h k t -> p (h k) t")[:, 0:4, :], 4)
                from_psum()
                o, osq = (a[w].rearrange("p b h v -> p (b h) v") for w in ("o", "osq"))
                vec.tensor_copy(o, ps(0, 2).rearrange("p (r v) -> p r v", v=P)).then_inc(*own.next())
                done()
                vec.tensor_tensor(osq, o, o, ALU.mult).then_inc(*own.next())
                done()
                vec.tensor_reduce(sum8, osq, AX, ALU.add).then_inc(*own.next())
                done()
                rooted(sum8, 1.0 / P, RMS_EPS)
                vec.tensor_tensor(o, o, bcast(sum8, 2, P), ALU.mult).then_inc(*own.next())
                done()
                vec.scalar_tensor_tensor(o, o, 1.0 - LAMBDA_INIT, bcast(misc[:, 0:P], 1, 8), ALU.mult, ALU.mult).then_inc(*served())
                add_stream("mix_out", 4)

            def vec_cross(a, phase):
                vec.wait_ge(params_loaded, loads[phase])
                rms_stream(a["mem"], a["mn"], a["norm"][:, 0, :], phase)
                rms_stream(h, a["hn"], a["norm"][:, 1, :], phase)
                take_matrix(hT, 4)

                def head_norm(key, b0, dst, gain):
                    panel_done(key)
                    ahead = {"xa_wk_2": "xa_wv_2"}.get(key, key)
                    d8, s8 = (v.rearrange("p b (h e) -> p (b h) e", h=XH) for v in (dst, a["sq"]))
                    vec.tensor_copy(d8, ps(b0, 4).rearrange("p (r e) -> p r e", e=XD)).then_inc(*own.next())
                    more(1, ahead)
                    done()
                    vec.tensor_tensor(s8, d8, d8, ALU.mult).then_inc(*own.next())
                    more(1, ahead)
                    done()
                    vec.tensor_reduce(sum8, s8, AX, ALU.add).then_inc(*own.next())
                    done()
                    rooted(sum8, 1.0 / XD, RMS_EPS)
                    vec.tensor_tensor(d8, d8, bcast(sum8, 2, XD), ALU.mult).then_inc(*own.next())
                    more(1, ahead)
                    done()
                    vec.tensor_tensor(d8, d8, bcast(gain, 1, 8), ALU.mult).then_inc(*served())

                head_norm("xa_wk_2", 0, a["k"], a["gain"][:, 0, :])
                split_to(end["xa_wv_2"] + SPLIT)
                take_turned(a["kT"][:, 0:4, :], 0)
                take_matrix(hT)
                head_norm("xa_wq_2", 4, a["q"], a["gain"][:, 1, :])
                take_turned(a["qT"][:, 0:4, :], 0)
                from_psum()
                softmax(ps(4, 4).rearrange("p (r k) -> p r k", k=T), a["p"], top8, sum8, served)
                take_turned(a["pT"].rearrange("p h k t -> p (h k) t")[:, 0:4, :], 0)
                from_psum()
                take_split(hT[:, 0], hT[:, 1], 4, 4)
                add_stream("xa_wo_2", 0)

            def vec_ffn(a):
                for n in range(6):
                    b0, w = 4 * ((n + 1) % 2), min(4, FF_TILES - 4 * n)
                    panel_done(f"up{n}")
                    ahead = f"up{min(n + 1, 5)}"
                    v = ps(b0, 4).rearrange("p (i t) -> p i t", t=T)
                    c = a["conv"][:, n % 2]
                    for i in range(w):
                        f = 4 * n + i
                        vec.tensor_scalar(c[:, i, :], v[:, i, :], a["taps"][:, 2, f:f + 1], a["bias"][:, f:f + 1],
                                          ALU.mult, ALU.add).then_inc(*own.next())
                    done()
                    for tap in (1, 0):
                        back = 2 - tap
                        for i in range(w):
                            f = 4 * n + i
                            vec.scalar_tensor_tensor(c[:, i, back:], v[:, i, 0:T - back], a["taps"][:, tap, f:f + 1],
                                                     c[:, i, back:], ALU.mult, ALU.add).then_inc(
                                *(own.mark(vec_for_act) if tap == 0 and i == w - 1 else own.next()))
                        more(1, ahead)
                        done()
                    vec.wait_ge(act_for_vec, from_act.up())
                    vec.tensor_tensor(a["hid"][:, 4 * n:4 * n + w, :], c[:, 0:w, :], v[:, w:2 * w, :], ALU.mult).then_inc(*served())
                done()
                feed("down", a["hid"])
                add_stream("down", 4)

            def vec_peer(a, phase):
                first_u, first_v, d0 = begin[phase + "_u"], begin[phase + "_v"], experts_before[phase]
                for n in range(2):
                    panel_done(f"{phase}_q{n}")
                    vec.tensor_copy(a["qT"][:, 8 * n:8 * n + 8, :].rearrange("p a b -> p (a b)"), ps(4 * (1 - n), 4)).then_inc(*served())

                def due():
                    split_to(min(n_split.n + 1, first_u + NK // 2))

                def top_sixteen(n, src, spare, val, idx):
                    for i in range(n):
                        vec.max(val(i)[:, 0:8], src(i)).then_inc(*own.next())
                        if i % 4 == 3:
                            due()
                    done()
                    for i in range(n):
                        vec.max_index(idx(i)[:, 0:8], val(i)[:, 0:8], src(i)).then_inc(*own.next())
                        if i % 4 == 3:
                            due()
                    for i in range(n):
                        vec.match_replace(spare(i), val(i)[:, 0:8], src(i), LOWEST).then_inc(*own.next())
                        if i % 4 == 3:
                            due()
                    done()
                    for i in range(n):
                        vec.max(val(i)[:, 8:16], spare(i)).then_inc(*own.next())
                        if i % 4 == 3:
                            due()
                    done()
                    for i in range(n):
                        vec.max_index(idx(i)[:, 8:16], val(i)[:, 8:16], spare(i)).then_inc(*own.next())
                        if i % 4 == 3:
                            due()
                    done()

                split_to(end[phase + "_keys"] + SPLIT)
                vec.wait_ge(act_for_vec, from_act.up())
                for tb in range(TB):
                    s, s2, val, idx = a["s"][:, tb], a["s2"], a["val"], a["idx"].bitcast(U32)
                    top_sixteen(HC, lambda i: s[:, i, :], lambda i: s2[:, i, :], lambda i: val[:, i, :], lambda i: idx[:, i, :])
                    idxf = a["idxf"]
                    vec.tensor_copy(idxf, idx).then_inc(*own.next())
                    v1 = val.rearrange("p (h c) k -> p h c k", c=2)
                    cand, cand2 = a["cand"], a["cand2"]
                    c4 = cand.rearrange("p h (a b) -> p h a b", a=TOPK)
                    for hd in range(PH):
                        vec.tensor_tensor(c4[:, hd], bcast(v1[:, hd, 0, :], 2, TOPK), bcast(v1[:, hd, 1, :], 1, TOPK),
                                          ALU.add).then_inc(*own.next())
                    due()
                    done()
                    top, pos = a["top"], a["pos"].bitcast(U32)
                    top_sixteen(PH, lambda i: cand[:, i, :], lambda i: cand2[:, i, :], lambda i: top[:, i, :], lambda i: pos[:, i, :])
                    ab = a["ab"].bitcast(U32)
                    vec.tensor_scalar(ab[:, 0], pos, 4, None, ALU.logical_shift_right).then_inc(*own.next())
                    vec.tensor_scalar(ab[:, 1], pos, 15, None, ALU.bitwise_and).then_inc(*own.next())
                    due()
                    done()
                    abf = a["abf"]
                    vec.tensor_copy(abf, ab).then_inc(*own.next())
                    done()
                    i1 = idxf.rearrange("p (h c) k -> p h c k", c=2)
                    sel = a["sel"]
                    for w in range(2):
                        for hd in range(PH):
                            vec.tensor_tensor(sel[:, hd], bcast(abf[:, w, hd, :], 2, TOPK), bcast(iota[:, 0:TOPK], 1, TOPK),
                                              ALU.is_equal).then_inc(*own.next())
                        due()
                        done()
                        for hd in range(PH):
                            vec.tensor_tensor(sel[:, hd], sel[:, hd], bcast(i1[:, hd, w, :], 1, TOPK), ALU.mult).then_inc(*own.next())
                        due()
                        done()
                        vec.tensor_reduce(a["ijg"][:, w, tb], sel, AX, ALU.add).then_inc(*own.next())
                        due()
                        done()
                    vec.tensor_tensor(a["ijg"][:, 2, tb], top, top[:, :, 0:1].broadcast_to([P, PH, TOPK]), ALU.subtract).then_inc(
                        *(own.mark(vec_for_act) if tb == TB - 1 else own.next()))
                    done()
                split_to(first_u + NK // 2)
                gate, den = a["ijg"][:, 2].rearrange("p b h k -> p (b h) k"), a["den"].rearrange("p b h -> p (b h)")
                vec.wait_ge(act_for_vec, from_act.up())
                vec.tensor_reduce(den, gate, AX, ALU.add).then_inc(*own.next())
                done()
                vec.reciprocal(den, den).then_inc(*own.next())
                done()
                vec.tensor_tensor(gate, gate, bcast(den, 2, TOPK), ALU.mult).then_inc(*own.mark(vec_for_pe))
                with vec.Fori(NK // 2 // RING, NK // RING) as it:
                    for r in range(RING):
                        n = first_u + r
                        split_chunk(n % RING, n % SPLIT, it * 16 + 16 * (n // RING + 1), it * RING + (n - 1),
                                    it * RING + split_count[n])
                n_split.n = first_v
                own.last = (chunk_split, split_count[first_v - 1])
                split_to(first_v + SPLIT)
                vec.wait_ge(psum_for_vec, psum_v.up())
                vec.tensor_copy(routes.rearrange("p a b -> p (a b)"), ps(0, 2)[:, 0:3 * T]).then_inc(*served())
                done()
                vec.tensor_copy(misc[:, 509:510], iota[:, 0:1]).then_inc(*own.mark(routes_ready))

                A_, _ = onehot_views()
                base, G = gates_before[phase], a["G"]

                def onehots(g, half):
                    for q in range(4):
                        i = vec.tensor_scalar(A_[:, half, q, :], iota, routes[:, 0, bass.ds(g * 4 + q, 1)],
                                              routes[:, 2, bass.ds(g * 4 + q, 1)], ALU.is_equal, ALU.mult)
                    i.then_inc(onehots_made, 1)

                def place(g, half):
                    vec.wait_ge(onehots_used, g + (base + 1))
                    v = G[:, :, bass.ds(g * 4, 4)].rearrange("p i q -> p q i")
                    vec.tensor_tensor(v, ps(2 + half, 1).rearrange("p (q i) -> p q i", q=4), v, ALU.mult).then_inc(gates_placed, 1)

                onehots(0, 0)
                onehots(1, 1)
                vec.wait_ge(gelu_done, d0 + NK)
                with vec.Fori(0, T // 8 - 1) as it:
                    for half in range(2):
                        place(it * 2 + half, half)
                        onehots(it * 2 + half + 2, half)
                for half in range(2):
                    place(T // 4 - 2 + half, half)
                vec.wait_ge(gates_placed, base + T // 4)

                def weigh(tile, i, buf):
                    w = G[:, bass.ds(tile, 1), :].rearrange("p o t -> p (o t)")
                    round_to(tile_w[:, buf, 0, :], w).then_inc(weights_hi, 1)
                    vec.wait_ge(weights_hi, i + 1)
                    vec.tensor_tensor(tile_w[:, buf, 1, :], w, tile_w[:, buf, 0, :].bitcast(F32), ALU.subtract).then_inc(weights_ready, 1)

                vec.wait_ge(onehots_used, base + T // 4)
                weigh(0, d0, 0)
                weigh(1, d0 + 1, 1)
                with vec.Fori(0, NK // RING - 1) as it:
                    for r in range(RING):
                        vec.wait_ge(chunks_done, it * RING + (first_v + r + 1))
                        weigh(it * RING + (r + 2), it * RING + (d0 + r + 2), r % 2)
                        n = first_v + r + 2
                        split_chunk(n % RING, n % SPLIT, it * 16 + 16 * (n // RING + 1), it * RING + (n - 1),
                                    it * RING + split_count[n])
                n_split.n = first_v + NK - SPLIT
                for i in range(NK - RING, NK - 2):
                    vec.wait_ge(chunks_done, first_v + i + 1)
                    weigh(i + 2, d0 + i + 2, i % 2)
                    split_to(first_v + i + 3)
                own.last = (weights_ready, d0 + NK)
                ln_stream(phase + "_v", 0, phase)

            vec.wait_ge(input_loaded, 64)
            for n, phase in enumerate(phases):
                if phase in ("mixers", "ffn"):
                    rms_stream(h, A[phase]["hn"], A[phase]["norm"][:, 0, :], phase)
                if phase != "cross":
                    take_matrix(hT)
                if phase == "retention":
                    vec_retention(A[phase], phase)
                if phase == "mla":
                    vec_mla(A[phase], phase)
                if phase == "mixers":
                    vec_mixers(A[phase])
                if phase == "cross":
                    vec_cross(A[phase], phase)
                if phase == "ffn":
                    vec_ffn(A[phase])
                if phase.startswith("peer"):
                    vec_peer(A[phase], phase)

        @block.scalar
        def _(act):
            own = Last(act_step)
            psum_a, from_vec = Count(), Count()

            def done():
                act.wait_ge(*own.last)

            for dst, src in [(h[:, tb, :], x["x"][0, tb * P:(tb + 1) * P, :]) for tb in range(TB)] \
                    + [(ident, x["c_ident"]), (iota, x["c_iota"])]:
                act.dma_start(dst, src).then_inc(input_loaded, 16)

            def load_params(phase):
                for dst, src in params.get(phase, []):
                    act.dma_start(dst, src).then_inc(params_loaded, 16)

            def copy_turned(dst, b0, nb=2):
                act.wait_ge(psum_for_act, psum_a.up())
                act.activation(dst.rearrange("p a b -> p (a b)"), ps(b0, nb), ACT.Copy).then_inc(*own.mark(act_served))

            def root(v):
                act.wait_ge(vec_for_act, from_vec.up())
                act.activation(v, v, ACT.Sqrt).then_inc(*own.mark(act_for_vec))

            def act_retention(a):
                lg = a["lg"]
                act.activation(lg, lg, ACT.Exp).then_inc(*own.next())
                done()
                act.activation(lg, lg, ACT.Ln, scale=-1.0, bias=1.0).then_inc(*own.mark(act_for_vec))
                act.wait_ge(vec_for_act, from_vec.up())
                act.activation(a["cos"], a["cos"], ACT.Sin).then_inc(*own.next())
                act.activation(a["sin"], a["sin"], ACT.Sin).then_inc(*own.next())
                act.wait_ge(vec_for_act, from_vec.up())
                dec = a["decay"].rearrange("p a b -> p (a b)")
                act.activation(dec, dec, ACT.Exp).then_inc(*own.mark(act_for_vec))
                for n in range(4):
                    b0 = 4 * ((n + 3) % 2)
                    act.wait_ge(chunks_done, end[f"ret_in{n + 2}"])
                    dst = (a["v"], a["g"])[n // 2][:, :, (n % 2) * 1024:(n % 2 + 1) * 1024]
                    for tb in range(TB):
                        i = act.activation(dst[:, tb, :], ps(b0 + 2 * tb, 2), ACT.Copy if n < 2 else ACT.Silu)
                        i.then_inc(*(own.mark(act_served) if tb else own.next()))
                root(rstd[:, 0:4])
                root(rstd[:, 4:8])
                root(rstd[:, 0:TB])

            def in_place(v, func, **kw):
                act.wait_ge(vec_for_act, from_vec.up())
                act.activation(v, v, func, **kw).then_inc(*own.mark(act_for_vec))

            def tell_vec():
                done()
                act.activation(misc[:, 508:509], iota[:, 0:1], ACT.Copy).then_inc(*own.mark(act_for_vec))

            def rows8(p):
                return p.rearrange("p b h k -> p (b h k)")

            def turned_p(pT, b0):
                copy_turned(pT.rearrange("p h k t -> p (h k) t")[:, 4:8, :], b0)

            def act_mla(a):
                act.wait_ge(vec_for_act, from_vec.up())
                act.activation(a["cos"], a["cos"], ACT.Sin).then_inc(*own.next())
                act.activation(a["sin"], a["sin"], ACT.Sin).then_inc(*own.mark(act_for_vec))
                root(rstd[:, 0:4])
                for key, dst in (("mla_uq", "qnT"), ("mla_ukv", "knT")):
                    for n in range(2):
                        act.wait_ge(chunks_done, end[f"{key}{n}"])
                        act.activation(a[dst][:, 4 * n:4 * n + 4, :].rearrange("p a b -> p (a b)"), ps(4 * (1 - n), 2),
                                       ACT.Copy).then_inc(*own.mark(act_served))
                act.wait_ge(psum_for_act, psum_a.up())
                act.activation(a["qrT"].rearrange("p a b -> p (a b)"), ps(4, 4, ROPE), ACT.Copy).then_inc(*own.mark(act_served))
                for n in range(2):
                    in_place(rows8(a["p"]), ACT.Exp, scale=MLA_SCALE)
                    turned_p(a["pT"], 6)
                root(rstd[:, 0:TB])

            def act_mixers(a):
                def flat(v):
                    return v.rearrange("p a b -> p (a b)")

                for n in range(4):
                    b0 = 4 * ((n + 1) % 2)
                    act.wait_ge(chunks_done, end[f"slots{n}"])
                    src = ps(b0, 2).rearrange("p (s t) -> p s t", t=T)
                    dst = a["z"][:, 8 * n:8 * n + 8, 1:T + 1] if n < 2 else a["qk"][:, n - 2]
                    for side in range(2):
                        act.activation(dst.rearrange("p (s two) t -> p s two t", two=2)[:, :, side, :],
                                       src[side * C:(side + 1) * C], ACT.Copy).then_inc(*(own.mark(act_served) if side else own.next()))
                    if n == 1:
                        tell_vec()
                for key, b0, c in (("diff_v", 4, slice(POOL_W, POOL_W + DIFF_W)), ("pool_in", 0, slice(0, POOL_W))):
                    act.wait_ge(chunks_done, end[key])
                    act.activation(a["pv"][:, :, c], ps(b0, 4).rearrange("p (b c) -> p b c", b=TB)[:, :, 0:c.stop - c.start],
                                   ACT.Copy).then_inc(*own.mark(act_served))
                act.wait_ge(vec_for_act, from_vec.up())
                act.activation(a["zm"][:, 12, :], a["zm"][:, 12, :], ACT.Tanh).then_inc(*own.next())
                act.activation(a["zm"][:, 14:16, :], a["zm"][:, 14:16, :], ACT.Sigmoid).then_inc(*own.mark(act_for_pe))
                act.wait_ge(psum_for_act, psum_a.up())
                for w, dst in enumerate(("lw", "a")):
                    for hd in range(NH):
                        act.activation(a[dst][:, hd, :], ps(2 * w + hd // 2, 1, C)[:, (hd % 2) * T:(hd % 2 + 1) * T],
                                       ACT.Sigmoid, bias=a["cols"][:, w, hd:hd + 1]).then_inc(*own.next())
                act.activation(flat(a["g"]), ps(4, 2, C), ACT.Copy).then_inc(*own.mark(act_served))
                tell_vec()
                act.wait_ge(vec_for_act, from_vec.up())
                act.activation(flat(a["Pd"]), flat(a["L"]), ACT.Exp).then_inc(*own.next())
                act.activation(flat(a["Pi"]), flat(a["L"]), ACT.Exp, scale=-1.0).then_inc(*own.next())
                act.activation(flat(a["Pp"]), flat(a["Pp"]), ACT.Exp).then_inc(*own.mark(act_for_vec))
                act.wait_ge(psum_for_act, psum_a.up())
                act.activation(flat(a["kk2"]), ps(6, 2, C), ACT.Sqrt).then_inc(*own.mark(act_served))
                tell_vec()
                act.wait_ge(psum_for_act, psum_a.up())
                act.activation(a["tm"][:, 0:2].rearrange("p w u c -> p (w u c)"), ps(0, 4, C), ACT.Copy).then_inc(*own.mark(act_served))
                for dst, b0 in (("AkV", 0), ("U0", 6), ("X", 4)):
                    act.wait_ge(psum_for_act, psum_a.up())
                    if dst == "AkV":
                        act.dma_start(a["alibi"].rearrange("p a b c -> p (a b c)"), x["c_alibi"]).then_inc(alibi_loaded, 16)
                    act.activation(flat(a[dst]), ps(b0, 2, C), ACT.Copy).then_inc(*own.mark(act_served))
                root(misc[0:C, 288:304])
                act.wait_ge(psum_for_act, psum_a.up())
                act.activation(flat(a["rT"]), ps(6, 2, C), ACT.Copy).then_inc(*own.mark(act_served))
                sq, qk = (a[w].rearrange("p w s t -> p (w s t)") for w in ("sq", "qk"))
                act.activation(sq, qk, ACT.Square).then_inc(*own.mark(act_for_pe))
                in_place(a["lam"][:, 0:2], ACT.Exp)
                root(a["rs"].rearrange("p w s t -> p (w s t)"))
                for c in range(2):
                    in_place(rows8(a["p"][:, c]), ACT.Exp)
                turned_p(a["pT"], 6)
                root(sum8_)
                copy_turned(a["oT"], 2)

            sum8_ = misc[:, 264:272]

            def act_cross(a):
                root(rstd[:, 0:TB])
                root(rstd[:, 0:TB])
                root(sum8_)
                act.wait_ge(chunks_done, end["xa_wv_2"])
                act.activation(a["v"].rearrange("p a b -> p (a b)"), ps(4, 4), ACT.Copy).then_inc(*own.mark(act_served))
                copy_turned(a["kT"][:, 4:8, :], 2)
                root(sum8_)
                copy_turned(a["qT"][:, 4:8, :], 2)
                in_place(rows8(a["p"]), ACT.Exp, scale=XD ** -0.5)
                turned_p(a["pT"], 2)

            def act_ffn(a):
                for n in range(6):
                    w = min(4, FF_TILES - 4 * n)
                    in_place(a["conv"][:, n % 2, 0:w, :].rearrange("p a b -> p (a b)"), ACT.Gelu)

            def act_peer(a, phase):
                first_u, d0 = begin[phase + "_u"], experts_before[phase]
                act.wait_ge(chunks_done, end[phase + "_keys"])
                for tb in range(TB):
                    act.activation(a["s"][:, tb].rearrange("p a b -> p (a b)"), ps(4 * tb, 4), ACT.Copy).then_inc(
                        *(own.mark(act_served) if tb else own.next()))
                tell_vec()

                def gelu(tile, buf):
                    act.wait_ge(chunks_done, tile + (first_u + 1))
                    act.activation(a["G"][:, bass.ds(tile, 1), :].rearrange("p o t -> p (o t)"), ps(6 + buf, 1)[:, 0:T],
                                   ACT.Gelu).then_inc(gelu_done, 1)

                with act.Fori(0, NK // 2 // RING) as it:
                    for r in range(RING):
                        gelu(it * RING + r, r % 2)
                in_place(a["ijg"][:, 2].rearrange("p b h k -> p (b h k)"), ACT.Exp)
                with act.Fori(NK // 2 // RING, NK // RING) as it:
                    for r in range(RING):
                        gelu(it * RING + r, r % 2)
                _, B_ = onehot_views()
                base = gates_before[phase]

                def j_group(g, half, fresh):
                    v = less_j[:, half].rearrange("p q n -> p (q n)")
                    act.wait_ge(j_less, g + (base + 1))
                    act.activation(v, v, ACT.Abs).then_inc(j_apart, 1)
                    if not fresh:
                        act.wait_ge(onehots_used, g + (base - 1))
                    act.wait_ge(j_apart, g + (base + 1))
                    act.activation(B_[:, half].rearrange("p q n -> p (q n)"), v, ACT.Relu, scale=-1.0, bias=1.0).then_inc(j_onehots, 1)

                j_group(0, 0, True)
                j_group(1, 1, True)
                with act.Fori(1, T // 8) as it:
                    for half in range(2):
                        j_group(it * 2 + half, half, False)
                act.wait_ge(weights_ready, d0 + NK)
                load_params(phase)
                root(rstd[:, 0:TB])

            for n, phase in enumerate(phases):
                if n:
                    act.wait_ge(phase_done, n)
                if not phase.startswith("peer"):
                    load_params(phase)
                    if phase in ("retention", "mixers", "cross", "ffn"):
                        act.wait_ge(params_loaded, loads[phase])
                if phase in ("mixers", "ffn"):
                    root(rstd[:, 0:TB])
                if phase == "retention":
                    act_retention(A[phase])
                if phase == "mla":
                    act_mla(A[phase])
                if phase == "mixers":
                    act_mixers(A[phase])
                if phase == "cross":
                    act_cross(A[phase])
                if phase == "ffn":
                    act_ffn(A[phase])
                if phase.startswith("peer"):
                    act_peer(A[phase], phase)


def kernel(**inputs):
    import numpy as _np
    import concourse.bacc as _bacc
    from concourse import mybir as _mybir
    from concourse.bass_utils import run_bass_kernel_spmd as _run

    nc = _bacc.Bacc("TRN2", target_bir_lowering=False, num_devices=1)
    arrays, x = {}, {}
    for name, value in {**inputs, **constants(), **columns(inputs), **turned(inputs)}.items():
        if name in ("peer_u", "peer_sub_keys"):
            continue
        a = _np.ascontiguousarray(value)
        arrays[f"in_{name}"] = a
        x[name] = nc.dram_tensor(f"in_{name}", a.shape, _mybir.dt.from_np(a.dtype), kind="ExternalInput").ap()
    out = nc.dram_tensor("out", (1, T, D), F32, kind="ExternalOutput").ap()
    build(nc, x, out)
    return _run(nc, [arrays], core_ids=[0]).results[0]["out"]
```

```python
from contextlib import ExitStack

import numpy as np

import concourse.bass as bass
from concourse import mybir

F32 = mybir.dt.float32
F32R = mybir.dt.float32r
I32 = mybir.dt.int32
U32 = mybir.dt.uint32
ALU = mybir.AluOpType
ACT = mybir.ActivationFunctionType
AX = mybir.AxisListType.X

P = 128
T = 256
TB = T // P
D = 1024
KD = D // P
BANK = 512
RING = 4
SPLIT = 2
BY_VEC = 704
SLOT = 1024
ALPHA = 4.0 ** 0.25
LN_EPS = 1e-5
RMS_EPS = 1e-6

RET_HEADS, RET_DK, RET_DV = 4, 256, 512
RET_HV = RET_HEADS * RET_DV

MLA_HEADS, NOPE, ROPE, VDIM = 8, 128, 64, 128
Q_RANK, KV_RANK = 384, 256
MLA_IN = Q_RANK + KV_RANK + ROPE
MLA_SCALE = float((NOPE + ROPE) ** -0.5)

PH, NK, TOPK = 8, 128, 16
HC = 2 * PH
HALF = NK // 2
GROUPS = T // 4

POOL_W, RWKV_W, DIFF_W = 256, 256, 512
POOL_WINDOWS = (2, 4, 8, 16)
C = 64
NC_ = T // C
NH = 4
UN = NC_ * NH
LEVELS = 6
RWKV_EPS = 64e-5
LAMBDA_INIT = 0.2
XH, XD = 4, 256
D_FF = 2816
FF_TILES = D_FF // P

TWO_PI_HI = 6.28125
TWO_PI_LO = float(2 * np.pi - 6.28125)
ROUND = 12582912.0
PI_IN = 3.1415925
LOWEST = -3.0e38

WHOLE = ("peer0_keys", "peer1_keys")

PHASES = ("retention", "peer0", "mla", "peer1", "mixers", "cross", "ffn")


def rows(name, layer, k_tiles, c0, cols):
    return [(name, layer, k * P, P, ((c0, cols),)) for k in range(k_tiles)]


def weight_plan(phases):
    plan = []
    for phase in phases:
        if phase == "retention":
            for n in range(6):
                plan.append((f"ret_in{n}", rows("ret_w_in", 0, KD, n * 1024, 1024)))
            plan.append(("ret_out", rows("ret_w_out", 0, RET_HV // P, 0, D)))
        if phase.startswith("peer"):
            l = int(phase[-1])
            for n in range(2):
                plan.append((f"{phase}_q{n}", rows("peer_w_q", l, KD, n * 1024, 1024)))
            plan.append((phase + "_keys", [("keys_turned", l, n, P, ((0, 1024),)) for n in range(2)]))
            plan.append((phase + "_u", [("u_turned", l, n, P, ((0, 1024),)) for n in range(NK)]))
            plan.append((phase + "_v", [("peer_v", l, n, P, ((0, 1024),)) for n in range(NK)]))
        if phase == "mla":
            plan.append(("mla_in", rows("mla_w_in", 0, KD, 0, MLA_IN)))
            for n in range(2):
                plan.append((f"mla_uq{n}", rows("mla_w_uq", 0, Q_RANK // P, n * 768, 768)))
            for n in range(2):
                plan.append((f"mla_ukv{n}", rows("mla_w_ukv", 0, KV_RANK // P, n * 1024, 1024)))
            plan.append(("mla_out", rows("mla_w_out", 0, MLA_HEADS, 0, D)))
        if phase == "mixers":
            for n in range(4):
                plan.append((f"slots{n}", rows("w_in_2", 0, KD, POOL_W + n * 512, 512)))
            plan.append(("diff_v", rows("w_in_2", 0, KD, POOL_W + 2048, DIFF_W)))
            plan.append(("pool_in", rows("w_in_2", 0, KD, 0, POOL_W)))
            plan.append(("mix_out", rows("w_out_2", 0, KD, 0, D)))
        if phase == "cross":
            for n, w in enumerate(("xa_wk_2", "xa_wv_2", "xa_wq_2", "xa_wo_2")):
                plan.append((w, rows(w, 0, KD, 0, D)))
        if phase == "ffn":
            for n in range(6):
                w = min(4, FF_TILES - 4 * n) * P
                plan.append((f"up{n}", [("ffn_w_up_2", 0, k * P, P, ((n * 512, w), (D_FF + n * 512, w)))
                                        for k in range(KD)]))
            plan.append(("down", rows("ffn_w_down_2", 0, FF_TILES, 0, D)))
    return plan


def constants():
    out = {}
    out["c_ident"] = np.eye(P, dtype=np.float32)
    out["c_iota"] = np.tile(np.arange(P, dtype=np.float32), (P, 1))
    f = (np.float32(10000.0) ** (-np.arange(0, RET_DK, 2, dtype=np.float32) / np.float32(RET_DK))).astype(np.float32)
    out["c_ret_freq"] = f[:, None].copy()
    f = (np.float32(10000.0) ** (-np.arange(0, ROPE, 2, dtype=np.float32) / np.float32(ROPE))).astype(np.float32)
    out["c_mla_freq"] = np.tile(f, (P, 1))
    m = np.arange(T).reshape(TB, P).T[:, :, None]
    n = np.arange(T)[None, None, :]
    d = (n - m).astype(np.float32)
    out["c_ahead"] = np.stack([np.maximum(d, 0), np.maximum(-d, 0)], 1).reshape(P, 2 * TB * T)
    slopes = 2.0 ** (-8.0 * (np.arange(4) + 1) / 4)
    seen = (n // C) <= (m // C)
    bias = np.where(seen[:, :, None, :], -slopes[None, None, :, None] * np.abs(d)[:, :, None, :], LOWEST)
    out["c_alibi"] = bias.astype(np.float32).reshape(P, TB * 4 * T)
    pool = np.zeros((P, TB, 4, T), np.float32)
    for g, w in enumerate(POOL_WINDOWS):
        count = np.minimum(n + 1, w)
        pool[:, :, g, :] = ((m <= n) & (m > n - w)) / count - (m == n)
    out["c_pool"] = pool.reshape(P, TB * 4 * T)
    s, t = np.arange(C)[:, None], np.arange(C)[None, :]
    before = np.concatenate([s < t, s <= t], 1).astype(np.float32)
    levels = [((s < t) & (s >> (b + 1) == t >> (b + 1)) & (s >> b != t >> b)) for b in range(LEVELS)]
    reset = np.tile((np.arange(T) % C != 0).astype(np.float32), (C, NH))
    out["c_rwkv"] = np.concatenate([before] + [x.astype(np.float32) for x in levels] + [reset], 1)
    return {k: np.ascontiguousarray(v, dtype=np.float32) for k, v in out.items()}


def columns(x):
    def cols(v, p):
        return np.asarray(v).reshape(-1, p).T

    rwkv = [cols(x[n], C) for n in ("rwkv_mu_2", "rwkv_w0_2", "rwkv_a0_2", "rwkv_k_k_2", "rwkv_k_a_2", "rwkv_r_k_2",
                                    "diff_q_norm_2", "diff_k_norm_2")]
    return {"pool_scale_cols": np.ascontiguousarray(cols(x["pool_scale_2"], P)),
            "positions_cols": np.ascontiguousarray(cols(x["positions"], P)),
            "channel_cols": np.ascontiguousarray(np.concatenate(rwkv, 1)),
            "conv_cols": np.ascontiguousarray(np.concatenate([cols(x["ffn_conv_w_2"], P), cols(x["ffn_conv_b_2"], P)], 1))}


def turned(x):
    u = np.asarray(x["peer_u"]).reshape(-1, NK, NK, KD, P)
    keys = np.asarray(x["peer_sub_keys"]).reshape(-1, 2, PH, NK, P)
    return {"u_turned": np.ascontiguousarray(u.transpose(0, 1, 4, 3, 2)),
            "keys_turned": np.ascontiguousarray(keys.transpose(0, 1, 4, 2, 3))}


class Count:

    def __init__(self, n=0):
        self.n = n

    def up(self, by=1):
        self.n = self.n + by
        return self.n


class Last:

    def __init__(self, step):
        self.step, self.counts, self.last = step, {}, None

    def next(self):
        return self.mark(self.step)

    def mark(self, sem, by=1):
        n = self.counts.setdefault(id(sem), Count())
        self.last = (sem, n.up(by))
        return sem, by

    def set(self, sem, n):
        self.counts[id(sem)] = Count(n)
        self.last = (sem, n)


class Banks:

    def __init__(self, served):
        self.served = served
        self.lent = {who: Count() for who in served}
        self.of = {}

    def lend(self, banks, who):
        n = self.lent[who].up()
        for b in banks:
            self.of[b] = (self.served[who], n)
        return self.served[who], n


class Memory:

    def __init__(self, base, start, size):
        self.base, self.at, self.end = base, start, start + size

    def take(self, *dims, parts=P):
        n = int(np.prod(dims))
        assert self.at + n <= self.end, ("SBUF", dims, self.at, self.end)
        v = self.base[0:parts, self.at:self.at + n]
        self.at += n
        if len(dims) == 1:
            return v
        names = "abcde"[:len(dims)]
        return v.rearrange(f"p ({' '.join(names)}) -> p {' '.join(names)}", **dict(zip(names, dims)))


def bcast(ap, axis, n):
    v = ap.unsqueeze(axis)
    return v.broadcast_to([*v.shape[:axis], n, *v.shape[axis + 1:]])


def build(nc, x, out, phases=PHASES):
    ctx = ExitStack()
    with ctx:
        def sem(name):
            return ctx.enter_context(nc.semaphore(name))

        ARENA = 32768
        LASTING = TB * D + 2 * P + RING * SLOT + 3072 + 3 * T + 640
        sb = ctx.enter_context(nc.sbuf_tensor("sb", [P, LASTING + ARENA], F32))
        lasting = Memory(sb, 0, LASTING)
        h = lasting.take(TB, D)
        ident = lasting.take(P)
        iota = lasting.take(P)
        ring = lasting.take(RING, SLOT)
        pair_at = lasting.at
        pair = lasting.take(3072)
        routes_at = lasting.at
        routes = lasting.take(3, T)
        stats = lasting.take(4, 2, 6)
        mv = lasting.take(2, 2)
        var8 = lasting.take(8, 2)
        rstd = lasting.take(16)
        misc = lasting.take(512)

        rounded = ctx.enter_context(nc.sbuf_tensor("rounded", [P, 2 * KD * T + 2 * SPLIT * SLOT + 4 * T], F32R))
        split_parts = Memory(rounded, 0, 2 * KD * T + 2 * SPLIT * SLOT + 4 * T)
        hT = split_parts.take(2, KD, T)
        ring_hi = split_parts.take(SPLIT, SLOT)
        ring_lo = split_parts.take(SPLIT, SLOT)
        tile_w = split_parts.take(2, 2, T)

        def arena():
            return Memory(sb, LASTING, ARENA)

        psum = ctx.enter_context(nc.psum_tensor("psum", [P, 8, BANK], F32))

        def ps(b0, n, parts=P):
            return psum[0:parts, b0:b0 + n, :].rearrange("p a b -> p (a b)")

        ring_loaded = [sem(f"ring_loaded{n}") for n in range(RING)]
        chunks_done = sem("chunks_done")
        psum_for_vec, psum_for_act = sem("psum_for_vec"), sem("psum_for_act")
        vec_served, act_served = sem("vec_served"), sem("act_served")
        vec_for_act, act_for_vec = sem("vec_for_act"), sem("act_for_vec")
        vec_for_pe, act_for_pe = sem("vec_for_pe"), sem("act_for_pe")
        vec_step, act_step = sem("vec_step"), sem("act_step")
        onehots_made, onehots_used = sem("onehots_made"), sem("onehots_used")
        gates_placed, routes_ready = sem("gates_placed"), sem("routes_ready")
        j_less, j_apart, j_onehots = sem("j_less"), sem("j_apart"), sem("j_onehots")
        gelu_done, weights_hi, weights_ready = sem("gelu_done"), sem("weights_hi"), sem("weights_ready")
        chunk_hi, tile_hi, tile_lo, chunk_split = sem("chunk_hi"), sem("tile_hi"), sem("tile_lo"), sem("chunk_split")
        alibi_loaded, norm_loaded = sem("alibi_loaded"), sem("norm_loaded")
        input_loaded, params_loaded, phase_done = sem("input_loaded"), sem("params_loaded"), sem("phase_done")
        stored = sem("stored")

        plan = weight_plan(phases)
        begin, end, n_chunks = {}, {}, 0
        for key, chunks in plan:
            begin[key] = n_chunks
            n_chunks += len(chunks)
            end[key] = n_chunks
        chunk_size = {begin[key] + i: (k, sum(w for _, w in runs))
                      for key, chunks in plan for i, (_, _, _, k, runs) in enumerate(chunks)}
        hi_count, tile_count, split_count = {}, {}, {}
        for key, chunks in plan:
            if key not in WHOLE:
                mine = tile_count if key.startswith("peer") and key.endswith(("_u", "_v")) else hi_count
                for n in range(begin[key], end[key]):
                    split_count[n] = len(split_count) + 1
                    mine[n] = len(mine) + 1

        def whole(name):
            a = x[name]
            dims = "abcdef"[:len(a.shape)]
            return a.rearrange(f"{' '.join(dims)} -> ({' '.join(dims)})")

        params, norms, A = {}, {}, {}

        def param(phase, dst, src):
            params.setdefault(phase, []).append((dst, src))

        def everywhere(ap, parts=P):
            return ap.partition_broadcast(parts)

        def norm_params(phase, place, g, b, l):
            A[phase]["norm"] = place
            norms[phase] = [(place[:, i, :], everywhere(x[name][l])) for i, name in enumerate((g, b)) if name]

        for phase in phases:
            m = arena()
            a = A[phase] = {}
            if phase == "retention":
                a["qT"], a["kT"] = m.take(8, T), m.take(8, T)
                a["v"], a["g"] = m.take(TB, RET_HV), m.take(TB, RET_HV)
                a["y"] = m.take(TB, RET_HV)
                a["decay"] = m.take(4, TB * T)
                a["s"] = m.take(4, TB, T)
                a["tmp"] = m.take(2, 4, T)
                a["gn"] = m.take(2, RET_HV)
                a["ahead"] = m.take(2, TB * T)
                a["cos"], a["sin"] = m.take(T), m.take(T)
                a["posi"], a["ang"], a["turn"] = m.take(T), m.take(T), m.take(T)
                a["lg"] = m.take(8)
                a["freq"] = m.take(1)
                a["yT"] = a["v"].rearrange("p a b -> p (a b)").rearrange("p (k t) -> p k t", t=T)
                param(phase, a["posi"].bitcast(I32), everywhere(x["positions"][0]))
                param(phase, a["freq"], x["c_ret_freq"])
                param(phase, a["ahead"].rearrange("p a b -> p (a b)"), x["c_ahead"])
                param(phase, a["lg"], everywhere(whole("ret_log1m_decay")))
                param(phase, a["gn"][:, 0, :], everywhere(x["ret_gn_g"][0]))
                param(phase, a["gn"][:, 1, :], everywhere(x["ret_gn_b"][0]))
                norm_params(phase, m.take(2, D), "ln_mix_g", "ln_mix_b", 0)
            if phase.startswith("peer"):
                l = int(phase[-1])
                a["G"] = m.take(NK, T)
                up = Memory(sb, LASTING + NK // 2 * T, NK // 2 * T)
                a["s"] = up.take(TB, HC, NK)
                late = Memory(sb, up.at, 8192)
                a["qT"] = up.take(HC, T)
                up.take(8192 - HC * T)
                a["s2"], a["cand"], a["cand2"] = late.take(HC, NK), late.take(PH, TOPK * TOPK), late.take(PH, TOPK * TOPK)
                a["sel"] = late.take(PH, TOPK, TOPK)
                a["val"], a["idx"], a["idxf"] = (up.take(HC, TOPK) for _ in range(3))
                a["top"], a["pos"] = up.take(PH, TOPK), up.take(PH, TOPK)
                a["ab"], a["abf"] = up.take(2, PH, TOPK), up.take(2, PH, TOPK)
                late = Memory(sb, pair_at + 2048, 1024)
                a["ijg"], a["den"] = late.take(3, TB, PH, TOPK), late.take(TB, PH)
                norm_params(phase, arena().take(2, D), "ln_ffn_g", "ln_ffn_b", l)
            if phase == "mla":
                a["c"], a["sq"] = m.take(TB, MLA_IN), m.take(TB, Q_RANK + KV_RANK)
                a["krT"] = m.take(T, parts=ROPE)
                a["qnT"], a["knT"] = m.take(MLA_HEADS, T), m.take(MLA_HEADS, T)
                a["qr"], a["qrT"] = m.take(TB, MLA_HEADS, ROPE), m.take(MLA_HEADS, T, parts=ROPE)
                a["v"] = m.take(TB, MLA_HEADS * VDIM)
                a["p"], a["pT"] = m.take(TB, 4, T), m.take(4, TB, T)
                a["tmp"] = m.take(4, TB * 4 * ROPE // 2)
                a["cos"], a["sin"], a["ang"], a["turn"] = (m.take(TB, ROPE // 2) for _ in range(4))
                a["freq"], a["posi"], a["pos"] = m.take(ROPE // 2), m.take(TB), m.take(TB)
                a["gain"] = m.take(Q_RANK + KV_RANK)
                param(phase, a["freq"], x["c_mla_freq"])
                param(phase, a["posi"].bitcast(I32), x["positions_cols"])
                param(phase, a["gain"][:, 0:Q_RANK], everywhere(x["mla_q_norm"][0]))
                param(phase, a["gain"][:, Q_RANK:], everywhere(x["mla_kv_norm"][0]))
                norm_params(phase, m.take(2, D), "ln_mix_g", "ln_mix_b", 1)
            if phase == "mixers":
                U = (UN, C)
                a["pv"] = m.take(TB, POOL_W + DIFF_W)
                a["qk"] = m.take(2, 8, T, parts=C)
                a["poolT"], a["pool_scale"] = m.take(2, T), m.take(2)
                a["pool_pairs"] = m.take(4, 2, C, parts=C)
                a["g"] = m.take(4, RWKV_W, parts=C)
                late = Memory(sb, m.at, 2048)
                a["alibi"] = m.take(TB, 4, T)
                a["bt"], a["kt"] = late.take(*U, parts=C), late.take(*U, parts=C)
                late = Memory(sb, m.at, 2048)
                a["pool"] = m.take(TB, 4, T)
                a["rk"], a["X"] = late.take(*U, parts=C), late.take(*U, parts=C)
                a["pool_w"] = m.take(4, C, parts=C)
                a["masks"] = m.take(2 * C + LEVELS * C + NH * T, parts=C)
                a["sq"] = Memory(sb, m.at, D).take(2, 2 * T, parts=C)
                a["w2"], a["a2"] = m.take(RWKV_W, parts=C), m.take(RWKV_W, parts=C)
                a["g2"] = m.take(2, RWKV_W, parts=C)
                a["ln"] = m.take(2, RWKV_W, parts=C)
                a["channels"] = m.take(16 + 5 * NH + 4, parts=C)
                a["mu"] = a["channels"][:, 0:16]
                a["cols"] = a["channels"][:, 16:16 + 5 * NH].rearrange("p (i h) -> p i h", h=NH)
                a["qk_gain"] = a["channels"][:, 16 + 5 * NH:].rearrange("p (w c) -> p w c", w=2)
                a["pend"] = m.take(UN, parts=C)
                a["lq"], a["lam"] = m.take(2, 2, C), m.take(8)
                a["ones"] = m.take(C, parts=C)
                late = Memory(sb, m.at, 2048)
                a["hn"] = m.take(TB, D)
                a["kk2"], a["kx"] = late.take(NH, T, parts=C), late.take(NH, T, parts=C)
                a["d"] = a["kk2"]
                late = Memory(sb, late.at - 2048, 2048)
                a["Tm"], a["TmT"] = late.take(*U, parts=C), late.take(*U, parts=C)
                late = Memory(sb, late.at - 2048, 2048)
                a["o"], a["osq"] = late.take(TB, 4, P), late.take(TB, 4, P)
                late = Memory(sb, m.at, 4112)
                a["z"] = m.take(16, T + 1, parts=C)
                a["lw"], a["L"], a["Pd"], a["Pp"] = (late.take(NH, T, parts=C) for _ in range(4))
                late = Memory(sb, late.at - 4096, 4096)
                a["tm"] = late.take(4, *U, parts=C)
                late, zm_at = Memory(sb, m.at, 4096), m.at
                a["zm"] = m.take(16, T, parts=C)
                a["Q"], a["Mt"], a["y"], a["ysq"] = (late.take(*U, parts=C) for _ in range(4))
                a["gated"] = a["ysq"].rearrange("p (c h) v -> p c h v", c=NC_)
                late = Memory(sb, late.at - 4096, 4096)
                a["rs"] = late.take(2, 8, T, parts=C)
                late = Memory(sb, m.at, 2048)
                a["ar"] = m.take(UN, 2, C, parts=C)
                a["pT"] = late.take(4, TB, T)
                late = Memory(sb, m.at, 4096)
                a["mab"], a["mak"] = m.take(UN, 2 * C, parts=C), m.take(UN, 2 * C, parts=C)
                a["p"] = late.take(2, TB, 4, T)
                late = Memory(sb, pair_at, 3072)
                a["Pi"], a["a"], a["kk"] = (late.take(NH, T, parts=C) for _ in range(3))
                late = Memory(sb, late.at - 3072, 3072)
                a["aoff"], a["AkV"], a["G1"] = (late.take(*U, parts=C) for _ in range(3))
                a["U0"] = a["aoff"]
                a["S"] = Memory(sb, routes_at, 768).take(3, NH, C, parts=C)
                norm_params(phase, Memory(sb, zm_at, D).take(1, D), "mix_norm_g_2", None, 0)
                param(phase, a["pool"].rearrange("p a b c -> p (a b c)"), x["c_pool"])
                param(phase, a["masks"], x["c_rwkv"])
                param(phase, a["pool_scale"], x["pool_scale_cols"])
                param(phase, a["pool_w"], x["pool_w_2"][0].rearrange("g c d -> c g d"))
                param(phase, a["w2"], x["rwkv_w2_2"][0])
                param(phase, a["a2"], x["rwkv_a2_2"][0])
                param(phase, a["g2"], x["rwkv_g2_2"][0].rearrange("(s p) c -> p s c", p=C))
                param(phase, a["ln"][:, 0, :], everywhere(x["rwkv_ln_w_2"][0], C))
                param(phase, a["ln"][:, 1, :], everywhere(x["rwkv_ln_b_2"][0], C))
                param(phase, a["channels"], x["channel_cols"])
                for i, name in enumerate(("diff_lq1_2", "diff_lk1_2", "diff_lq2_2", "diff_lk2_2")):
                    param(phase, a["lq"][:, i % 2, i // 2, :], everywhere(x[name][0]))
                param(phase, misc[:, 0:P], everywhere(x["diff_subln_2"][0]))
            if phase == "cross":
                a["mem"], a["mn"], a["hn"] = m.take(TB, D), m.take(TB, D), m.take(TB, D)
                a["k"], a["q"], a["v"], a["sq"] = (m.take(TB, D) for _ in range(4))
                a["kT"], a["qT"] = m.take(KD, T), m.take(KD, T)
                a["p"], a["pT"] = m.take(TB, 4, T), m.take(4, TB, T)
                a["gain"] = m.take(2, XD)
                param(phase, a["mem"], x["mem_2"][0].rearrange("(b p) d -> p b d", p=P))
                a["norm"] = a["v"]
                param(phase, a["norm"][:, 0, :], everywhere(x["mem_norm_g_2"][0]))
                param(phase, a["norm"][:, 1, :], everywhere(x["xa_norm_g_2"][0]))
                param(phase, a["gain"][:, 0, :], everywhere(x["xa_k_norm_2"][0]))
                param(phase, a["gain"][:, 1, :], everywhere(x["xa_q_norm_2"][0]))
            if phase == "ffn":
                a["hn"], a["hid"] = m.take(TB, D), m.take(FF_TILES, T)
                a["conv"] = m.take(2, 4, T)
                a["taps_bias"] = m.take(4 * FF_TILES)
                a["taps"] = a["taps_bias"][:, 0:3 * FF_TILES].rearrange("p (w t) -> p w t", w=3)
                a["bias"] = a["taps_bias"][:, 3 * FF_TILES:]
                norm_params(phase, m.take(1, D), "ffn_norm_g_2", None, 0)
                param(phase, a["taps_bias"], x["conv_cols"])

        gates_before, experts_before = {}, {}
        for n, phase in enumerate(p for p in phases if p.startswith("peer")):
            gates_before[phase], experts_before[phase] = 2 * n * GROUPS, n * NK

        i_onehot = pair[:, 0:1024].rearrange("p (b q n) -> p b q n", b=2, q=4)[:, :, :, 0:HALF]
        j_onehot = pair[:, 1024:2048].rearrange("p (b q n) -> p b q n", b=2, q=4)

        less_j = pair[:, 2048:3072].rearrange("p (b q n) -> p b q n", b=2, q=4)

        block = ctx.enter_context(nc.Block())

        @block.sync
        def _(sync):
            def chunk_source(name, l, r0, k, runs):
                if name in ("keys_turned", "u_turned"):
                    return x[name][l][r0].rearrange("p a b -> p (a b)")
                c0, w = runs[0]
                if len(runs) == 2:
                    return x[name][l][r0:r0 + k, :].rearrange("k (two f) -> k two f", two=2)[:, :, c0:c0 + w]
                return x[name][l][r0:r0 + k, c0:c0 + w]

            def load(n, k, src):
                if n - RING in hi_count:
                    sync.wait_ge(chunk_split, split_count[n - RING])
                elif n >= RING:
                    sync.wait_ge(chunks_done, n - RING + 1)
                cols = src.shape[-1] * (src.shape[1] if len(src.shape) == 3 else 1)
                dst = ring[0:k, n % RING, 0:cols]
                if len(src.shape) == 3:
                    dst = dst.rearrange("p (a b) -> p a b", a=src.shape[1])
                sync.dma_start(dst, src).then_inc(ring_loaded[n % RING], 16)

            n = 0
            for key, chunks in plan:
                if not key.startswith("peer") or not key.endswith(("_u", "_v")):
                    for name, l, r0, k, runs in chunks:
                        load(n, k, chunk_source(name, l, r0, k, runs))
                        n += 1
                    continue
                l = int(key[4])
                if key.endswith("_u"):
                    src = x["u_turned"][l].rearrange("i p k j -> i p (k j)")
                else:
                    src = x["peer_v"][l].rearrange("(i j) d -> i j d", j=NK)
                for r in range(RING):
                    load(n + r, P, src[r])
                with sync.Fori(1, NK // RING) as it:
                    for r in range(RING):
                        sync.wait_ge(chunks_done, it * RING + (n + r - RING + 1))
                        sync.dma_start(ring[:, (n + r) % RING, :], src[it * RING + r]).then_inc(ring_loaded[(n + r) % RING], 16)
                n += NK
            sync.wait_ge(phase_done, len(phases))
            for tb in range(TB):
                sync.dma_start(out[0, tb * P:(tb + 1) * P, :], h[:, tb, :]).then_inc(stored, 16)
            sync.wait_ge(stored, 16 * TB)

        @block.gpsimd
        def _(gp):
            def rest_of_lo(n, further=0):
                gp.wait_ge(tile_hi, further + tile_count[n])
                gp.tensor_tensor(ring_lo[:, n % SPLIT, BY_VEC:], ring[:, n % RING, BY_VEC:],
                                 ring_hi[:, n % SPLIT, BY_VEC:].bitcast(F32), ALU.subtract).then_inc(tile_lo, 1)

            def group(t, g, half, fresh=False):
                if not fresh:
                    gp.wait_ge(j_onehots, g + (base - 1))
                gp.tensor_tensor(less_j[:, half], bcast(iota, 1, 4), bcast(routes[:, 1, bass.ds(t * 4, 4)], 2, P),
                                 ALU.subtract).then_inc(j_less, 1)

            for phase in phases:
                if phase.startswith("peer"):
                    u, v, base = begin[phase + "_u"], begin[phase + "_v"], gates_before[phase]
                    for n in range(u, u + SPLIT):
                        rest_of_lo(n)
                    with gp.Fori(0, HALF // RING) as it:
                        for r in range(RING):
                            rest_of_lo(u + r + SPLIT, it * RING)
                    gp.wait_ge(routes_ready, 1 + base // (2 * GROUPS))
                    group(0, 0, 0, fresh=True)
                    group(1, 1, 1, fresh=True)
                    with gp.Fori(0, HALF // RING - 1) as it:
                        for r in range(RING):
                            group(it * RING + (r + 2), it * RING + (r + 2), r % 2)
                            rest_of_lo(u + HALF + r + SPLIT, it * RING)
                    for k in range(HALF - RING, HALF):
                        group((k + 2) % GROUPS, k + 2, k % 2)
                        rest_of_lo(u + HALF + k + SPLIT)
                    group(2, GROUPS + 2, 0)
                    group(3, GROUPS + 3, 1)
                    with gp.Fori(0, HALF // RING - 1) as it:
                        for r in range(RING):
                            group(it * RING + (r + 4), it * RING + (GROUPS + r + 4), r % 2)
                            rest_of_lo(v + r + SPLIT, it * RING)
                    with gp.Fori(HALF // RING - 1, NK // RING - 1) as it:
                        for r in range(RING):
                            rest_of_lo(v + r + SPLIT, it * RING)
                    for n in range(v + NK - RING + SPLIT, v + NK):
                        rest_of_lo(n)

        loads, norm_loads, at, norms_at = {}, {}, 0, 0
        for phase in phases:
            at += len(params.get(phase, []))
            norms_at += len(norms.get(phase, []))
            loads[phase], norm_loads[phase] = 16 * at, 16 * norms_at

        @block.tensor
        def _(pe):
            banks = Banks({"v": vec_served, "a": act_served})
            to_pe, act_to_pe = Count(), Count()

            def hold(bs):
                for who, served in banks.served.items():
                    owed = [banks.of[b][1] for b in bs if b in banks.of and banks.of[b][0] is served]
                    if owed:
                        pe.wait_ge(served, max(owed))

            def arrived(n):
                if n in split_count:
                    pe.wait_ge(chunk_split, split_count[n])
                else:
                    pe.wait_ge(ring_loaded[n % RING], 16 * (n // RING + 1))

            def parts(n):
                return ring_hi[:, n % SPLIT, :], ring_lo[:, n % SPLIT, :]

            def passes(o, a, b, first, last):
                for i, (p, q) in enumerate(((0, 0), (0, 1), (1, 0))):
                    mm = pe.matmul(o, a[p], b[q], start=(first and i == 0),
                                   stop=(last and i == 2), skip_group_check=True)
                return mm

            def panel(key, lhs, form, b0, tiles, fed=None):
                kk = end[key] - begin[key]
                for k in range(kk):
                    if fed is not None and k >= fed and k % 4 == 0:
                        pe.wait_ge(vec_for_pe, to_pe.up())
                    n = begin[key] + k
                    arrived(n)
                    w, act_ = parts(n), lhs(k)
                    todo = []
                    if form == "tokens":
                        for tb in range(TB):
                            for c in range(0, tiles, BANK):
                                todo.append((ps(b0 + 2 * tb + c // BANK, 1)[:, 0:min(BANK, tiles - c)],
                                             [v[:, tb * P:(tb + 1) * P] for v in act_],
                                             [v[:, c:min(c + BANK, tiles)] for v in w], True))
                    else:
                        for i in range(tiles):
                            todo.append((ps(b0 + i // 2, 1)[:, (i % 2) * T:(i % 2) * T + T],
                                         [v[:, i * P:(i + 1) * P] for v in w], act_, i % 2 == 0))
                    for o, a, b, first in todo:
                        mm = passes(o, a, b, k == 0 and first, k == kk - 1)
                    mm.then_inc(chunks_done, 1)

            def transpose_in(src, n_k, k_rows=P, b0=0, who="vv"):
                per = BANK // T
                nb = n_k // per
                for k in range(n_k):
                    for tb in range(TB):
                        mm = pe.transpose(ps(b0 + k // per, 1, k_rows)[:, (k % per) * T + tb * P:(k % per) * T + (tb + 1) * P],
                                          src(k, tb), ident)
                    if k == n_k // 2 - 1:
                        mm.then_inc(psum_for_vec, 1)
                mm.then_inc(psum_for_act if who == "va" else psum_for_vec, 1)
                return [banks.lend(range(b0, b0 + nb // 2), "v"), banks.lend(range(b0 + nb // 2, b0 + nb), who[1])]

            def wait_all(tokens):
                for s, v in tokens:
                    pe.wait_ge(s, v)

            def stream_T(n, src=None):
                if src is not None:
                    pe.wait_ge(vec_for_pe, to_pe.up())
                elif n:
                    pe.wait_ge(phase_done, n)
                else:
                    pe.wait_ge(input_loaded, 64)
                src = h if src is None else src
                hold(range(4))
                wait_all(transpose_in(lambda k, tb: src[:, tb, k * P:(k + 1) * P], KD))

            def split_of(v):
                return lambda k: (v[:, 0, k, :], v[:, 1, k, :])

            hk = split_of(hT)

            def four_by_four(k):
                return hk(k % KD)

            def pe_retention(a):
                for n, who in enumerate("vvaaaa"):
                    b0 = 4 * ((n + 1) % 2)
                    hold(range(b0, b0 + 4))
                    if n < 2:
                        panel(f"ret_in{n}", hk, "features", b0, 8)
                    else:
                        panel(f"ret_in{n}", hk, "tokens", b0, 1024)
                    tok = banks.lend(range(b0, b0 + 4), who)
                    if n == 1:
                        rotated = tok
                    if n == 3:
                        v_ready = tok
                pe.wait_ge(*rotated)
                hold(range(4, 8))
                for hd in range(RET_HEADS):
                    for mb in range(TB):
                        for d in range(2):
                            mm = pe.matmul(ps(4 + hd, 1)[:, mb * T:(mb + 1) * T],
                                           a["kT"][:, 2 * hd + d, mb * P:(mb + 1) * P], a["qT"][:, 2 * hd + d, :],
                                           start=(mb == 0 and d == 0), stop=(d == 1), skip_group_check=True)
                mm.then_inc(psum_for_vec, 1)
                decayed = banks.lend(range(4, 8), "v")
                pe.wait_ge(*decayed)
                pe.wait_ge(*v_ready)
                for tb in range(TB):
                    b0 = 4 * tb
                    hold(range(b0, b0 + 4))
                    for hd in range(RET_HEADS):
                        for mb in range(TB):
                            mm = pe.matmul(ps(b0 + hd, 1), a["s"][:, hd, mb, tb * P:(tb + 1) * P],
                                           a["v"][:, mb, hd * BANK:(hd + 1) * BANK], start=(mb == 0), stop=(mb == 1))
                    mm.then_inc(psum_for_vec, 1)
                    gated = banks.lend(range(b0, b0 + 4), "v")
                pe.wait_ge(*gated)
                toks = []
                for half in range(2):
                    toks += transpose_in(lambda k, tb: a["y"][:, tb, (8 * half + k) * P:(8 * half + k + 1) * P], 8, b0=4 * half)
                wait_all(toks)
                hold(range(4))
                panel("ret_out", four_by_four, "tokens", 0, D, fed=8)
                banks.lend(range(4), "v")

            def pe_peer(phase, a):
                for n in range(2):
                    b0 = 4 * (1 - n)
                    hold(range(b0, b0 + 4))
                    panel(f"{phase}_q{n}", hk, "features", b0, 8)
                    q = banks.lend(range(b0, b0 + 4), "v")
                pe.wait_ge(*q)
                hold(range(8))
                for n in range(2):
                    c = begin[phase + "_keys"] + n
                    arrived(c)
                    for tb in range(TB):
                        for i in range(8):
                            hc = 8 * n + i
                            mm = pe.matmul(ps(4 * tb + hc // 4, 1)[:, (hc % 4) * P:(hc % 4 + 1) * P],
                                           a["qT"][:, hc, tb * P:(tb + 1) * P], ring[:, c % RING, i * P:(i + 1) * P],
                                           start=(hc % 4 == 0), stop=True, skip_group_check=True)
                    mm.then_inc(chunks_done, 1)
                banks.lend(range(8), "a")

                hold([6, 7])
                n, d0 = begin[phase + "_u"], experts_before[phase]

                tile_less = tile_count[n] - split_count[n]

                def hidden(n, split, i, buf, fresh=False):
                    pe.wait_ge(chunk_split, split)
                    pe.wait_ge(tile_lo, split + tile_less)
                    if not fresh:
                        pe.wait_ge(gelu_done, i - 1)
                    u = parts(n)
                    for k in range(KD):
                        for w, (p, q) in enumerate(((0, 0), (0, 1), (1, 0))):
                            mm = pe.matmul(ps(6 + buf, 1)[:, 0:T], u[p][:, k * P:(k + 1) * P], hT[:, q, k, :], start=(k == 0 and w == 0),
                                           stop=(k == KD - 1 and w == 2))
                    mm.then_inc(chunks_done, 1)

                for r in range(RING):
                    hidden(n + r, split_count[n + r], d0 + r, r % 2, fresh=r < 2)
                with pe.Fori(1, HALF // RING) as it:
                    for r in range(RING):
                        hidden(n + r, it * RING + split_count[n + r], it * RING + (d0 + r), r % 2)

                pe.wait_ge(vec_for_pe, to_pe.up())
                hold([0, 1])
                for w in range(3):
                    for tb in range(TB):
                        mm = pe.transpose(ps(0, 2)[:, w * T + tb * P:w * T + (tb + 1) * P],
                                          a["ijg"][:, w, tb, :, :].rearrange("p a b -> p (a b)"), ident)
                mm.then_inc(psum_for_vec, 1)
                banks.lend([0, 1], "v")
                hold([4, 5])
                base = gates_before[phase]

                def gates(g, half, fresh=False):
                    if not fresh:
                        pe.wait_ge(gates_placed, g + (base - 1))
                    pe.wait_ge(onehots_made, g + (base + 1))
                    pe.wait_ge(j_onehots, g + (base + 1))
                    for q in range(4):
                        mm = pe.matmul(ps(4 + half, 1)[:, q * HALF:(q + 1) * HALF], j_onehot[:, half, q, :],
                                       i_onehot[:, half, q, :], start=(q == 0), stop=True, skip_group_check=True)
                    mm.then_inc(onehots_used, 1)

                for r in range(RING):
                    hidden(n + HALF + r, split_count[n + HALF + r], d0 + HALF + r, r % 2)
                    gates(r, r % 2, fresh=r < 2)
                with pe.Fori(1, HALF // RING) as it:
                    for r in range(RING):
                        hidden(n + HALF + r, it * RING + split_count[n + HALF + r], it * RING + (d0 + HALF + r), r % 2)
                        gates(it * RING + r, r % 2)
                gates(GROUPS, 0)
                gates(GROUPS + 1, 1)

                hold(range(4))
                n = begin[phase + "_v"]

                def output(n, split, i, buf, first=False, last=False):
                    pe.wait_ge(chunk_split, split)
                    pe.wait_ge(tile_lo, split + tile_less)
                    pe.wait_ge(weights_ready, i + 1)
                    v = parts(n)
                    for tb in range(TB):
                        for c in range(2):
                            for w, (p, q) in enumerate(((0, 0), (0, 1), (1, 0))):
                                mm = pe.matmul(ps(2 * tb + c, 1), tile_w[:, buf, p, tb * P:(tb + 1) * P],
                                               v[q][:, c * BANK:(c + 1) * BANK],
                                               start=(first and w == 0), stop=(last and w == 2), skip_group_check=True)
                    mm.then_inc(chunks_done, 1)

                for i in range(RING):
                    output(n + i, split_count[n + i], d0 + i, i % 2, first=(i == 0))
                    gates(GROUPS + 2 + i, i % 2)
                with pe.Fori(1, HALF // RING - 1) as it:
                    for r in range(RING):
                        output(n + r, it * RING + split_count[n + r], it * RING + (d0 + r), r % 2)
                        gates(it * RING + (GROUPS + 2 + r), r % 2)
                for i in range(HALF - RING, HALF):
                    output(n + i, split_count[n + i], d0 + i, i % 2)
                    if i < HALF - 2:
                        gates(GROUPS + 2 + i, i % 2)
                with pe.Fori(HALF // RING, NK // RING - 1) as it:
                    for r in range(RING):
                        output(n + r, it * RING + split_count[n + r], it * RING + (d0 + r), r % 2)
                for i in range(NK - RING, NK):
                    output(n + i, split_count[n + i], d0 + i, i % 2, last=(i == NK - 1))
                banks.lend(range(4), "v")

            def turn_p(p, b0):
                return transpose_in(lambda k, tb: p[:, tb, k // TB, (k % TB) * P:(k % TB + 1) * P], 8, b0=b0, who="va")

            def pe_mla(a):
                hold(range(4, 8))
                panel("mla_in", hk, "tokens", 4, MLA_IN)
                pe.wait_ge(*banks.lend(range(4, 8), "v"))
                hold(range(3))
                for k in range(5):
                    for tb in range(TB):
                        pe.transpose(ps(k // 2, 1)[:, (k % 2) * T + tb * P:(k % 2) * T + (tb + 1) * P],
                                     a["c"][:, tb, k * P:(k + 1) * P], ident)
                for tb in range(TB):
                    mm = pe.transpose(ps(2, 1, ROPE)[:, T + tb * P:T + (tb + 1) * P],
                                      a["c"][:, tb, Q_RANK + KV_RANK:MLA_IN], ident)
                mm.then_inc(psum_for_vec, 1)
                pe.wait_ge(*banks.lend(range(3), "v"))
                toks = []
                for n in range(2):
                    b0 = 4 * (1 - n)
                    hold(range(b0, b0 + 3))
                    for k in range(3):
                        c = begin[f"mla_uq{n}"] + k
                        arrived(c)
                        w = [v[:, 0:768].rearrange("p (h e) -> p h e", h=4) for v in parts(c)]
                        lat = hk(k)
                        for hd in range(4):
                            passes(ps(b0 + hd // 2, 1)[:, (hd % 2) * T:(hd % 2 + 1) * T], [v[:, hd, 0:NOPE] for v in w], lat,
                                   k == 0 and hd % 2 == 0, k == 2)
                        for tb in range(TB):
                            mm = passes(ps(b0 + 2, 1)[:, tb * T:(tb + 1) * T].rearrange("p (h e) -> p h e", h=4),
                                        [v[:, tb * P:(tb + 1) * P] for v in lat], [v[:, :, NOPE:] for v in w],
                                        k == 0 and tb == 0, k == 2)
                        mm.then_inc(chunks_done, 1)
                    toks += [banks.lend([b0, b0 + 1], "a"), banks.lend([b0 + 2], "v")]
                for n in range(2):
                    b0 = 4 * (1 - n)
                    hold(range(b0, b0 + 4))
                    for k in range(2):
                        c = begin[f"mla_ukv{n}"] + k
                        arrived(c)
                        w = [v.rearrange("p (h e) -> p h e", h=4) for v in parts(c)]
                        lat = hk(3 + k)
                        for hd in range(4):
                            passes(ps(b0 + hd // 2, 1)[:, (hd % 2) * T:(hd % 2 + 1) * T], [v[:, hd, 0:NOPE] for v in w], lat,
                                   k == 0 and hd % 2 == 0, k == 1)
                        for tb in range(TB):
                            mm = passes(ps(b0 + 2 + tb, 1).rearrange("p (h e) -> p h e", h=4),
                                        [v[:, tb * P:(tb + 1) * P] for v in lat], [v[:, :, NOPE:] for v in w],
                                        k == 0, k == 1)
                        mm.then_inc(chunks_done, 1)
                    toks += [banks.lend([b0, b0 + 1], "a"), banks.lend([b0 + 2, b0 + 3], "v")]
                wait_all(toks[:4])
                hold(range(4, 8))
                for hd in range(MLA_HEADS):
                    for tb in range(TB):
                        mm = pe.transpose(ps(4 + hd // 2, 1, ROPE)[:, (hd % 2) * T + tb * P:(hd % 2) * T + (tb + 1) * P],
                                          a["qr"][:, tb, hd, :], ident)
                mm.then_inc(psum_for_act, 1)
                toks.append(banks.lend(range(4, 8), "a"))
                wait_all(toks[4:])
                for n in range(2):
                    hold(range(4))
                    for tb in range(TB):
                        for i in range(4):
                            hd = 4 * n + i
                            o = ps(2 * tb + i // 2, 1)[:, (i % 2) * T:(i % 2 + 1) * T]
                            pe.matmul(o, a["qnT"][:, hd, tb * P:(tb + 1) * P], a["knT"][:, hd, :],
                                      start=(i % 2 == 0), stop=False, skip_group_check=True)
                            mm = pe.matmul(o, a["qrT"][:, hd, tb * P:(tb + 1) * P], a["krT"],
                                           start=False, stop=True, skip_group_check=True)
                    mm.then_inc(psum_for_vec, 1)
                    pe.wait_ge(*banks.lend(range(4), "v"))
                    hold(range(4, 8))
                    wait_all(turn_p(a["p"], 4))
                    hold([0, 1])
                    for i in range(4):
                        for kb in range(TB):
                            mm = pe.matmul(ps(i // 2, 1)[:, (i % 2) * T:(i % 2 + 1) * T],
                                           a["v"][:, kb, (4 * n + i) * VDIM:(4 * n + i + 1) * VDIM], a["pT"][:, i, kb, :],
                                           start=(i % 2 == 0 and kb == 0), stop=(kb == 1), skip_group_check=True)
                    mm.then_inc(psum_for_vec, 1)
                    o_ready = banks.lend([0, 1], "v")
                pe.wait_ge(*o_ready)
                hold(range(4, 8))
                panel("mla_out", hk, "tokens", 4, D)
                banks.lend(range(4, 8), "v")

            def pe_mixers(a):
                for n in range(4):
                    b0 = 4 * ((n + 1) % 2)
                    hold(range(b0, b0 + 4))
                    panel(f"slots{n}", hk, "features", b0, 4)
                    banks.lend(range(b0, b0 + 4), "a")
                hold(range(4, 8))
                panel("diff_v", hk, "tokens", 4, DIFF_W)
                banks.lend(range(4, 8), "a")
                hold(range(4))
                panel("pool_in", hk, "tokens", 0, POOL_W)
                pe.wait_ge(*banks.lend(range(4), "a"))
                hold([0, 1])
                for g in range(4):
                    for tb in range(TB):
                        mm = pe.matmul(ps(g // 2, 1, C)[:, (g % 2) * T:(g % 2 + 1) * T],
                                       a["pv"][:, tb, g * C:(g + 1) * C], a["pool"][:, tb, g, :],
                                       start=(g % 2 == 0 and tb == 0), stop=(tb == 1), skip_group_check=True)
                mm.then_inc(psum_for_vec, 1)
                pe.wait_ge(*banks.lend([0, 1], "v"))
                hold([2, 3])
                for g in range(4):
                    mm = pe.matmul(ps(2, 1)[:, (g // 2) * T:(g // 2 + 1) * T],
                                   a["pool_pairs"][:, g, :, :].rearrange("p two c -> p (two c)"), a["d"][:, g, :],
                                   start=(g == 0), stop=(g % 2 == 1), skip_group_check=True)
                mm.then_inc(psum_for_vec, 1)
                banks.lend([2], "v")
                pe.wait_ge(act_for_pe, act_to_pe.up())
                hold(range(6))
                for w, (wt, slot) in enumerate((("w2", 12), ("a2", 13))):
                    for hd in range(NH):
                        mm = pe.matmul(ps(2 * w + hd // 2, 1, C)[:, (hd % 2) * T:(hd % 2 + 1) * T],
                                       a[wt][:, hd * C:(hd + 1) * C], a["zm"][:, slot, :],
                                       start=(hd % 2 == 0), stop=True, skip_group_check=True)
                for c in range(NC_):
                    for s in range(2):
                        mm = pe.matmul(ps(4 + c // 2, 1, C)[:, (c % 2) * T:(c % 2 + 1) * T],
                                       a["zm"][:, 14 + s, c * C:(c + 1) * C], a["g2"][:, s, :],
                                       start=(c % 2 == 0 and s == 0), stop=(s == 1), skip_group_check=True)
                mm.then_inc(psum_for_act, 1)
                banks.lend(range(6), "a")
                pe.wait_ge(vec_for_pe, to_pe.up())
                hold([6, 7])
                for i in range(2):
                    mm = pe.matmul(ps(6 + i, 1, C), a["ones"], a["kk2"][:, 2 * i:2 * i + 2, :].rearrange("p h t -> p (h t)"),
                                   start=True, stop=True)
                mm.then_inc(psum_for_act, 1)
                banks.lend([6, 7], "a")
                pe.wait_ge(vec_for_pe, to_pe.up())
                hold(range(8))
                vz = a["zm"][:, 8:12, :].rearrange("p h (c t) -> p (h c) t", c=NC_)
                idc = ident[0:C, 0:C]
                for w in range(4):
                    for u in range(UN):
                        src = (a["ar"][:, u, 0, :], a["bt"][:, u, :], a["kt"][:, u, :], vz[:, u, :])[w]
                        mm = pe.transpose(ps(2 * w + u // 8, 1, C)[:, (u % 8) * C:(u % 8 + 1) * C], src, idc)
                    if w == 1:
                        mm.then_inc(psum_for_act, 1)
                mm.then_inc(psum_for_vec, 1)
                turned = [banks.lend(range(4), "a"), banks.lend(range(4, 8), "v")]
                for w, src in enumerate(("bt", "kt")):
                    hold(range(4 * w, 4 * w + 4))
                    for u in range(UN):
                        mm = pe.matmul(ps(4 * w + u // 4, 1, C)[:, (u % 4) * P:(u % 4 + 1) * P], a[src][:, u, :],
                                       a["ar"][:, u, :, :].rearrange("p w t -> p (w t)"), start=(u % 4 == 0), stop=True,
                                       skip_group_check=True)
                    mm.then_inc(psum_for_vec, 1)
                    masked = banks.lend(range(4 * w, 4 * w + 4), "v")
                pe.wait_ge(*masked)
                wait_all(turned)

                def units(b0, lhs, rhs, first=True, last=True, us=range(UN)):
                    for u in us:
                        mm = pe.matmul(ps(b0 + u // 8, 1, C)[:, (u % 8) * C:(u % 8 + 1) * C], lhs(u), rhs(u),
                                       start=(first and u % 8 == 0), stop=last, skip_group_check=True)
                    return mm

                def of(name):
                    return lambda u: a[name][:, u, :]

                def part(name, w):
                    return lambda u: a[name][:, u, w * C:(w + 1) * C]

                def tm(w):
                    return lambda u: a["tm"][:, w, u, :]

                for b in range(LEVELS):
                    pe.wait_ge(vec_for_pe, to_pe.up())
                    if b:
                        hold([0, 1])
                        units(0, of("aoff"), of("Tm")).then_inc(psum_for_vec, 1)
                        x_ready = banks.lend([0, 1], "v")
                    else:
                        hold([2, 3])
                        for u in range(UN):
                            mm = pe.transpose(ps(2 + u // 8, 1, C)[:, (u % 8) * C:(u % 8 + 1) * C], a["aoff"][:, u, :], idc)
                        mm.then_inc(psum_for_vec, 1)
                        inverse = banks.lend([2, 3], "v")
                    if b < 4:
                        pe.wait_ge(act_for_pe, act_to_pe.up())
                        hold([6, 7])
                        for i in range(2):
                            mm = pe.matmul(ps(6 + i, 1, C), a["ones"], a["sq"][:, i, :], start=True, stop=True)
                        mm.then_inc(psum_for_vec, 1)
                        banks.lend([6, 7], "v")
                    if b == 0:
                        continue
                    pe.wait_ge(*x_ready)
                    hold(range(2, 6))
                    units(2, of("TmT"), of("X"))
                    units(4, of("X"), of("TmT")).then_inc(psum_for_vec, 1)
                    inverse = banks.lend(range(2, 6), "v")
                hold([0, 1])
                units(0, part("mak", 0), tm(3)).then_inc(psum_for_act, 1)
                akv = banks.lend([0, 1], "a")
                pe.wait_ge(*inverse)
                hold([2, 3])
                units(2, of("TmT"), tm(0)).then_inc(psum_for_vec, 1)
                g1 = banks.lend([2, 3], "v")
                pe.wait_ge(*akv)
                hold([6, 7])
                units(6, of("TmT"), of("AkV")).then_inc(psum_for_act, 1)
                u0 = banks.lend([6, 7], "a")
                pe.wait_ge(*g1)
                hold(range(4))
                units(0, of("G1"), part("mab", 1))
                units(2, of("G1"), tm(1)).then_inc(psum_for_vec, 1)
                qm = banks.lend(range(4), "v")
                hold([4, 5])
                units(4, lambda u: a["rk"][:, u, :], lambda u: a["ones"]).then_inc(psum_for_act, 1)
                banks.lend([4, 5], "a")
                pe.wait_ge(*u0)
                pe.wait_ge(*qm)
                hold(range(0, 8))
                units(0, part("mab", 1), of("U0"), last=False)
                units(0, part("mak", 1), tm(3), first=False, last=False)
                for c in range(NC_):
                    mine = [hd * NC_ + c for hd in range(NH)]
                    if c:
                        pe.wait_ge(*state)
                        mm = units(0, of("Q"), lambda u: a["S"][:, c - 1, u // NC_, :], first=False, us=mine)
                    if c < NC_ - 1:
                        terms = [(tm(1), of("U0")), (tm(2), tm(3))]
                        if c:
                            terms.append((of("Mt"), lambda u: a["S"][:, c - 1, u // NC_, :]))
                        for i, (lhs, rhs) in enumerate(terms):
                            for u in mine:
                                hd = u // NC_
                                mm = pe.matmul(ps(2 + c, 1, C)[:, hd * C:(hd + 1) * C], lhs(u), rhs(u),
                                               start=(i == 0 and hd == 0), stop=(i == len(terms) - 1), skip_group_check=True)
                        mm.then_inc(psum_for_vec, 1)
                        state = banks.lend([2 + c], "v")
                mm.then_inc(psum_for_vec, 1)
                pe.wait_ge(*banks.lend([0, 1], "v"))
                hold([6])
                for c in range(NC_):
                    for i in range(2):
                        mm = pe.transpose(ps(6, 1)[:, i * T + c * C:i * T + (c + 1) * C],
                                          a["gated"][:, c, 2 * i:2 * i + 2, :].rearrange("p h v -> p (h v)"), idc)
                mm.then_inc(psum_for_vec, 1)
                banks.lend([6], "v")
                hold(range(8))
                for c in range(2):
                    b0 = 4 * c
                    for tb in range(TB):
                        for hd in range(4):
                            mm = pe.matmul(ps(b0 + 2 * tb + hd // 2, 1)[:, (hd % 2) * T:(hd % 2 + 1) * T],
                                           a["qk"][:, 0, 2 * hd + c, tb * P:(tb + 1) * P], a["qk"][:, 1, 2 * hd + c, :],
                                           start=(hd % 2 == 0), stop=True, skip_group_check=True)
                    mm.then_inc(psum_for_vec, 1)
                    probs = banks.lend(range(b0, b0 + 4), "v")
                pe.wait_ge(*probs)
                wait_all(turn_p(a["p"][:, 0], 4))
                hold([0, 1])
                for tb in range(TB):
                    for hd in range(4):
                        for kb in range(TB):
                            mm = pe.matmul(ps(tb, 1)[:, hd * P:(hd + 1) * P], a["pT"][:, hd, kb, tb * P:(tb + 1) * P],
                                           a["pv"][:, kb, POOL_W + hd * P:POOL_W + (hd + 1) * P],
                                           start=(hd == 0 and kb == 0), stop=(kb == 1), skip_group_check=True)
                mm.then_inc(psum_for_vec, 1)
                pe.wait_ge(*banks.lend([0, 1], "v"))
                hold([2, 3])
                for hd in range(4):
                    for tb in range(TB):
                        mm = pe.transpose(ps(2 + hd // 2, 1)[:, (hd % 2) * T + tb * P:(hd % 2) * T + (tb + 1) * P],
                                          a["o"][:, tb, hd, :], ident)
                mm.then_inc(psum_for_vec, 1)
                pe.wait_ge(*banks.lend([2, 3], "v"))
                hold(range(4, 8))
                panel("mix_out", hk, "tokens", 4, D)
                banks.lend(range(4, 8), "v")

            def pe_cross(a):
                pe.wait_ge(vec_for_pe, to_pe.up())
                hold(range(4, 8))
                wait_all(transpose_in(lambda k, tb: a["mn"][:, tb, k * P:(k + 1) * P], KD, b0=4))
                hold(range(4))
                panel("xa_wk_2", hk, "tokens", 0, D)
                kn = banks.lend(range(4), "v")
                hold(range(4, 8))
                panel("xa_wv_2", hk, "tokens", 4, D)
                vv = banks.lend(range(4, 8), "a")
                pe.wait_ge(*kn)
                hold(range(4))
                wait_all(transpose_in(lambda k, tb: a["k"][:, tb, k * P:(k + 1) * P], KD, who="va"))
                stream_T(0, a["hn"])
                hold(range(4, 8))
                panel("xa_wq_2", hk, "tokens", 4, D)
                pe.wait_ge(*banks.lend(range(4, 8), "v"))
                hold(range(4))
                wait_all(transpose_in(lambda k, tb: a["q"][:, tb, k * P:(k + 1) * P], KD, who="va"))
                hold(range(4, 8))
                for tb in range(TB):
                    for hd in range(XH):
                        for d in range(2):
                            mm = pe.matmul(ps(4 + 2 * tb + hd // 2, 1)[:, (hd % 2) * T:(hd % 2 + 1) * T],
                                           a["qT"][:, 2 * hd + d, tb * P:(tb + 1) * P], a["kT"][:, 2 * hd + d, :],
                                           start=(hd % 2 == 0 and d == 0), stop=(d == 1), skip_group_check=True)
                mm.then_inc(psum_for_vec, 1)
                pe.wait_ge(*banks.lend(range(4, 8), "v"))
                hold(range(4))
                wait_all(turn_p(a["p"], 0))
                pe.wait_ge(*vv)
                hold(range(4, 8))
                for i in range(8):
                    for kb in range(TB):
                        mm = pe.matmul(ps(4 + i // 2, 1)[:, (i % 2) * T:(i % 2 + 1) * T],
                                       a["v"][:, kb, i * P:(i + 1) * P], a["pT"][:, i // 2, kb, :],
                                       start=(i % 2 == 0 and kb == 0), stop=(kb == 1), skip_group_check=True)
                mm.then_inc(psum_for_vec, 1)
                pe.wait_ge(*banks.lend(range(4, 8), "v"))
                hold(range(4))
                panel("xa_wo_2", hk, "tokens", 0, D)
                banks.lend(range(4), "v")

            def pe_ffn(a):
                for n in range(6):
                    b0 = 4 * ((n + 1) % 2)
                    hold(range(b0, b0 + 4))
                    panel(f"up{n}", hk, "features", b0, 2 * min(4, FF_TILES - 4 * n))
                    hid = banks.lend(range(b0, b0 + 4), "v")
                pe.wait_ge(*hid)
                hold(range(4, 8))
                panel("down", four_by_four, "tokens", 4, D, fed=0)
                banks.lend(range(4, 8), "v")

            for n, phase in enumerate(phases):
                if phase in ("mixers", "ffn"):
                    stream_T(n, A[phase]["hn"])
                elif phase != "cross":
                    stream_T(n)
                if phase == "retention":
                    pe_retention(A[phase])
                if phase == "mla":
                    pe_mla(A[phase])
                if phase == "mixers":
                    pe_mixers(A[phase])
                if phase == "cross":
                    pe_cross(A[phase])
                if phase == "ffn":
                    pe_ffn(A[phase])
                if phase.startswith("peer"):
                    pe_peer(phase, A[phase])

        @block.vector
        def _(vec):
            own = Last(vec_step)
            psum_v, from_act = Count(), Count()

            def done():
                vec.wait_ge(*own.last)

            n_split = Count()

            def round_to(hi, src):
                return vec.tensor_copy(hi, src)

            def lower(slot, part, count, k=P, wide=SLOT):
                vec.tensor_tensor(ring_lo[0:k, part, 0:wide], ring[0:k, slot, 0:wide], ring_hi[0:k, part, 0:wide].bitcast(F32),
                                  ALU.subtract).then_inc(chunk_split, 1)
                own.last = (chunk_split, count)

            def split_to(end_):
                while n_split.n < min(end_, n_chunks):
                    n = n_split.n
                    if n in tile_count:
                        vec.wait_ge(tile_hi, tile_count[n])
                        lower(n % RING, n % SPLIT, split_count[n], wide=BY_VEC)
                    elif n in hi_count:
                        k, wide = chunk_size[n]
                        vec.wait_ge(ring_loaded[n % RING], 16 * (n // RING + 1))
                        if n >= SPLIT:
                            vec.wait_ge(chunks_done, n - 1)
                        round_to(ring_hi[0:k, n % SPLIT, 0:wide], ring[0:k, n % RING, 0:wide]).then_inc(chunk_hi, 1)
                        vec.wait_ge(chunk_hi, hi_count[n])
                        lower(n % RING, n % SPLIT, split_count[n], k, wide)
                    n_split.up()

            def more(k, key):
                split_to(min(n_split.n + k, end[key] + SPLIT))

            def panel_done(key):
                split_to(end[key] + SPLIT)
                vec.wait_ge(chunks_done, end[key])

            def ln_stream(key, b0, phase):
                flat, norm = h.rearrange("p a b -> p (a b)"), A[phase]["norm"]
                panel_done(key)
                vec.scalar_tensor_tensor(flat, flat, ALPHA, ps(b0, 4), ALU.mult, ALU.add).then_inc(*own.mark(vec_served))
                done()
                for tb in range(TB):
                    for c in range(2):
                        vec.bn_stats(stats[:, 2 * tb + c, 0, :], h[:, tb, c * BANK:(c + 1) * BANK]).then_inc(*own.next())
                done()
                for tb in range(TB):
                    vec.bn_aggr(mv[:, tb, :], stats[:, 2 * tb:2 * tb + 2, 0, :]).then_inc(*own.next())
                done()
                vec.tensor_scalar(rstd[:, 0:TB], mv[:, :, 1], LN_EPS, None, ALU.add).then_inc(*own.mark(vec_for_act))
                more(2, key)
                vec.wait_ge(norm_loaded, norm_loads[phase])
                for tb in range(TB):
                    vec.scalar_tensor_tensor(h[:, tb, :], h[:, tb, :], mv[:, tb, 0:1], norm[:, 0, :],
                                             ALU.subtract, ALU.mult).then_inc(*own.next())
                vec.wait_ge(act_for_vec, from_act.up())
                vec.reciprocal(rstd[:, 0:TB], rstd[:, 0:TB]).then_inc(*own.next())
                done()
                for tb in range(TB):
                    vec.scalar_tensor_tensor(h[:, tb, :], h[:, tb, :], rstd[:, tb:tb + 1], norm[:, 1, :],
                                             ALU.mult, ALU.add).then_inc(*(own.mark(phase_done) if tb else own.next()))
                done()

            def take_turned(dst, b0):
                vec.wait_ge(psum_for_vec, psum_v.up())
                vec.tensor_copy(dst.rearrange("p a b -> p (a b)"), ps(b0, 2)).then_inc(*own.mark(vec_served))

            def take_split(hi, lo, b0, nb, wide=None):
                hi, lo = (v.rearrange("p a b -> p (a b)") for v in (hi, lo))
                src = ps(b0, nb)[:, 0:wide or nb * BANK]
                round_to(hi, src).then_inc(*own.next())
                done()
                vec.tensor_tensor(lo, src, hi.bitcast(F32), ALU.subtract).then_inc(*own.mark(vec_served))
                done()

            def feed(key, src, first=0):
                for k in range(first, end[key] - begin[key], 4):
                    if k >= KD:
                        split_to(begin[key] + k - 2)
                        vec.wait_ge(chunks_done, begin[key] + k - 4)
                    w = min(4, end[key] - begin[key] - k)
                    hi, lo = (hT[:, i, k % KD:k % KD + w, :] for i in range(2))
                    round_to(hi, src[:, k:k + w, :]).then_inc(*own.next())
                    done()
                    vec.tensor_tensor(lo, src[:, k:k + w, :], hi.bitcast(F32), ALU.subtract).then_inc(*own.mark(vec_for_pe))
                    done()

            def take_matrix(dst, b0=0):
                for i in range(2):
                    vec.wait_ge(psum_for_vec, psum_v.up())
                    take_split(dst[:, 0, 4 * i:4 * i + 4, :], dst[:, 1, 4 * i:4 * i + 4, :], b0 + 2 * i, 2)

            def reduced(dst, ang, turn, quarter):
                vec.tensor_scalar(turn, ang, 1.0 / (2 * np.pi), 0.25 if quarter else 0.0, ALU.mult, ALU.add).then_inc(*own.next())
                done()
                vec.tensor_scalar(turn, turn, ROUND, None, ALU.add).then_inc(*own.next())
                done()
                vec.tensor_scalar(turn, turn, -ROUND, None, ALU.add).then_inc(*own.next())
                done()
                vec.scalar_tensor_tensor(dst, turn, -TWO_PI_HI, ang, ALU.mult, ALU.add).then_inc(*own.next())
                done()
                vec.scalar_tensor_tensor(dst, turn, -TWO_PI_LO, dst, ALU.mult, ALU.add).then_inc(*own.next())
                done()
                if quarter:
                    vec.tensor_scalar(dst, dst, float(np.pi / 2), None, ALU.add).then_inc(*own.next())
                    done()
                vec.tensor_scalar(dst, dst, PI_IN, -PI_IN, ALU.min, ALU.max).then_inc(*own.next())
                done()

            def vec_retention(a, phase):
                split_to(2)
                vec.wait_ge(params_loaded, loads[phase])
                vec.tensor_copy(a["ang"], a["posi"].bitcast(I32)).then_inc(*own.next())
                done()
                vec.tensor_scalar(a["ang"], a["ang"], a["freq"], None, ALU.mult).then_inc(*own.next())
                done()
                reduced(a["cos"], a["ang"], a["turn"], True)
                reduced(a["sin"], a["ang"], a["turn"], False)
                vec.tensor_copy(a["turn"], a["ang"]).then_inc(*own.mark(vec_for_act))
                vec.wait_ge(act_for_vec, from_act.up())
                for hd in range(RET_HEADS):
                    vec.tensor_scalar(a["decay"][:, hd, :], a["ahead"][:, 0, :], a["lg"][:, hd:hd + 1], None,
                                      ALU.mult).then_inc(*own.next())
                done()
                for hd in range(RET_HEADS):
                    vec.scalar_tensor_tensor(a["decay"][:, hd, :], a["ahead"][:, 1, :], a["lg"][:, 4 + hd:5 + hd],
                                             a["decay"][:, hd, :], ALU.mult, ALU.add).then_inc(
                        *(own.mark(vec_for_act) if hd == RET_HEADS - 1 else own.next()))
                vec.wait_ge(act_for_vec, from_act.up())
                cos, sin = bcast(a["cos"], 1, RET_HEADS), bcast(a["sin"], 1, RET_HEADS)
                for w, (dst, b0) in enumerate(((a["qT"], 4), (a["kT"], 0))):
                    panel_done(f"ret_in{w}")
                    src = ps(b0, 4).rearrange("p (h two t) -> p h two t", two=2, t=T)
                    to = dst.rearrange("p (h two) t -> p h two t", two=2)
                    x1, x2 = src[:, :, 0, :], src[:, :, 1, :]
                    t1, t2 = a["tmp"][:, 0], a["tmp"][:, 1]
                    vec.tensor_tensor(t1, x1, cos, ALU.mult).then_inc(*own.next())
                    vec.tensor_tensor(t2, x2, sin, ALU.mult).then_inc(*own.next())
                    done()
                    vec.tensor_tensor(to[:, :, 0, :], t1, t2, ALU.subtract).then_inc(*own.next())
                    done()
                    vec.tensor_tensor(t1, x1, sin, ALU.mult).then_inc(*own.next())
                    vec.tensor_tensor(t2, x2, cos, ALU.mult).then_inc(*own.next())
                    done()
                    vec.tensor_tensor(to[:, :, 1, :], t1, t2, ALU.add).then_inc(*own.mark(vec_served))
                    done()
                split_to(end["ret_in5"] + SPLIT)
                vec.wait_ge(psum_for_vec, psum_v.up())
                vec.scalar_tensor_tensor(a["s"].rearrange("p a b c -> p (a b c)"), ps(4, 4), RET_DK ** -0.5,
                                         a["decay"].rearrange("p a b -> p (a b)"), ALU.mult, ALU.mult).then_inc(*own.mark(vec_served))
                for tb in range(TB):
                    vec.wait_ge(psum_for_vec, psum_v.up())
                    for hd in range(RET_HEADS):
                        vec.bn_stats(stats[:, hd, 0, :], ps(4 * tb + hd, 1)).then_inc(*own.next())
                    done()
                    for hd in range(RET_HEADS):
                        vec.bn_aggr(var8[:, 4 * tb + hd, :], stats[:, hd, 0, :]).then_inc(*own.next())
                    done()
                    r = rstd[:, 4 * tb:4 * tb + 4]
                    vec.tensor_scalar(r, var8[:, 4 * tb:4 * tb + 4, 1], LN_EPS, None, ALU.add).then_inc(*own.mark(vec_for_act))
                    heads = [slice(hd * BANK, (hd + 1) * BANK) for hd in range(RET_HEADS)]
                    for hd, s in enumerate(heads):
                        vec.scalar_tensor_tensor(a["y"][:, tb, s], ps(4 * tb + hd, 1), var8[:, 4 * tb + hd, 0:1], a["gn"][:, 0, s],
                                                 ALU.subtract, ALU.mult).then_inc(*own.next())
                    vec.wait_ge(act_for_vec, from_act.up())
                    vec.reciprocal(r, r).then_inc(*own.next())
                    done()
                    for hd, s in enumerate(heads):
                        vec.scalar_tensor_tensor(a["y"][:, tb, s], a["y"][:, tb, s], r[:, hd:hd + 1], a["gn"][:, 1, s],
                                                 ALU.mult, ALU.add).then_inc(*own.next())
                    done()
                    y = a["y"][:, tb, :]
                    vec.tensor_tensor(y, y, a["g"][:, tb, :], ALU.mult).then_inc(*own.mark(vec_served))
                    done()
                for i in range(4):
                    from_psum()
                    if i < 2:
                        take_split(hT[:, 0, 4 * i:4 * i + 4, :], hT[:, 1, 4 * i:4 * i + 4, :], 2 * i, 2)
                    else:
                        vec.tensor_copy(a["yT"][:, 4 * i:4 * i + 4, :].rearrange("p a b -> p (a b)"), ps(2 * i, 2)).then_inc(*served())
                done()
                feed("ret_out", a["yT"], KD)
                ln_stream("ret_out", 0, phase)

            def rms_stream(src, dst, gain, loaded):
                for tb in range(TB):
                    for c in range(2):
                        vec.bn_stats(stats[:, 2 * tb + c, 0, :], src[:, tb, c * BANK:(c + 1) * BANK]).then_inc(*own.next())
                done()
                for tb in range(TB):
                    vec.bn_aggr(mv[:, tb, :], stats[:, 2 * tb:2 * tb + 2, 0, :]).then_inc(*own.next())
                done()
                r = rstd[:, 0:TB]
                vec.tensor_tensor(r, mv[:, :, 0], mv[:, :, 0], ALU.mult).then_inc(*own.next())
                done()
                vec.scalar_tensor_tensor(r, r, RMS_EPS, mv[:, :, 1], ALU.add, ALU.add).then_inc(*own.mark(vec_for_act))
                vec.wait_ge(*loaded)
                for tb in range(TB):
                    vec.tensor_tensor(dst[:, tb, :], src[:, tb, :], gain, ALU.mult).then_inc(*own.next())
                vec.wait_ge(act_for_vec, from_act.up())
                vec.reciprocal(r, r).then_inc(*own.next())
                done()
                for tb in range(TB):
                    vec.tensor_scalar(dst[:, tb, :], dst[:, tb, :], rstd[:, tb:tb + 1], None, ALU.mult).then_inc(
                        *(own.mark(vec_for_pe) if tb == TB - 1 else own.next()))
                done()

            def add_stream(key, b0):
                flat = h.rearrange("p a b -> p (a b)")
                panel_done(key)
                vec.tensor_tensor(flat, flat, ps(b0, 4), ALU.add).then_inc(*own.mark(vec_served))
                done()
                vec.tensor_copy(misc[:, 511:512], iota[:, 0:1]).then_inc(*own.mark(phase_done))
                done()

            def softmax(src, p, top, total, last):
                rows_ = p.rearrange("p b h k -> p (b h) k")
                vec.tensor_reduce(top, src, AX, ALU.max).then_inc(*own.next())
                done()
                vec.tensor_tensor(rows_, src, bcast(top, 2, T), ALU.subtract).then_inc(*own.mark(vec_for_act))
                vec.wait_ge(act_for_vec, from_act.up())
                vec.tensor_reduce(total, rows_, AX, ALU.add).then_inc(*own.next())
                done()
                vec.reciprocal(total, total).then_inc(*own.next())
                done()
                vec.tensor_tensor(rows_, rows_, bcast(total, 2, T), ALU.mult).then_inc(*last())
                done()

            def served():
                return own.mark(vec_served)

            def from_psum():
                vec.wait_ge(psum_for_vec, psum_v.up())

            def rooted(v, scale, eps):
                vec.tensor_scalar(v, v, scale, eps, ALU.mult, ALU.add).then_inc(*own.mark(vec_for_act))
                vec.wait_ge(act_for_vec, from_act.up())
                vec.reciprocal(v, v).then_inc(*own.next())
                done()

            top8, sum8 = misc[:, 256:264], misc[:, 264:272]

            def vec_mla(a, phase):
                half = ROPE // 2
                vec.wait_ge(params_loaded, loads[phase])
                vec.tensor_copy(a["pos"], a["posi"].bitcast(I32)).then_inc(*own.next())
                done()
                for tb in range(TB):
                    vec.tensor_scalar(a["ang"][:, tb, :], a["freq"], a["pos"][:, tb:tb + 1], None, ALU.mult).then_inc(*own.next())
                done()
                reduced(a["cos"], a["ang"], a["turn"], True)
                reduced(a["sin"], a["ang"], a["turn"], False)
                vec.tensor_copy(a["turn"], a["ang"]).then_inc(*own.mark(vec_for_act))
                panel_done("mla_in")
                c, r = a["c"], rstd[:, 0:4]
                vec.tensor_copy(c, ps(4, 4).rearrange("p (b c) -> p b c", b=TB)[:, :, 0:MLA_IN]).then_inc(*own.next())
                done()
                vec.tensor_tensor(a["sq"], c[:, :, 0:Q_RANK + KV_RANK], c[:, :, 0:Q_RANK + KV_RANK], ALU.mult).then_inc(*own.next())
                done()
                vec.tensor_reduce(r[:, 0:2], a["sq"][:, :, 0:Q_RANK], AX, ALU.add).then_inc(*own.next())
                vec.tensor_reduce(r[:, 2:4], a["sq"][:, :, Q_RANK:], AX, ALU.add).then_inc(*own.next())
                done()
                vec.tensor_scalar(r[:, 0:2], r[:, 0:2], 1.0 / Q_RANK, LN_EPS, ALU.mult, ALU.add).then_inc(*own.next())
                vec.wait_ge(act_for_vec, from_act.up())
                vec.tensor_scalar(r[:, 2:4], r[:, 2:4], 1.0 / KV_RANK, LN_EPS, ALU.mult, ALU.add).then_inc(*own.mark(vec_for_act))
                vec.wait_ge(act_for_vec, from_act.up())
                vec.reciprocal(r, r).then_inc(*own.next())
                done()
                for tb in range(TB):
                    for i, s in enumerate((slice(0, Q_RANK), slice(Q_RANK, Q_RANK + KV_RANK))):
                        vec.scalar_tensor_tensor(c[:, tb, s], c[:, tb, s], r[:, 2 * i + tb:2 * i + tb + 1], a["gain"][:, s],
                                                 ALU.mult, ALU.mult).then_inc(*own.next())

                def rotate(x1, x2, o1, o2, cos, sin, t):
                    vec.tensor_tensor(t[0], x1, cos, ALU.mult).then_inc(*own.next())
                    vec.tensor_tensor(t[1], x2, sin, ALU.mult).then_inc(*own.next())
                    vec.tensor_tensor(t[2], x1, sin, ALU.mult).then_inc(*own.next())
                    vec.tensor_tensor(t[3], x2, cos, ALU.mult).then_inc(*own.next())
                    done()
                    vec.tensor_tensor(o1, t[0], t[1], ALU.subtract).then_inc(*own.next())
                    vec.tensor_tensor(o2, t[2], t[3], ALU.add).then_inc(*own.mark(vec_served))
                    done()

                k1, k2 = c[:, :, MLA_IN - ROPE:MLA_IN - half], c[:, :, MLA_IN - half:]
                rotate(k1, k2, k1, k2, a["cos"], a["sin"],
                       [a["tmp"][:, i, 0:TB * half].rearrange("p (b e) -> p b e", b=TB) for i in range(4)])
                from_psum()
                vec.tensor_copy(a["krT"], ps(2, 1, ROPE)[:, T:]).then_inc(*own.next())
                take_split(hT[:, 0, 0:5, :], hT[:, 1, 0:5, :], 0, 3, 5 * T)
                for i in range(2):
                    b0 = 4 * (1 - i)
                    panel_done(f"mla_uq{i}")
                    q = ps(b0 + 2, 1).rearrange("p (b h e) -> p b h e", b=TB, h=4)
                    to = a["qr"][:, :, 4 * i:4 * i + 4, :]
                    rotate(q[:, :, :, 0:half], q[:, :, :, half:], to[:, :, :, 0:half], to[:, :, :, half:],
                           bcast(a["cos"], 2, 4), bcast(a["sin"], 2, 4),
                           [a["tmp"][:, j, :].rearrange("p (b h e) -> p b h e", b=TB, h=4) for j in range(4)])
                for i in range(2):
                    b0 = 4 * (1 - i)
                    panel_done(f"mla_ukv{i}")
                    vec.tensor_copy(a["v"][:, :, i * BANK:(i + 1) * BANK],
                                    ps(b0 + 2, 2).rearrange("p (b c) -> p b c", b=TB)).then_inc(*served())
                for i in range(2):
                    from_psum()
                    softmax(ps(0, 4).rearrange("p (r k) -> p r k", k=T), a["p"], top8, sum8, served)
                    take_turned(a["pT"].rearrange("p h k t -> p (h k) t")[:, 0:4, :], 4)
                    from_psum()
                    take_split(hT[:, 0, 4 * i:4 * i + 4, :], hT[:, 1, 4 * i:4 * i + 4, :], 0, 2)
                ln_stream("mla_out", 4, phase)

            def vec_mixers(a):
                cols, zm = a["cols"], a["zm"]

                def col(i):
                    return bcast(cols[:, i, :], 2, T)

                def u3(v):
                    return v.rearrange("p h (c t) -> p (h c) t", c=NC_)

                def flat(v):
                    return v.rearrange("p a b -> p (a b)")

                vec.memset(a["z"][:, :, 0:1], 0.0).then_inc(*own.next())
                vec.memset(a["ones"], 1.0).then_inc(*own.next())
                vec.memset(a["pool_pairs"], 0.0).then_inc(*own.next())
                vec.wait_ge(params_loaded, loads["mixers"])
                done()
                for i in range(2):
                    vec.tensor_copy(a["pool_pairs"].rearrange("p (g two) s c -> p g two s c", two=2)[:, :, i, i, :],
                                    a["pool_w"].rearrange("p (g two) c -> p g two c", two=2)[:, :, i, :]).then_inc(*own.next())
                split_to(end["slots1"] + SPLIT)
                vec.wait_ge(act_for_vec, from_act.up())
                done()
                vec.tensor_tensor(zm, a["z"][:, :, 0:T], a["z"][:, :, 1:T + 1], ALU.subtract).then_inc(*own.next())
                more(6, "slots3")
                done()
                vec.tensor_tensor(zm, zm, bcast(a["mu"], 2, T), ALU.mult).then_inc(*own.next())
                more(6, "slots3")
                done()
                vec.tensor_tensor(zm, zm, a["z"][:, :, 1:T + 1], ALU.add).then_inc(*own.mark(vec_for_act))
                split_to(end["pool_in"] + SPLIT)
                done()
                from_psum()
                vec.tensor_copy(flat(a["d"]), ps(0, 2, C)).then_inc(*served())
                from_psum()
                vec.tensor_tensor(a["poolT"], ps(2, 1).rearrange("p (i t) -> p i t", t=T), bcast(a["pool_scale"], 2, T),
                                  ALU.mult).then_inc(*served())
                done()
                round_to(hT[:, 0, 0:2, :], a["poolT"]).then_inc(*own.next())
                done()
                vec.tensor_tensor(hT[:, 1, 0:2, :], a["poolT"], hT[:, 0, 0:2, :].bitcast(F32), ALU.subtract).then_inc(*own.next())
                r_, k_ = zm[:, 0:4, :], zm[:, 4:8, :]
                vec.tensor_tensor(a["kk"], k_, col(2), ALU.mult).then_inc(*own.next())
                vec.wait_ge(act_for_vec, from_act.up())
                vec.tensor_scalar(a["lw"], a["lw"], -float(np.exp(-0.5)), None, ALU.mult).then_inc(*own.next())
                done()
                vec.tensor_tensor_scan(flat(a["L"]), a["masks"][:, (2 + LEVELS) * C:], flat(a["lw"]), 0.0,
                                       ALU.mult, ALU.add).then_inc(*own.next())
                done()
                vec.tensor_tensor(a["Pp"], a["L"], a["lw"], ALU.subtract).then_inc(*own.mark(vec_for_act))
                done()
                vec.tensor_tensor(a["kk2"], a["kk"], a["kk"], ALU.mult).then_inc(*own.mark(vec_for_pe))
                kx = a["kx"]
                vec.tensor_scalar(kx, a["a"], -1.0, None, ALU.add).then_inc(*own.next())
                done()
                vec.tensor_tensor(kx, kx, col(3), ALU.mult).then_inc(*own.next())
                done()
                vec.scalar_tensor_tensor(kx, kx, 1.0, k_, ALU.add, ALU.mult).then_inc(*own.next())
                done()
                rk = a["rk"].rearrange("p (h c) t -> p h (c t)", h=NH)
                vec.tensor_tensor(rk, r_, kx, ALU.mult).then_inc(*own.next())
                done()
                vec.tensor_tensor(rk, rk, col(4), ALU.mult).then_inc(*own.next())
                vec.wait_ge(act_for_vec, from_act.up())
                vec.tensor_tensor(a["ar"][:, :, 1, :], u3(r_), u3(a["Pd"]), ALU.mult).then_inc(*own.next())
                vec.tensor_tensor(a["kt"], u3(kx), u3(a["Pi"]), ALU.mult).then_inc(*own.next())
                vec.tensor_copy(a["pend"], u3(a["Pd"])[:, :, C - 1]).then_inc(*own.next())
                vec.wait_ge(act_for_vec, from_act.up())
                n2 = a["kk2"]
                vec.tensor_scalar(n2, n2, 1e-12, None, ALU.max).then_inc(*own.next())
                done()
                vec.reciprocal(n2, n2).then_inc(*own.next())
                done()
                vec.tensor_tensor(a["kk"], a["kk"], n2, ALU.mult).then_inc(*own.next())
                done()
                vec.scalar_tensor_tensor(a["ar"][:, :, 0, :], u3(a["kk"]), -1.0, u3(a["Pp"]), ALU.mult, ALU.mult).then_inc(*own.next())
                done()
                vec.tensor_tensor(a["kk"], a["kk"], a["a"], ALU.mult).then_inc(*own.next())
                done()
                vec.tensor_tensor(a["bt"], u3(a["kk"]), u3(a["Pi"]), ALU.mult).then_inc(*own.mark(vec_for_pe))
                done()
                from_psum()
                vec.tensor_copy(a["tm"][:, 2:4].rearrange("p w u c -> p (w u c)"), ps(4, 4, C)).then_inc(*served())
                for i, name in enumerate(("mab", "mak")):
                    from_psum()
                    vec.tensor_tensor(a[name], ps(4 * i, 4, C).rearrange("p (u t) -> p u t", u=UN),
                                      bcast(a["masks"][:, 0:2 * C], 1, UN), ALU.mult).then_inc(*served())
                done()
                idc = bcast(ident[0:C, 0:C], 1, UN)
                def units(b0):
                    return ps(b0, 2, C).rearrange("p (u c) -> p u c", u=UN)

                for b in range(LEVELS):
                    vec.tensor_tensor(a["aoff"], a["mab"][:, :, 0:C], bcast(a["masks"][:, (2 + b) * C:(3 + b) * C], 1, UN),
                                      ALU.mult).then_inc(*own.mark(vec_for_pe))
                    from_psum()
                    if b:
                        vec.tensor_copy(a["X"], units(0)).then_inc(*served())
                    else:
                        vec.tensor_tensor(a["Tm"], idc, units(2), ALU.add).then_inc(*served())
                        done()
                        vec.tensor_tensor(a["TmT"], idc, a["aoff"], ALU.add).then_inc(*own.next())
                        done()
                    if b < 4:
                        quarter = slice(4 * b * T, 4 * (b + 1) * T)
                        rs, qk = (a[w].rearrange("p w s t -> p (w s t)")[:, quarter] for w in ("rs", "qk"))
                        from_psum()
                        vec.tensor_scalar(rs, ps(6, 2, C), 1.0 / C, RMS_EPS, ALU.mult, ALU.add).then_inc(*own.mark(vec_for_act))
                        vec.wait_ge(act_for_vec, from_act.up())
                        vec.reciprocal(rs, rs).then_inc(*own.next())
                        done()
                        vec.tensor_tensor(qk, qk, rs, ALU.mult).then_inc(*served())
                        done()
                    if b == 4:
                        for w in range(2):
                            for c in range(2):
                                v = a["qk"][:, w].rearrange("p (h c) t -> p h c t", c=2)[:, :, c, :]
                                vec.tensor_scalar(v, v, a["qk_gain"][:, w, c:c + 1], None, ALU.mult).then_inc(*own.next())
                    if b == 0:
                        continue
                    from_psum()
                    vec.tensor_tensor(a["Tm"], a["Tm"], units(2), ALU.add).then_inc(*own.next())
                    vec.tensor_tensor(a["TmT"], a["TmT"], units(4), ALU.add).then_inc(*served())
                    done()
                from_psum()
                vec.tensor_copy(a["G1"], units(2)).then_inc(*served())
                from_psum()
                vec.tensor_tensor(a["Q"], units(0), a["ar"][:, :, 1, :], ALU.add).then_inc(*own.next())
                vec.tensor_tensor(a["Mt"], units(2), idc, ALU.add).then_inc(*served())
                pend = a["pend"].rearrange("p (h c) -> p h c", h=NH)
                for c in range(NC_ - 1):
                    from_psum()
                    vec.tensor_tensor(a["S"][:, c], ps(2 + c, 1, C)[:, 0:NH * C].rearrange("p (h v) -> p h v", h=NH),
                                      bcast(pend[:, :, c], 2, C), ALU.mult).then_inc(*served())
                from_psum()
                y, ysq, mean, var = a["y"], a["ysq"], rstd[0:C, :], misc[0:C, 288:304]
                vec.tensor_reduce(mean, units(0), AX, ALU.add).then_inc(*own.next())
                done()
                vec.tensor_scalar(mean, mean, 1.0 / C, None, ALU.mult).then_inc(*own.next())
                done()
                vec.tensor_tensor(y, units(0), bcast(mean, 2, C), ALU.subtract).then_inc(*own.next())
                done()
                vec.tensor_tensor(ysq, y, y, ALU.mult).then_inc(*own.next())
                done()
                vec.tensor_reduce(var, ysq, AX, ALU.add).then_inc(*own.next())
                done()
                rooted(var, 1.0 / C, RWKV_EPS)
                vec.tensor_tensor(y, y, bcast(var, 2, C), ALU.mult).then_inc(*own.next())
                vec.tensor_tensor(a["X"], a["X"], a["tm"][:, 3], ALU.mult).then_inc(*own.next())
                done()
                y4 = y.rearrange("p (h c) v -> p h c v", h=NH)
                for i, op in enumerate((ALU.mult, ALU.add)):
                    for hd in range(NH):
                        vec.tensor_tensor(y4[:, hd], y4[:, hd], bcast(a["ln"][:, i, hd * C:(hd + 1) * C], 1, NC_), op).then_inc(*own.next())
                    done()
                vec.tensor_tensor(y, y, a["X"], ALU.add).then_inc(*own.next())
                done()
                g4 = a["g"].rearrange("p c (h v) -> p h c v", h=NH)
                for hd in range(NH):
                    vec.tensor_tensor(a["gated"][:, :, hd, :], y4[:, hd], g4[:, hd], ALU.mult).then_inc(
                        *(served() if hd == NH - 1 else own.next()))
                done()
                lq, lam = a["lq"], a["lam"]
                vec.tensor_tensor(lq[:, 0], lq[:, 0], lq[:, 1], ALU.mult).then_inc(*own.next())
                done()
                vec.tensor_reduce(lam[:, 0:2], lq[:, 0], AX, ALU.add).then_inc(*own.mark(vec_for_act))
                from_psum()
                take_split(hT[:, 0, 2:4, :], hT[:, 1, 2:4, :], 6, 1)
                vec.wait_ge(act_for_vec, from_act.up())
                vec.tensor_tensor(lam[:, 2:3], lam[:, 1:2], lam[:, 0:1], ALU.subtract).then_inc(*own.next())
                done()
                vec.tensor_scalar(lam[:, 2:3], lam[:, 2:3], -LAMBDA_INIT, None, ALU.add).then_inc(*own.next())
                vec.wait_ge(alibi_loaded, 16)
                for c in range(2):
                    from_psum()
                    p = a["p"][:, c]
                    rows_ = p.rearrange("p b h k -> p (b h) k")
                    vec.scalar_tensor_tensor(p.rearrange("p b h k -> p (b h k)"), ps(4 * c, 4), C ** -0.5,
                                             a["alibi"].rearrange("p b h k -> p (b h k)"), ALU.mult, ALU.add).then_inc(*own.next())
                    done()
                    softmax(rows_, p, top8, sum8, own.next if c else served)
                p0 = a["p"][:, 0].rearrange("p b h k -> p (b h k)")
                vec.scalar_tensor_tensor(p0, a["p"][:, 1].rearrange("p b h k -> p (b h k)"), lam[:, 2:3], p0,
                                         ALU.mult, ALU.add).then_inc(*served())
                take_turned(a["pT"].rearrange("p h k t -> p (h k) t")[:, 0:4, :], 4)
                from_psum()
                o, osq = (a[w].rearrange("p b h v -> p (b h) v") for w in ("o", "osq"))
                vec.tensor_copy(o, ps(0, 2).rearrange("p (r v) -> p r v", v=P)).then_inc(*own.next())
                done()
                vec.tensor_tensor(osq, o, o, ALU.mult).then_inc(*own.next())
                done()
                vec.tensor_reduce(sum8, osq, AX, ALU.add).then_inc(*own.next())
                done()
                rooted(sum8, 1.0 / P, RMS_EPS)
                vec.tensor_tensor(o, o, bcast(sum8, 2, P), ALU.mult).then_inc(*own.next())
                done()
                vec.scalar_tensor_tensor(o, o, 1.0 - LAMBDA_INIT, bcast(misc[:, 0:P], 1, 8), ALU.mult, ALU.mult).then_inc(*served())
                from_psum()
                take_split(hT[:, 0, 4:8, :], hT[:, 1, 4:8, :], 2, 2)
                add_stream("mix_out", 4)

            def vec_cross(a, phase):
                vec.wait_ge(params_loaded, loads[phase])
                rms_stream(a["mem"], a["mn"], a["norm"][:, 0, :], (params_loaded, loads[phase]))
                rms_stream(h, a["hn"], a["norm"][:, 1, :], (params_loaded, loads[phase]))
                take_matrix(hT, 4)

                def head_norm(key, b0, dst, gain):
                    panel_done(key)
                    ahead = {"xa_wk_2": "xa_wv_2"}.get(key, key)
                    d8, s8 = (v.rearrange("p b (h e) -> p (b h) e", h=XH) for v in (dst, a["sq"]))
                    vec.tensor_copy(d8, ps(b0, 4).rearrange("p (r e) -> p r e", e=XD)).then_inc(*own.next())
                    more(1, ahead)
                    done()
                    vec.tensor_tensor(s8, d8, d8, ALU.mult).then_inc(*own.next())
                    more(1, ahead)
                    done()
                    vec.tensor_reduce(sum8, s8, AX, ALU.add).then_inc(*own.next())
                    done()
                    rooted(sum8, 1.0 / XD, RMS_EPS)
                    vec.tensor_tensor(d8, d8, bcast(sum8, 2, XD), ALU.mult).then_inc(*own.next())
                    more(1, ahead)
                    done()
                    vec.tensor_tensor(d8, d8, bcast(gain, 1, 8), ALU.mult).then_inc(*served())

                head_norm("xa_wk_2", 0, a["k"], a["gain"][:, 0, :])
                split_to(end["xa_wv_2"] + SPLIT)
                take_turned(a["kT"][:, 0:4, :], 0)
                take_matrix(hT)
                head_norm("xa_wq_2", 4, a["q"], a["gain"][:, 1, :])
                take_turned(a["qT"][:, 0:4, :], 0)
                from_psum()
                softmax(ps(4, 4).rearrange("p (r k) -> p r k", k=T), a["p"], top8, sum8, served)
                take_turned(a["pT"].rearrange("p h k t -> p (h k) t")[:, 0:4, :], 0)
                from_psum()
                take_split(hT[:, 0], hT[:, 1], 4, 4)
                add_stream("xa_wo_2", 0)

            def vec_ffn(a):
                vec.wait_ge(params_loaded, loads["ffn"])
                for n in range(6):
                    b0, w = 4 * ((n + 1) % 2), min(4, FF_TILES - 4 * n)
                    panel_done(f"up{n}")
                    ahead = f"up{min(n + 1, 5)}"
                    v = ps(b0, 4).rearrange("p (i t) -> p i t", t=T)
                    c = a["conv"][:, n % 2]
                    for i in range(w):
                        f = 4 * n + i
                        vec.tensor_scalar(c[:, i, :], v[:, i, :], a["taps"][:, 2, f:f + 1], a["bias"][:, f:f + 1],
                                          ALU.mult, ALU.add).then_inc(*own.next())
                    done()
                    for tap in (1, 0):
                        back = 2 - tap
                        for i in range(w):
                            f = 4 * n + i
                            vec.scalar_tensor_tensor(c[:, i, back:], v[:, i, 0:T - back], a["taps"][:, tap, f:f + 1],
                                                     c[:, i, back:], ALU.mult, ALU.add).then_inc(
                                *(own.mark(vec_for_act) if tap == 0 and i == w - 1 else own.next()))
                        more(1, ahead)
                        done()
                    vec.wait_ge(act_for_vec, from_act.up())
                    vec.tensor_tensor(a["hid"][:, 4 * n:4 * n + w, :], c[:, 0:w, :], v[:, w:2 * w, :], ALU.mult).then_inc(*served())
                done()
                feed("down", a["hid"])
                add_stream("down", 4)

            def vec_peer(a, phase):
                first_u, first_v, d0 = begin[phase + "_u"], begin[phase + "_v"], experts_before[phase]
                for n in range(2):
                    panel_done(f"{phase}_q{n}")
                    vec.tensor_copy(a["qT"][:, 8 * n:8 * n + 8, :].rearrange("p a b -> p (a b)"), ps(4 * (1 - n), 4)).then_inc(*served())

                def due():
                    split_to(min(n_split.n + 1, first_u + NK // 2))

                def top_sixteen(n, src, spare, val, idx):
                    for i in range(n):
                        vec.max(val(i)[:, 0:8], src(i)).then_inc(*own.next())
                        if i % 5 == 4:
                            due()
                    done()
                    for i in range(n):
                        vec.max_index(idx(i)[:, 0:8], val(i)[:, 0:8], src(i)).then_inc(*own.next())
                        if i % 5 == 4:
                            due()
                    for i in range(n):
                        vec.match_replace(spare(i), val(i)[:, 0:8], src(i), LOWEST).then_inc(*own.next())
                        if i % 5 == 4:
                            due()
                    done()
                    for i in range(n):
                        vec.max(val(i)[:, 8:16], spare(i)).then_inc(*own.next())
                        if i % 5 == 4:
                            due()
                    done()
                    for i in range(n):
                        vec.max_index(idx(i)[:, 8:16], val(i)[:, 8:16], spare(i)).then_inc(*own.next())
                        if i % 5 == 4:
                            due()
                    done()

                split_to(end[phase + "_keys"] + SPLIT)
                vec.wait_ge(act_for_vec, from_act.up())
                for tb in range(TB):
                    s, s2, val, idx = a["s"][:, tb], a["s2"], a["val"], a["idx"].bitcast(U32)
                    top_sixteen(HC, lambda i: s[:, i, :], lambda i: s2[:, i, :], lambda i: val[:, i, :], lambda i: idx[:, i, :])
                    idxf = a["idxf"]
                    vec.tensor_copy(idxf, idx).then_inc(*own.next())
                    v1 = val.rearrange("p (h c) k -> p h c k", c=2)
                    cand, cand2 = a["cand"], a["cand2"]
                    c4 = cand.rearrange("p h (a b) -> p h a b", a=TOPK)
                    for hd in range(PH):
                        vec.tensor_tensor(c4[:, hd], bcast(v1[:, hd, 0, :], 2, TOPK), bcast(v1[:, hd, 1, :], 1, TOPK),
                                          ALU.add).then_inc(*own.next())
                    due()
                    done()
                    top, pos = a["top"], a["pos"].bitcast(U32)
                    top_sixteen(PH, lambda i: cand[:, i, :], lambda i: cand2[:, i, :], lambda i: top[:, i, :], lambda i: pos[:, i, :])
                    ab = a["ab"].bitcast(U32)
                    vec.tensor_scalar(ab[:, 0], pos, 4, None, ALU.logical_shift_right).then_inc(*own.next())
                    vec.tensor_scalar(ab[:, 1], pos, 15, None, ALU.bitwise_and).then_inc(*own.next())
                    due()
                    done()
                    abf = a["abf"]
                    vec.tensor_copy(abf, ab).then_inc(*own.next())
                    done()
                    i1 = idxf.rearrange("p (h c) k -> p h c k", c=2)
                    sel = a["sel"]
                    for w in range(2):
                        for hd in range(PH):
                            vec.tensor_tensor(sel[:, hd], bcast(abf[:, w, hd, :], 2, TOPK), bcast(iota[:, 0:TOPK], 1, TOPK),
                                              ALU.is_equal).then_inc(*own.next())
                        due()
                        done()
                        for hd in range(PH):
                            vec.tensor_tensor(sel[:, hd], sel[:, hd], bcast(i1[:, hd, w, :], 1, TOPK), ALU.mult).then_inc(*own.next())
                        due()
                        done()
                        vec.tensor_reduce(a["ijg"][:, w, tb], sel, AX, ALU.add).then_inc(*own.next())
                        due()
                        done()
                    vec.tensor_tensor(a["ijg"][:, 2, tb], top, top[:, :, 0:1].broadcast_to([P, PH, TOPK]), ALU.subtract).then_inc(
                        *(own.mark(vec_for_act) if tb == TB - 1 else own.next()))
                    done()
                split_to(first_u + NK // 2)
                gate, den = a["ijg"][:, 2].rearrange("p b h k -> p (b h) k"), a["den"].rearrange("p b h -> p (b h)")
                vec.wait_ge(act_for_vec, from_act.up())
                vec.tensor_reduce(den, gate, AX, ALU.add).then_inc(*own.next())
                done()
                vec.reciprocal(den, den).then_inc(*own.next())
                done()
                vec.tensor_tensor(gate, gate, bcast(den, 2, TOPK), ALU.mult).then_inc(*own.mark(vec_for_pe))
                split_to(first_u + HALF + SPLIT)
                vec.wait_ge(psum_for_vec, psum_v.up())
                vec.tensor_copy(routes.rearrange("p a b -> p (a b)"), ps(0, 2)[:, 0:3 * T]).then_inc(*served())
                done()
                vec.tensor_copy(misc[:, 509:510], iota[:, 0:1]).then_inc(*own.mark(routes_ready))

                base, G = gates_before[phase], a["G"]

                def onehots(t, upper, half):
                    keys = iota[:, upper * HALF:(upper + 1) * HALF]
                    for q in range(4):
                        i = vec.tensor_scalar(i_onehot[:, half, q, :], keys, routes[:, 0, bass.ds(t * 4 + q, 1)],
                                              routes[:, 2, bass.ds(t * 4 + q, 1)], ALU.is_equal, ALU.mult)
                    i.then_inc(onehots_made, 1)

                def place(t, upper, half):
                    vec.wait_ge(onehots_used, t + (base + upper * GROUPS + 1))
                    v = G[:, upper * HALF:(upper + 1) * HALF, bass.ds(t * 4, 4)].rearrange("p i q -> p q i")
                    vec.tensor_tensor(v, ps(4 + half, 1)[:, 0:4 * HALF].rearrange("p (q i) -> p q i", q=4), v,
                                      ALU.mult).then_inc(gates_placed, 1)

                def lower_tile(n, further=0):
                    vec.wait_ge(tile_hi, further + tile_count[n])
                    lower(n % RING, n % SPLIT, None, wide=BY_VEC)

                onehots(0, 0, 0)
                onehots(1, 0, 1)
                vec.wait_ge(gelu_done, d0 + HALF)
                n = first_u + HALF + SPLIT
                with vec.Fori(0, HALF // RING - 1) as it:
                    for r in range(RING):
                        lower_tile(n + r, it * RING)
                        place(it * RING + r, 0, r % 2)
                        onehots(it * RING + (r + 2), 0, r % 2)
                for k in range(HALF - RING, HALF):
                    lower_tile(n + k)
                    place(k, 0, k % 2)
                    onehots((k + 2) % GROUPS, (k + 2) // GROUPS, k % 2)

                def weigh(tile, i, buf):
                    w = G[:, bass.ds(tile, 1), :].rearrange("p o t -> p (o t)")
                    round_to(tile_w[:, buf, 0, :], w).then_inc(weights_hi, 1)
                    vec.wait_ge(weights_hi, i + 1)
                    vec.tensor_tensor(tile_w[:, buf, 1, :], w, tile_w[:, buf, 0, :].bitcast(F32), ALU.subtract).then_inc(weights_ready, 1)

                vec.wait_ge(gates_placed, base + GROUPS)
                weigh(0, d0, 0)
                weigh(1, d0 + 1, 1)
                vec.wait_ge(gelu_done, d0 + NK)
                for k in range(2):
                    place(k, 1, k)
                    onehots(k + 2, 1, k)

                def next_tile(k, n, further, buf):
                    vec.wait_ge(chunks_done, further + (n - 1))
                    weigh(k + 2, k + (d0 + 2), buf)
                    lower_tile(n, further)

                n = first_v + SPLIT
                with vec.Fori(0, HALF // RING - 1) as it:
                    for r in range(RING):
                        next_tile(it * RING + r, n + r, it * RING, r % 2)
                        place(it * RING + (r + 2), 1, r % 2)
                        onehots(it * RING + (r + 4), 1, r % 2)
                for k in range(HALF - RING, HALF - 2):
                    next_tile(k, n + k, 0, k % 2)
                    place(k + 2, 1, k % 2)
                vec.wait_ge(gates_placed, base + 2 * GROUPS)
                for k in range(HALF - 2, HALF):
                    next_tile(k, n + k, 0, k % 2)
                with vec.Fori(HALF // RING, NK // RING - 1) as it:
                    for r in range(RING):
                        next_tile(it * RING + r, n + r, it * RING, r % 2)
                for k in range(NK - RING, NK - 2):
                    next_tile(k, n + k, 0, k % 2)
                n_split.n = first_v + NK
                own.last = (chunk_split, split_count[first_v + NK - 1])
                ln_stream(phase + "_v", 0, phase)

            vec.wait_ge(input_loaded, 64)
            for n, phase in enumerate(phases):
                if phase in ("mixers", "ffn"):
                    rms_stream(h, A[phase]["hn"], A[phase]["norm"][:, 0, :], (norm_loaded, norm_loads[phase]))
                if phase != "cross":
                    take_matrix(hT)
                if phase == "retention":
                    vec_retention(A[phase], phase)
                if phase == "mla":
                    vec_mla(A[phase], phase)
                if phase == "mixers":
                    vec_mixers(A[phase])
                if phase == "cross":
                    vec_cross(A[phase], phase)
                if phase == "ffn":
                    vec_ffn(A[phase])
                if phase.startswith("peer"):
                    vec_peer(A[phase], phase)

        @block.scalar
        def _(act):
            own = Last(act_step)
            psum_a, from_vec = Count(), Count()

            def done():
                act.wait_ge(*own.last)

            for dst, src in [(h[:, tb, :], x["x"][0, tb * P:(tb + 1) * P, :]) for tb in range(TB)] \
                    + [(ident, x["c_ident"]), (iota, x["c_iota"])]:
                act.dma_start(dst, src).then_inc(input_loaded, 16)

            def load_params(phase):
                for dst, src in norms.get(phase, []):
                    act.dma_start(dst, src).then_inc(norm_loaded, 16)
                for dst, src in params.get(phase, []):
                    act.dma_start(dst, src).then_inc(params_loaded, 16)

            def copy_turned(dst, b0, nb=2):
                act.wait_ge(psum_for_act, psum_a.up())
                act.activation(dst.rearrange("p a b -> p (a b)"), ps(b0, nb), ACT.Copy).then_inc(*own.mark(act_served))

            def root(v):
                act.wait_ge(vec_for_act, from_vec.up())
                act.activation(v, v, ACT.Sqrt).then_inc(*own.mark(act_for_vec))

            def act_retention(a):
                lg = a["lg"]
                act.activation(lg, lg, ACT.Exp).then_inc(*own.next())
                done()
                act.activation(lg, lg, ACT.Ln, scale=-1.0, bias=1.0).then_inc(*own.mark(act_for_vec))
                act.wait_ge(vec_for_act, from_vec.up())
                act.activation(a["cos"], a["cos"], ACT.Sin).then_inc(*own.next())
                act.activation(a["sin"], a["sin"], ACT.Sin).then_inc(*own.next())
                act.wait_ge(vec_for_act, from_vec.up())
                dec = a["decay"].rearrange("p a b -> p (a b)")
                act.activation(dec, dec, ACT.Exp).then_inc(*own.mark(act_for_vec))
                for n in range(4):
                    b0 = 4 * ((n + 3) % 2)
                    act.wait_ge(chunks_done, end[f"ret_in{n + 2}"])
                    dst = (a["v"], a["g"])[n // 2][:, :, (n % 2) * 1024:(n % 2 + 1) * 1024]
                    for tb in range(TB):
                        i = act.activation(dst[:, tb, :], ps(b0 + 2 * tb, 2), ACT.Copy if n < 2 else ACT.Silu)
                        i.then_inc(*(own.mark(act_served) if tb else own.next()))
                root(rstd[:, 0:4])
                root(rstd[:, 4:8])
                root(rstd[:, 0:TB])

            def in_place(v, func, **kw):
                act.wait_ge(vec_for_act, from_vec.up())
                act.activation(v, v, func, **kw).then_inc(*own.mark(act_for_vec))

            def tell_vec():
                done()
                act.activation(misc[:, 508:509], iota[:, 0:1], ACT.Copy).then_inc(*own.mark(act_for_vec))

            def rows8(p):
                return p.rearrange("p b h k -> p (b h k)")

            def turned_p(pT, b0):
                copy_turned(pT.rearrange("p h k t -> p (h k) t")[:, 4:8, :], b0)

            def act_mla(a):
                act.wait_ge(vec_for_act, from_vec.up())
                act.activation(a["cos"], a["cos"], ACT.Sin).then_inc(*own.next())
                act.activation(a["sin"], a["sin"], ACT.Sin).then_inc(*own.mark(act_for_vec))
                root(rstd[:, 0:4])
                for key, dst in (("mla_uq", "qnT"), ("mla_ukv", "knT")):
                    for n in range(2):
                        act.wait_ge(chunks_done, end[f"{key}{n}"])
                        act.activation(a[dst][:, 4 * n:4 * n + 4, :].rearrange("p a b -> p (a b)"), ps(4 * (1 - n), 2),
                                       ACT.Copy).then_inc(*own.mark(act_served))
                act.wait_ge(psum_for_act, psum_a.up())
                act.activation(a["qrT"].rearrange("p a b -> p (a b)"), ps(4, 4, ROPE), ACT.Copy).then_inc(*own.mark(act_served))
                for n in range(2):
                    in_place(rows8(a["p"]), ACT.Exp, scale=MLA_SCALE)
                    turned_p(a["pT"], 6)
                root(rstd[:, 0:TB])

            def act_mixers(a):
                def flat(v):
                    return v.rearrange("p a b -> p (a b)")

                for n in range(4):
                    b0 = 4 * ((n + 1) % 2)
                    act.wait_ge(chunks_done, end[f"slots{n}"])
                    src = ps(b0, 2).rearrange("p (s t) -> p s t", t=T)
                    dst = a["z"][:, 8 * n:8 * n + 8, 1:T + 1] if n < 2 else a["qk"][:, n - 2]
                    for side in range(2):
                        act.activation(dst.rearrange("p (s two) t -> p s two t", two=2)[:, :, side, :],
                                       src[side * C:(side + 1) * C], ACT.Copy).then_inc(*(own.mark(act_served) if side else own.next()))
                    if n == 1:
                        tell_vec()
                for key, b0, c in (("diff_v", 4, slice(POOL_W, POOL_W + DIFF_W)), ("pool_in", 0, slice(0, POOL_W))):
                    act.wait_ge(chunks_done, end[key])
                    act.activation(a["pv"][:, :, c], ps(b0, 4).rearrange("p (b c) -> p b c", b=TB)[:, :, 0:c.stop - c.start],
                                   ACT.Copy).then_inc(*own.mark(act_served))
                act.wait_ge(vec_for_act, from_vec.up())
                act.activation(a["zm"][:, 12, :], a["zm"][:, 12, :], ACT.Tanh).then_inc(*own.next())
                act.activation(a["zm"][:, 14:16, :], a["zm"][:, 14:16, :], ACT.Sigmoid).then_inc(*own.mark(act_for_pe))
                act.wait_ge(psum_for_act, psum_a.up())
                for w, dst in enumerate(("lw", "a")):
                    for hd in range(NH):
                        act.activation(a[dst][:, hd, :], ps(2 * w + hd // 2, 1, C)[:, (hd % 2) * T:(hd % 2 + 1) * T],
                                       ACT.Sigmoid, bias=a["cols"][:, w, hd:hd + 1]).then_inc(*own.next())
                act.activation(flat(a["g"]), ps(4, 2, C), ACT.Copy).then_inc(*own.mark(act_served))
                tell_vec()
                act.wait_ge(vec_for_act, from_vec.up())
                act.activation(flat(a["Pd"]), flat(a["L"]), ACT.Exp).then_inc(*own.next())
                act.activation(flat(a["Pi"]), flat(a["L"]), ACT.Exp, scale=-1.0).then_inc(*own.next())
                act.activation(flat(a["Pp"]), flat(a["Pp"]), ACT.Exp).then_inc(*own.mark(act_for_vec))
                act.wait_ge(psum_for_act, psum_a.up())
                act.activation(flat(a["kk2"]), ps(6, 2, C), ACT.Sqrt).then_inc(*own.mark(act_served))
                tell_vec()
                act.wait_ge(psum_for_act, psum_a.up())
                act.activation(a["tm"][:, 0:2].rearrange("p w u c -> p (w u c)"), ps(0, 4, C), ACT.Copy).then_inc(*own.mark(act_served))
                rs, qk = (a[w].rearrange("p w s t -> p (w s t)") for w in ("rs", "qk"))
                for b in range(4):
                    quarter = slice(4 * b * T, 4 * (b + 1) * T)
                    act.activation(flat(a["sq"]), qk[:, quarter], ACT.Square).then_inc(*own.mark(act_for_pe))
                    root(rs[:, quarter])
                for dst, b0 in (("AkV", 0), ("U0", 6), ("X", 4)):
                    act.wait_ge(psum_for_act, psum_a.up())
                    if dst == "AkV":
                        act.dma_start(a["alibi"].rearrange("p a b c -> p (a b c)"), x["c_alibi"]).then_inc(alibi_loaded, 16)
                    act.activation(flat(a[dst]), ps(b0, 2, C), ACT.Copy).then_inc(*own.mark(act_served))
                root(misc[0:C, 288:304])
                in_place(a["lam"][:, 0:2], ACT.Exp)
                for c in range(2):
                    in_place(rows8(a["p"][:, c]), ACT.Exp)
                turned_p(a["pT"], 6)
                root(sum8_)

            sum8_ = misc[:, 264:272]

            def act_cross(a):
                root(rstd[:, 0:TB])
                root(rstd[:, 0:TB])
                root(sum8_)
                act.wait_ge(chunks_done, end["xa_wv_2"])
                act.activation(a["v"].rearrange("p a b -> p (a b)"), ps(4, 4), ACT.Copy).then_inc(*own.mark(act_served))
                copy_turned(a["kT"][:, 4:8, :], 2)
                root(sum8_)
                copy_turned(a["qT"][:, 4:8, :], 2)
                in_place(rows8(a["p"]), ACT.Exp, scale=XD ** -0.5)
                turned_p(a["pT"], 2)

            def act_ffn(a):
                for n in range(6):
                    w = min(4, FF_TILES - 4 * n)
                    in_place(a["conv"][:, n % 2, 0:w, :].rearrange("p a b -> p (a b)"), ACT.Gelu)

            def act_peer(a, phase):
                first_u, d0 = begin[phase + "_u"], experts_before[phase]
                def round_tile(n, loaded, read):
                    act.wait_ge(ring_loaded[n % RING], loaded)
                    act.wait_ge(chunks_done, read)
                    act.activation(ring_hi[:, n % SPLIT, :], ring[:, n % RING, :], ACT.Copy).then_inc(tile_hi, 1)

                def round_now(n):
                    round_tile(n, 16 * (n // RING + 1), n - 1)

                round_now(first_u)
                act.wait_ge(chunks_done, end[phase + "_keys"])
                round_now(first_u + 1)
                for tb in range(TB):
                    act.activation(a["s"][:, tb].rearrange("p a b -> p (a b)"), ps(4 * tb, 4), ACT.Copy).then_inc(
                        *(own.mark(act_served) if tb else own.next()))
                tell_vec()

                base = gates_before[phase]

                def j_group(g, half, fresh=False):
                    v = less_j[:, half].rearrange("p q n -> p (q n)")
                    act.wait_ge(j_less, g + (base + 1))
                    act.activation(v, v, ACT.Abs).then_inc(j_apart, 1)
                    if not fresh:
                        act.wait_ge(onehots_used, g + (base - 1))
                    act.wait_ge(j_apart, g + (base + 1))
                    act.activation(j_onehot[:, half].rearrange("p q n -> p (q n)"), v, ACT.Relu, scale=-1.0, bias=1.0).then_inc(j_onehots, 1)

                def round_and_gelu(tile, r, further):
                    n = first_u + r + SPLIT
                    round_tile(n, further * (16 // RING) + 16 * (n // RING + 1), further + (n - 1))
                    act.activation(a["G"][:, bass.ds(tile, 1), :].rearrange("p o t -> p (o t)"),
                                   ps(6 + r % 2, 1)[:, 0:T], ACT.Gelu).then_inc(gelu_done, 1)

                with act.Fori(0, HALF // RING) as it:
                    for r in range(RING):
                        round_and_gelu(it * RING + r, r, it * RING)
                in_place(a["ijg"][:, 2].rearrange("p b h k -> p (b h k)"), ACT.Exp)
                j_group(0, 0, fresh=True)
                j_group(1, 1, fresh=True)
                with act.Fori(HALF // RING, NK // RING) as it:
                    for r in range(RING):
                        round_and_gelu(it * RING + r, r, it * RING)
                        j_group(it * RING + (r + 2 - HALF), r % 2)
                j_group(GROUPS + 2, 0)
                j_group(GROUPS + 3, 1)
                first_v = begin[phase + "_v"]
                with act.Fori(0, HALF // RING - 1) as it:
                    for r in range(RING):
                        n = first_v + r + SPLIT
                        round_tile(n, it * 16 + 16 * (n // RING + 1), it * RING + (n - 1))
                        j_group(it * RING + (GROUPS + 4 + r), r % 2)
                with act.Fori(HALF // RING - 1, NK // RING - 1) as it:
                    for r in range(RING):
                        n = first_v + r + SPLIT
                        round_tile(n, it * 16 + 16 * (n // RING + 1), it * RING + (n - 1))
                for n in range(first_v + NK - RING + SPLIT, first_v + NK):
                    round_now(n)
                act.wait_ge(weights_ready, d0 + NK)
                load_params(phase)
                root(rstd[:, 0:TB])

            for n, phase in enumerate(phases):
                if n:
                    act.wait_ge(phase_done, n)
                if not phase.startswith("peer"):
                    load_params(phase)
                    if phase in ("mixers", "ffn"):
                        root(rstd[:, 0:TB])
                    if phase in ("retention", "mixers"):
                        act.wait_ge(params_loaded, loads[phase])
                if phase == "retention":
                    act_retention(A[phase])
                if phase == "mla":
                    act_mla(A[phase])
                if phase == "mixers":
                    act_mixers(A[phase])
                if phase == "cross":
                    act_cross(A[phase])
                if phase == "ffn":
                    act_ffn(A[phase])
                if phase.startswith("peer"):
                    act_peer(A[phase], phase)


def kernel(**inputs):
    import numpy as _np
    import concourse.bacc as _bacc
    from concourse import mybir as _mybir
    from concourse.bass_utils import run_bass_kernel_spmd as _run

    nc = _bacc.Bacc("TRN2", target_bir_lowering=False, num_devices=1)
    arrays, x = {}, {}
    for name, value in {**inputs, **constants(), **columns(inputs), **turned(inputs)}.items():
        if name in ("peer_u", "peer_sub_keys"):
            continue
        a = _np.ascontiguousarray(value)
        arrays[f"in_{name}"] = a
        x[name] = nc.dram_tensor(f"in_{name}", a.shape, _mybir.dt.from_np(a.dtype), kind="ExternalInput").ap()
    out = nc.dram_tensor("out", (1, T, D), F32, kind="ExternalOutput").ap()
    build(nc, x, out)
    return _run(nc, [arrays], core_ids=[0]).results[0]["out"]
```
